# Optimizing a Trainium2 kernel written in Bass

```python
import math
import jax, jax.numpy as jnp
from jax import lax
import numpy as np
import jax
import jax.numpy as jnp

D_MODEL = 1024
BATCH = 1
SEQ = 512
DEPTH = 2

HEAD_DIM = 64
H_A = D_MODEL // HEAD_DIM
KV_A = 4
G_A = H_A // KV_A
WINDOW_A = 128
BLOCK_A = 128
H_B = D_MODEL // HEAD_DIM
DILATED_GROUPS = ((128, 1), (512, 4), (2048, 16))
N_GROUPS_B = len(DILATED_GROUPS)
BLOCK_B = 64
D_FF = -(-8 * D_MODEL // (3 * 256)) * 256
RMS_EPS = 1e-6
NEG = -1e30


def rmsnorm(x, g):
    x32 = x.astype(jnp.float32)
    y = x32 * lax.rsqrt(jnp.mean(x32 * x32, axis=-1, keepdims=True) + RMS_EPS)
    return (y * g.astype(jnp.float32)).astype(x.dtype)

def alibi_slopes(n):
    return 2.0 ** (-8.0 * jnp.arange(1, n + 1, dtype=jnp.float32) / n)

def banded_attention(q, k, v, slopes, dist_unit, window, block):
    n, L, hk, g, dh = q.shape
    c = window // block
    nb = -(-L // block)
    lp = nb * block
    kw = (2 * c + 1) * block
    qb = jnp.pad(q, ((0, 0), (0, lp - L), (0, 0), (0, 0), (0, 0))).reshape(n, nb, block, hk, g, dh)
    pad_k = ((0, 0), (window, window + lp - L), (0, 0), (0, 0))
    kb = jnp.pad(k, pad_k).reshape(n, nb + 2 * c, block, hk, dh)
    vb = jnp.pad(v, pad_k).reshape(n, nb + 2 * c, block, hk, dh)
    kwin = jnp.concatenate([kb[:, j:j + nb] for j in range(2 * c + 1)], axis=2)
    vwin = jnp.concatenate([vb[:, j:j + nb] for j in range(2 * c + 1)], axis=2)
    scores = jnp.einsum('nbqhgd,nbkhd->nbhgqk', qb, kwin,
                        preferred_element_type=jnp.float32) * (dh ** -0.5)
    rel = jnp.arange(kw)[None, :] - window - jnp.arange(block)[:, None]
    key_pos = jnp.arange(nb)[:, None] * block - window + jnp.arange(kw)[None, :]
    valid = (jnp.abs(rel)[None] <= window) & ((key_pos >= 0) & (key_pos < L))[:, None, :]
    dist = jnp.abs(rel).astype(jnp.float32) * dist_unit
    scores = scores - slopes.astype(jnp.float32)[:, :, None, None] * dist
    scores = jnp.where(valid[None, :, None, None], scores, NEG)
    m = jnp.max(scores, axis=-1)
    p = jnp.exp(scores - m[..., None])
    den = jnp.sum(p, axis=-1)
    lse = m + jnp.log(den)
    out = jnp.einsum('nbhgqk,nbkhd->nbqhgd', p.astype(v.dtype), vwin,
                     preferred_element_type=jnp.float32)
    out = out / jnp.moveaxis(den, -1, 2)[..., None]
    out = out.reshape(n, lp, hk, g, dh)[:, :L]
    lse = jnp.moveaxis(lse, -1, 2).reshape(n, lp, hk, g)[:, :L]
    return out.astype(q.dtype), lse

def window_gqa_sink(h, w_qkv, w_out, sink):
    b, s, _ = h.shape
    qkv = h @ w_qkv
    q = qkv[..., :H_A * HEAD_DIM].reshape(b, s, KV_A, G_A, HEAD_DIM)
    k = qkv[..., H_A * HEAD_DIM:(H_A + KV_A) * HEAD_DIM].reshape(b, s, KV_A, HEAD_DIM)
    v = qkv[..., (H_A + KV_A) * HEAD_DIM:].reshape(b, s, KV_A, HEAD_DIM)
    slopes = alibi_slopes(H_A).reshape(KV_A, G_A)
    o, lse = banded_attention(q, k, v, slopes, 1, WINDOW_A, BLOCK_A)
    o = o * jax.nn.sigmoid(lse - sink.astype(jnp.float32).reshape(KV_A, G_A))[..., None]
    return o.astype(h.dtype).reshape(b, s, H_A * HEAD_DIM) @ w_out

def to_residue(t, dil):
    b, s, hh, dh = t.shape
    return t.reshape(b, s // dil, dil, hh, dh).transpose(0, 2, 1, 3, 4).reshape(b * dil, s // dil, hh, dh)

def from_residue(t, b, dil):
    rest = t.shape[2:]
    L = t.shape[1]
    t = t.reshape((b, dil, L) + rest)
    t = jnp.swapaxes(t, 1, 2)
    return t.reshape((b, L * dil) + rest)

def dilated_mixture_attention(h, w_qkv, w_out):
    b, s, _ = h.shape
    qkv = (h @ w_qkv).reshape(b, s, N_GROUPS_B, 3, H_B, HEAD_DIM)
    slopes = alibi_slopes(H_B)[:, None]
    outs, lses = [], []
    for gi, (win, dil) in enumerate(DILATED_GROUPS):
        q = to_residue(qkv[:, :, gi, 0], dil)[:, :, :, None]
        k = to_residue(qkv[:, :, gi, 1], dil)
        v = to_residue(qkv[:, :, gi, 2], dil)
        o, lse = banded_attention(q, k, v, slopes, dil, win // (2 * dil), BLOCK_B)
        outs.append(from_residue(o[:, :, :, 0], b, dil))
        lses.append(from_residue(lse[:, :, :, 0], b, dil))
    wts = jax.nn.softmax(jnp.stack(lses), axis=0)
    o = jnp.einsum('gbsh,gbshd->bshd', wts, jnp.stack(outs).astype(jnp.float32))
    return o.astype(h.dtype).reshape(b, s, H_B * HEAD_DIM) @ w_out

def swiglu(h, w_gate, w_up, w_down):
    return (jax.nn.silu(h @ w_gate) * (h @ w_up)) @ w_down

def first_inputs(seed: int = 0) -> dict:
    key = jax.random.key(seed)
    ks = jax.random.split(key, 14)
    n_a = (DEPTH + 1) // 2
    n_b = DEPTH // 2
    qkv_a = (H_A + 2 * KV_A) * HEAD_DIM
    qkv_b = N_GROUPS_B * 3 * H_B * HEAD_DIM
    f32 = jnp.float32

    def w(k, shape, fan_in):
        return jax.random.normal(k, shape, f32) * fan_in ** -0.5

    return {
        "x": jax.random.normal(ks[0], (BATCH, SEQ, D_MODEL), f32),
        "norm_mix": 1.0 + 0.02 * jax.random.normal(ks[1], (DEPTH, D_MODEL), f32),
        "norm_ffn": 1.0 + 0.02 * jax.random.normal(ks[2], (DEPTH, D_MODEL), f32),
        "w_qkv_a": w(ks[3], (n_a, D_MODEL, qkv_a), D_MODEL),
        "w_out_a": w(ks[4], (n_a, H_A * HEAD_DIM, D_MODEL), H_A * HEAD_DIM),
        "sink_a": 0.5 * jax.random.normal(ks[5], (n_a, H_A), f32),
        "w_qkv_b": w(ks[6], (n_b, D_MODEL, qkv_b), D_MODEL),
        "w_out_b": w(ks[7], (n_b, H_B * HEAD_DIM, D_MODEL), H_B * HEAD_DIM),
        "w_gate": w(ks[8], (DEPTH, D_MODEL, D_FF), D_MODEL),
        "w_up": w(ks[9], (DEPTH, D_MODEL, D_FF), D_MODEL),
        "w_down": w(ks[10], (DEPTH, D_FF, D_MODEL), D_FF),
        "norm_final": 1.0 + 0.02 * jax.random.normal(ks[11], (D_MODEL,), f32),
    }

def first_block(x, norm_mix, norm_ffn, w_qkv_a, w_out_a, sink_a, w_qkv_b, w_out_b,
              w_gate, w_up, w_down, norm_final):
    for i in range(DEPTH):
        h = rmsnorm(x, norm_mix[i])
        j = i // 2
        if i % 2 == 0:
            x = x + window_gqa_sink(h, w_qkv_a[j], w_out_a[j], sink_a[j])
        else:
            x = x + dilated_mixture_attention(h, w_qkv_b[j], w_out_b[j])
        h = rmsnorm(x, norm_ffn[i])
        x = x + swiglu(h, w_gate[i], w_up[i], w_down[i])
    return rmsnorm(x, norm_final)


DEPTH_2 = 1

CTX_LEN = 256
GRID_W = 64
H_M = 8
D_HM = 64
W_M = H_M * D_HM
H_R = 8
D_HR = 64
W_R = H_R * D_HR
MIX_W = W_M + W_R
W_LORA = 64
A_LORA = 64
G_LORA = 128
CONV_K = 3
CONV_CH = 2 * W_M + 3 * W_R
SECTION_WIDTHS = (W_M, W_M, W_R, W_R, W_R, W_M, W_M, 4 * H_M, W_LORA, W_LORA, A_LORA, G_LORA)
IN_COLS = sum(SECTION_WIDTHS)
SPLIT_POINTS = tuple(int(v) for v in np.cumsum(SECTION_WIDTHS)[:-1])
CHUNK = 64
N_GROUPS = 4
E_PER_GROUP = 8
N_EXPERTS = N_GROUPS * E_PER_GROUP
TOP_K_IN_GROUP = 2
D_EXPERT = 512
MOE_BLOCK = 256
ALPHA = (2.0 * DEPTH_2) ** 0.25
BETA = (8.0 * DEPTH_2) ** -0.25
DECAY_SCALE = math.exp(-0.5)
LN_EPS = 1e-6
GN_EPS = 64e-5


def _layernorm(z, gain=None, bias=None):
    zf = z.astype(jnp.float32)
    mu = jnp.mean(zf, -1, keepdims=True)
    var = jnp.mean(jnp.square(zf - mu), -1, keepdims=True)
    y = (zf - mu) * lax.rsqrt(var + LN_EPS)
    if gain is not None:
        y = y * gain + bias
    return y.astype(z.dtype)

def _headnorm(z, eps):
    zf = z.astype(jnp.float32)
    mu = jnp.mean(zf, -1, keepdims=True)
    var = jnp.mean(jnp.square(zf - mu), -1, keepdims=True)
    return (zf - mu) * lax.rsqrt(var + eps)

def _modulate(z, shift, scale):
    return _layernorm(z) * (1 + scale) + shift

def _rev_segments(u):
    return jnp.concatenate([jnp.flip(u[:, :CTX_LEN], 1), jnp.flip(u[:, CTX_LEN:], 1)], axis=1)

def _dir_stack(u_fwd, u_bwd):
    return jnp.concatenate([u_fwd, _rev_segments(u_bwd)], axis=0)

def _dir_merge(y):
    b = y.shape[0] // 2
    return y[:b] + _rev_segments(y[b:])

def _conv_grid(u, w, rows):
    b, l, ch = u.shape
    img = u.reshape(b, rows, l // rows, ch)
    out = lax.conv_general_dilated(img, w[:, :, None, :].astype(u.dtype), (1, 1), 'SAME',
                                   dimension_numbers=('NHWC', 'HWIO', 'NHWC'), feature_group_count=ch)
    return out.reshape(b, l, ch)

def _conv_seq(u, w_row):
    ch = u.shape[-1]
    return lax.conv_general_dilated(u, w_row[:, None, :].astype(u.dtype), (1,), 'SAME',
                                    dimension_numbers=('NWC', 'WIO', 'NWC'), feature_group_count=ch)

def _mlstm_chunkwise(q, k, v, log_i, log_f):
    z, t, h, dh = q.shape
    nc = t // CHUNK
    def chunks(a):
        a = a.astype(jnp.float32).reshape((z, nc, CHUNK, h) + a.shape[3:])
        return jnp.swapaxes(jnp.swapaxes(a, 0, 1), 2, 3)
    qc, kc, vc, lic, lfc = chunks(q), chunks(k), chunks(v), chunks(log_i), chunks(log_f)
    tri = jnp.tril(jnp.ones((CHUNK, CHUNK), bool))

    def step(carry, inp):
        c_mat, n_vec, m = carry
        qb, kb, vb, li, lf = inp
        b = jnp.cumsum(lf, -1)
        dmat = jnp.where(tri, b[..., :, None] - b[..., None, :] + li[..., None, :], -jnp.inf)
        m_inter = b + m[..., None]
        m_t = jnp.maximum(m_inter, jnp.max(dmat, -1))
        s = jnp.einsum('zhtd,zhsd->zhts', qb, kb) * jnp.exp(dmat - m_t[..., None])
        inter = jnp.exp(m_inter - m_t)
        num = inter[..., None] * jnp.einsum('zhtd,zhde->zhte', qb, c_mat) + jnp.einsum('zhts,zhse->zhte', s, vb)
        den = inter * jnp.einsum('zhtd,zhd->zht', qb, n_vec) + jnp.sum(s, -1)
        h_out = num / jnp.maximum(jnp.abs(den), jnp.exp(-m_t))[..., None]
        b_last = b[..., -1]
        g = b_last[..., None] - b + li
        m_new = jnp.maximum(b_last + m, jnp.max(g, -1))
        wts = jnp.exp(g - m_new[..., None])
        decay = jnp.exp(b_last + m - m_new)
        c_mat = decay[..., None, None] * c_mat + jnp.einsum('zhs,zhsd,zhse->zhde', wts, kb, vb)
        n_vec = decay[..., None] * n_vec + jnp.einsum('zhs,zhsd->zhd', wts, kb)
        return (c_mat, n_vec, m_new), h_out

    init = (jnp.zeros((z, h, dh, dh), jnp.float32), jnp.zeros((z, h, dh), jnp.float32), jnp.zeros((z, h), jnp.float32))
    _, hs = lax.scan(step, init, (qc, kc, vc, lic, lfc))
    return jnp.swapaxes(jnp.swapaxes(hs, 2, 3), 0, 1).reshape(z, t, h, dh)

def _mlstm_group(mq, mk, mv, mo, gates, b_i, b_f, norm_w):
    b, t, _ = mq.shape
    q = jax.nn.silu(mq).reshape(b, t, H_M, D_HM)
    k = jax.nn.silu(mk).reshape(b, t, H_M, D_HM) * (D_HM ** -0.5)
    v = mv.reshape(b, t, H_M, D_HM)
    gt = gates.astype(jnp.float32).reshape(b, t, 4, H_M)
    li_f = gt[:, :, 0] + b_i[0]
    lf_f = jax.nn.log_sigmoid(gt[:, :, 1] + b_f[0])
    li_b = gt[:, :, 2] + b_i[1]
    lf_b = jax.nn.log_sigmoid(gt[:, :, 3] + b_f[1])
    h = _mlstm_chunkwise(_dir_stack(q, q), _dir_stack(k, k), _dir_stack(v, v),
                         _dir_stack(li_f, li_b), _dir_stack(lf_f, lf_b))
    h = _headnorm(_dir_merge(h), LN_EPS) * norm_w.reshape(H_M, D_HM)
    return jax.nn.sigmoid(mo) * h.reshape(b, t, W_M)

def _rwkv7_scan(r, w, k, v, kh, a):
    z, t, h, n = r.shape
    seq = tuple(jnp.moveaxis(s.astype(jnp.float32), 1, 0) for s in (r, w, k, v, kh, a))

    def step(state, inp):
        r_t, w_t, k_t, v_t, kh_t, a_t = inp
        removed = jnp.einsum('zhvk,zhk->zhv', state, kh_t)
        state = (state * w_t[:, :, None, :] - removed[..., None] * (kh_t * a_t)[:, :, None, :]
                 + v_t[..., None] * k_t[:, :, None, :])
        return state, jnp.einsum('zhvk,zhk->zhv', state, r_t)

    _, y = lax.scan(step, jnp.zeros((z, h, n, n), jnp.float32), seq)
    return jnp.moveaxis(y, 0, 1)

def _rwkv7_group(rr, rk, rv, lw_f, lw_b, la, lg, w0, w_b_mat, a0, a_b_mat, g_b_mat, kk, ka, bonus_w, gn_w, gn_b):
    b, t, _ = rr.shape
    shp = (b, t, H_R, D_HR)
    w_fwd = jnp.exp(-DECAY_SCALE * jax.nn.sigmoid((w0[0] + jnp.tanh(lw_f) @ w_b_mat[0]).astype(jnp.float32)))
    w_bwd = jnp.exp(-DECAY_SCALE * jax.nn.sigmoid((w0[1] + jnp.tanh(lw_b) @ w_b_mat[1]).astype(jnp.float32)))
    a = jax.nn.sigmoid(a0 + la @ a_b_mat)
    g = jax.nn.sigmoid(lg) @ g_b_mat
    kap = (rk * kk).reshape(shp).astype(jnp.float32)
    kh = kap / jnp.maximum(jnp.sqrt(jnp.sum(jnp.square(kap), -1, keepdims=True)), 1e-12)
    kmod = (rk * (1 + (a - 1) * ka)).reshape(shp)
    r = rr.reshape(shp)
    v = rv.reshape(shp)
    a_h = a.reshape(shp)
    y = _rwkv7_scan(_dir_stack(r, r), _dir_stack(w_fwd.reshape(shp), w_bwd.reshape(shp)), _dir_stack(kmod, kmod),
                    _dir_stack(v, v), _dir_stack(kh, kh), _dir_stack(a_h, a_h))
    y = _headnorm(_dir_merge(y), GN_EPS) * gn_w.reshape(H_R, D_HR) + gn_b.reshape(H_R, D_HR)
    bonus = jnp.sum(r * kmod * bonus_w, -1, keepdims=True) * v
    return (y + bonus).reshape(b, t, W_R) * g

def _mixer(h_ctx, h_lat, rows, w_in, conv_w, m_bias_i, m_bias_f, m_norm_w, r_w0, r_wB, r_a0, r_aB, r_gB,
           r_kk, r_ka, r_bonus, r_norm_w, r_norm_b):
    p_ctx = h_ctx @ w_in
    p_lat = h_lat @ w_in
    p_ctx = jnp.concatenate([_conv_seq(p_ctx[..., :CONV_CH], conv_w[CONV_K // 2]), p_ctx[..., CONV_CH:]], -1)
    p_lat = jnp.concatenate([_conv_grid(p_lat[..., :CONV_CH], conv_w, rows), p_lat[..., CONV_CH:]], -1)
    u = jnp.concatenate([p_ctx, p_lat], axis=1)
    mq, mk, rr, rk, rv, mv, mo, gates, lw_f, lw_b, la, lg = jnp.split(u, SPLIT_POINTS, axis=-1)
    out_m = _mlstm_group(mq, mk, mv, mo, gates, m_bias_i, m_bias_f, m_norm_w)
    out_r = _rwkv7_group(rr, rk, rv, lw_f, lw_b, la, lg, r_w0, r_wB, r_a0, r_aB, r_gB, r_kk, r_ka, r_bonus,
                         r_norm_w, r_norm_b)
    return jnp.concatenate([out_m.astype(out_r.dtype), out_r], -1)

def _hier_moe(h, rt_g, rt_g_b, rt_e, rt_e_b, ex_gate, ex_up, ex_down):
    b, t, d = h.shape
    tok = h.reshape(b * t, d)
    n = tok.shape[0]
    lg = (tok @ rt_g + rt_g_b).astype(jnp.float32)
    p_grp = jax.nn.softmax(lg, axis=-1)
    grp = jnp.argmax(lg, axis=-1).astype(jnp.int32)
    p_top = jnp.take_along_axis(p_grp, grp[:, None], axis=-1)
    le = (tok @ rt_e + rt_e_b).astype(jnp.float32).reshape(n, N_GROUPS, E_PER_GROUP)
    le_grp = jnp.take_along_axis(le, jnp.broadcast_to(grp[:, None, None], (n, 1, E_PER_GROUP)), axis=1)[:, 0]
    top_val, top_idx = lax.top_k(le_grp, TOP_K_IN_GROUP)
    wts = jax.nn.softmax(top_val, axis=-1) * p_top
    e_flat = (grp[:, None] * E_PER_GROUP + top_idx.astype(jnp.int32)).reshape(-1)
    w_flat = wts.reshape(-1)
    t_flat = jnp.repeat(jnp.arange(n, dtype=jnp.int32), TOP_K_IN_GROUP)
    order = jnp.argsort(e_flat)
    e_s, t_s, w_s = e_flat[order], t_flat[order], w_flat[order]
    counts = jnp.zeros((N_EXPERTS,), jnp.int32).at[e_flat].add(1)
    starts = jnp.cumsum(counts) - counts
    padded = (counts + MOE_BLOCK - 1) // MOE_BLOCK * MOE_BLOCK
    pad_ends = jnp.cumsum(padded)
    pad_starts = pad_ends - padded
    dest = pad_starts[e_s] + jnp.arange(e_s.shape[0], dtype=jnp.int32) - starts[e_s]
    n_pairs = n * TOP_K_IN_GROUP
    buf = (-(-n_pairs // MOE_BLOCK) + N_EXPERTS) * MOE_BLOCK
    tok_buf = jnp.full((buf,), n, jnp.int32).at[dest].set(t_s)
    w_buf = jnp.zeros((buf,), w_s.dtype).at[dest].set(w_s)
    n_blk = buf // MOE_BLOCK
    blk_exp = jnp.minimum(jnp.searchsorted(pad_ends, jnp.arange(n_blk, dtype=jnp.int32) * MOE_BLOCK, side='right'),
                          N_EXPERTS - 1)
    tok_pad = jnp.concatenate([tok, jnp.zeros((1, d), tok.dtype)], 0)

    def expert_block(args):
        idx, w, e = args
        xb = tok_pad[idx]
        hb = jax.nn.silu(xb @ ex_gate[e]) * (xb @ ex_up[e])
        return (hb @ ex_down[e]) * w[:, None]

    y = lax.map(expert_block, (tok_buf.reshape(n_blk, MOE_BLOCK), w_buf.reshape(n_blk, MOE_BLOCK), blk_exp))
    out = jnp.zeros((n + 1, d), y.dtype).at[tok_buf].add(y.reshape(buf, d))
    return out[:n].reshape(b, t, d).astype(h.dtype)

def second_inputs(seed: int = 0) -> dict:
    key = jax.random.key(seed)
    ks = jax.random.split(key, 40)
    def nrm(k, shape, s):
        return jax.random.normal(k, shape, jnp.float32) * s
    L = DEPTH_2
    return {
        'x': nrm(ks[0], (BATCH, SEQ, D_MODEL), 1.0),
        'c': nrm(ks[1], (BATCH, D_MODEL), 1.0),
        'ctx': nrm(ks[2], (BATCH, CTX_LEN, D_MODEL), 1.0),
        'c_ctx': nrm(ks[3], (D_MODEL,), 1.0),
        'w_ada': nrm(ks[4], (L, D_MODEL, 6 * D_MODEL), D_MODEL ** -0.5),
        'b_ada': nrm(ks[5], (L, 6 * D_MODEL), 0.02),
        'w_in': nrm(ks[6], (L, D_MODEL, IN_COLS), D_MODEL ** -0.5),
        'conv_w': nrm(ks[7], (L, CONV_K, CONV_K, CONV_CH), 0.3),
        'm_bias_i': nrm(ks[8], (L, 2, H_M), 0.5),
        'm_bias_f': 3.0 + nrm(ks[9], (L, 2, H_M), 0.5),
        'm_norm_w': 1.0 + nrm(ks[10], (L, W_M), 0.05),
        'r_w0': nrm(ks[11], (L, 2, W_R), 0.5),
        'r_wB': nrm(ks[12], (L, 2, W_LORA, W_R), W_LORA ** -0.5),
        'r_a0': nrm(ks[13], (L, W_R), 0.5),
        'r_aB': nrm(ks[14], (L, A_LORA, W_R), A_LORA ** -0.5),
        'r_gB': nrm(ks[15], (L, G_LORA, W_R), G_LORA ** -0.5),
        'r_kk': 0.85 + nrm(ks[16], (L, W_R), 0.05),
        'r_ka': 1.0 + nrm(ks[17], (L, W_R), 0.05),
        'r_bonus': nrm(ks[18], (L, H_R, D_HR), 0.1),
        'r_norm_w': 1.0 + nrm(ks[19], (L, W_R), 0.05),
        'r_norm_b': nrm(ks[20], (L, W_R), 0.02),
        'w_out': nrm(ks[21], (L, MIX_W, D_MODEL), BETA * MIX_W ** -0.5),
        'ln1_g': 1.0 + nrm(ks[22], (L, D_MODEL), 0.05),
        'ln1_b': nrm(ks[23], (L, D_MODEL), 0.02),
        'ln2_g': 1.0 + nrm(ks[24], (L, D_MODEL), 0.05),
        'ln2_b': nrm(ks[25], (L, D_MODEL), 0.02),
        'rt_g': nrm(ks[26], (L, D_MODEL, N_GROUPS), D_MODEL ** -0.5),
        'rt_g_b': nrm(ks[27], (L, N_GROUPS), 0.01),
        'rt_e': nrm(ks[28], (L, D_MODEL, N_EXPERTS), D_MODEL ** -0.5),
        'rt_e_b': nrm(ks[29], (L, N_EXPERTS), 0.01),
        'ex_gate': nrm(ks[30], (L, N_EXPERTS, D_MODEL, D_EXPERT), D_MODEL ** -0.5),
        'ex_up': nrm(ks[31], (L, N_EXPERTS, D_MODEL, D_EXPERT), D_MODEL ** -0.5),
        'ex_down': nrm(ks[32], (L, N_EXPERTS, D_EXPERT, D_MODEL), BETA * D_EXPERT ** -0.5),
    }

def second_block(x, c, ctx, c_ctx, w_ada, b_ada, w_in, conv_w, m_bias_i, m_bias_f, m_norm_w, r_w0, r_wB, r_a0, r_aB,
              r_gB, r_kk, r_ka, r_bonus, r_norm_w, r_norm_b, w_out, ln1_g, ln1_b, ln2_g, ln2_b, rt_g, rt_g_b, rt_e,
              rt_e_b, ex_gate, ex_up, ex_down):
    rows = x.shape[1] // GRID_W
    for l in range(DEPTH_2):
        mod = jax.nn.silu(c) @ w_ada[l] + b_ada[l]
        mod_c = jax.nn.silu(c_ctx) @ w_ada[l] + b_ada[l]
        sh1, sc1, g1, sh2, sc2, g2 = jnp.split(mod[:, None, :], 6, axis=-1)
        sh1c, sc1c, g1c, sh2c, sc2c, g2c = jnp.split(mod_c, 6)
        mixed = _mixer(_modulate(ctx, sh1c, sc1c), _modulate(x, sh1, sc1), rows, w_in[l], conv_w[l], m_bias_i[l],
                       m_bias_f[l], m_norm_w[l], r_w0[l], r_wB[l], r_a0[l], r_aB[l], r_gB[l], r_kk[l], r_ka[l],
                       r_bonus[l], r_norm_w[l], r_norm_b[l])
        x = _layernorm(ALPHA * x + g1 * (mixed[:, CTX_LEN:] @ w_out[l]), ln1_g[l], ln1_b[l])
        ffn = _hier_moe(_modulate(x, sh2, sc2), rt_g[l], rt_g_b[l], rt_e[l], rt_e_b[l], ex_gate[l], ex_up[l], ex_down[l])
        x = _layernorm(ALPHA * x + g2 * ffn, ln2_g[l], ln2_b[l])
        if l + 1 < DEPTH_2:
            ctx = _layernorm(ALPHA * ctx + g1c * (mixed[:, :CTX_LEN] @ w_out[l]), ln1_g[l], ln1_b[l])
            ffn_c = _hier_moe(_modulate(ctx, sh2c, sc2c), rt_g[l], rt_g_b[l], rt_e[l], rt_e_b[l], ex_gate[l],
                              ex_up[l], ex_down[l])
            ctx = _layernorm(ALPHA * ctx + g2c * ffn_c, ln2_g[l], ln2_b[l])
    return x


def setup_inputs(seed=0):
    out = dict(first_inputs(seed))
    for name, value in second_inputs(seed + 1).items():
        if name != "x":
            out[name + "_2"] = value
    return out


def reference(
    x, norm_mix, norm_ffn, w_qkv_a, w_out_a, sink_a, w_qkv_b, w_out_b, w_gate, w_up, w_down,
    norm_final, c_2, ctx_2, c_ctx_2, w_ada_2, b_ada_2, w_in_2, conv_w_2, m_bias_i_2, m_bias_f_2,
    m_norm_w_2, r_w0_2, r_wB_2, r_a0_2, r_aB_2, r_gB_2, r_kk_2, r_ka_2, r_bonus_2, r_norm_w_2,
    r_norm_b_2, w_out_2, ln1_g_2, ln1_b_2, ln2_g_2, ln2_b_2, rt_g_2, rt_g_b_2, rt_e_2, rt_e_b_2,
    ex_gate_2, ex_up_2, ex_down_2,
):
    x = first_block(
        x, norm_mix, norm_ffn, w_qkv_a, w_out_a, sink_a, w_qkv_b, w_out_b, w_gate, w_up, w_down,
        norm_final,
    )
    return second_block(
        x, c_2, ctx_2, c_ctx_2, w_ada_2, b_ada_2, w_in_2, conv_w_2, m_bias_i_2, m_bias_f_2,
        m_norm_w_2, r_w0_2, r_wB_2, r_a0_2, r_aB_2, r_gB_2, r_kk_2, r_ka_2, r_bonus_2,
        r_norm_w_2, r_norm_b_2, w_out_2, ln1_g_2, ln1_b_2, ln2_g_2, ln2_b_2, rt_g_2, rt_g_b_2,
        rt_e_2, rt_e_b_2, ex_gate_2, ex_up_2, ex_down_2,
    )


_drawn_inputs = setup_inputs


def setup_inputs(seed=0):
    import zlib

    import numpy as np

    out = dict(_drawn_inputs(seed))
    spreads = {}
    factors = {'norm_mix': 3.337,
     'sink_a': 21.344,
     'ctx_2': 3.955,
     'c_ctx_2': 3.542,
     'm_bias_i_2': 14.157,
     'm_bias_f_2': 2.698,
     'm_norm_w_2': 4.641,
     'r_kk_2': 138.409,
     'r_ka_2': 3.158,
     'r_norm_w_2': 4.119,
     'r_norm_b_2': 19.394,
     'ln2_b_2': 2.823,
     'rt_g_b_2': 19.681,
     'rt_e_b_2': 14.563}
    for name, (base, spread) in spreads.items():
        noise = np.random.default_rng([zlib.crc32(name.encode()), seed]).standard_normal(out[name].shape)
        drawn = base * np.exp(spread * noise) if base else spread * noise
        out[name] = jnp.asarray(drawn.astype(out[name].dtype))
    for name, factor in factors.items():
        out[name] = (out[name] * factor).astype(out[name].dtype)
    return out
```

```python
from contextlib import ExitStack

import numpy as np

import concourse.bass as bass
from concourse import mybir

F32 = mybir.dt.float32
U32 = mybir.dt.uint32
ALU = mybir.AluOpType
ACT = mybir.ActivationFunctionType
AX = mybir.AxisListType

P = 128
D = 1024
DC = D // P
T = 512
TT = T // P
DH = 64
HEADS = 16
D_FF = -(-8 * D // (3 * 256)) * 256
FC = D_FF // P
BLOCKS = 16
UNIT = BLOCKS * P
RING = 4
EPS = 1e-6
FAR = 1e33

U_QKV_A = 12 * DC // BLOCKS
U_OUT = DC * DC // BLOCKS
U_GATE_UP = FC
U_DOWN = FC * DC // BLOCKS
U_V_B = 3 * DC * DC // BLOCKS
U_QK_B = 3


class Weights:

    def __init__(self, ring, stream, loaded, used, units):
        self.ring, self.stream, self.loaded, self.used, self.units = ring, stream, loaded, used, units
        self.at = 0

    def arrived(self, pe, j, i):
        n = self.at + i
        pe.wait_ge(self.loaded[n % RING], 16 * (j + (n // RING + 1)))
        return self.ring[n % RING]

    def load(self, sp, n):
        sp.dma_start(self.ring[n % RING][:, :], self.stream[n]).then_inc(self.loaded[n % RING], 16)

    def feed(self, sp, units):
        def one(j, i):
            n = self.at + i
            sp.wait_ge(self.used, j * RING + (n + 1))
            sp.dma_start(self.ring[n % RING][:, :], self.stream[j * RING + (n + RING)]).then_inc(
                self.loaded[n % RING], 16)
        last = max(0, min(units, self.units - RING - self.at))
        whole = last // RING
        if whole > 1:
            with sp.Fori(0, whole) as j:
                for i in range(RING):
                    one(j, i)
        else:
            whole = 0
        for i in range(whole * RING, last):
            one(0, i)


def over(eng, count, step, body, least=2):
    whole = count // step if count // step >= least else 0
    if whole:
        with eng.Fori(0, whole) as j:
            for i in range(step):
                body(j, i)
    for i in range(whole * step, count):
        body(0, i)


class Core:

    def __init__(self, nc):
        self.nc, self.retired = nc, []

    def semaphores(self, name, names):
        fresh = [self.nc.alloc_semaphore(f"{name}_{n}") for n in names]
        if self.retired:
            self.nc.clear_and_free_semaphores(self.retired)
        self.retired = fresh
        return fresh


def ident_of(c, n=P):
    return c.ident[0:n, 0:n]



def rms_stage(nc, c, src, dst, gain, name):
    with ExitStack() as ctx:
        sq = ctx.enter_context(nc.sbuf_tensor(f"{name}_sq", [P, DC, T], F32))
        rstd = ctx.enter_context(nc.sbuf_tensor(f"{name}_rstd", [P, 2, T], F32))
        squared, summed, mean_ready, root_ready, rstd_ready, scaled = c.semaphores(
            name, ("squared", "summed", "mean_ready", "root_ready", "rstd_ready", "scaled"))
        with nc.Block() as block:
            @block.scalar
            def _(act):
                for k in range(DC):
                    act.activation(sq[:, k, :], src[:, k, :], ACT.Square).then_inc(squared, 1)
                act.wait_ge(mean_ready, 1)
                act.activation(rstd[:, 1, :], rstd[:, 0, :], ACT.Sqrt).then_inc(root_ready, 1)

            @block.tensor
            def _(pe):
                for k in range(DC):
                    pe.wait_ge(squared, k + 1)
                    m = pe.matmul(c.bank[0][:, :], c.ones[:, :], sq[:, k, :], start=(k == 0), stop=(k == DC - 1))
                m.then_inc(summed, 1)

            @block.vector
            def _(dve):
                dve.wait_ge(summed, 1)
                dve.tensor_scalar(rstd[:, 0, :], c.bank[0][:, :], 1.0 / D, EPS, ALU.mult, ALU.add).then_inc(mean_ready, 1)
                dve.wait_ge(root_ready, 1)
                dve.reciprocal(rstd[:, 0, :], rstd[:, 1, :]).then_inc(rstd_ready, 1)
                dve.wait_ge(rstd_ready, 1)
                for k in range(DC):
                    dve.scalar_tensor_tensor(out=dst[:, k, :], in0=src[:, k, :], scalar=c.cols[:, gain + k:gain + k + 1],
                                             in1=rstd[:, 0, :], op0=ALU.mult, op1=ALU.mult).then_inc(scaled, 1)



def ffn_stage(nc, c, w, h, x, name):
    with ExitStack() as ctx:
        hidden = ctx.enter_context(nc.sbuf_tensor(f"{name}_hidden", [P, FC, T], F32))
        silu = ctx.enter_context(nc.sbuf_tensor(f"{name}_silu", [P, 2, T], F32))
        gate_done, silu_ready, hidden_ready, down_done, added = c.semaphores(
            name, ("gate_done", "silu_ready", "hidden_ready", "down_done", "added"))
        bank = c.bank
        with nc.Block() as block:
            @block.sync
            def _(sp):
                w.feed(sp, U_GATE_UP + U_DOWN)

            @block.tensor
            def _(pe):
                def gate_up(first, j, i):
                    unit = w.arrived(pe, j, first + i)
                    if first + i >= 2:
                        pe.wait_ge(hidden_ready, j * RING + (first + i - 1))
                    for half in range(2):
                        for k in range(DC):
                            b = (half * DC + k) * P
                            m = pe.matmul(bank[2 * (i % 2) + half][:, :], unit[:, b:b + P], h[:, k, :],
                                          start=(k == 0), stop=(k == DC - 1))
                        m.then_inc((gate_done, w.used)[half], 1)

                for i in range(RING):
                    gate_up(0, 0, i)
                over(pe, FC - RING, RING, lambda j, i: gate_up(RING, j, i))
                pe.wait_ge(hidden_ready, FC)
                for m_ in range(DC):
                    if m_ >= 2:
                        pe.wait_ge(added, m_ - 1)
                    for k in range(FC):
                        b = m_ * FC + k
                        if b % BLOCKS == 0:
                            unit = w.arrived(pe, 0, FC + b // BLOCKS)
                        q = b % BLOCKS * P
                        m = pe.matmul(bank[4 + m_ % 2][:, :], unit[:, q:q + P], hidden[:, k, :],
                                      start=(k == 0), stop=(k == FC - 1))
                        if b % BLOCKS == BLOCKS - 1:
                            m.then_inc(w.used, 1)
                        elif k == FC - 1:
                            m.then_inc(down_done, 1)

            @block.scalar
            def _(act):
                def one(j, i):
                    act.wait_ge(gate_done, j * RING + (i + 1))
                    act.activation(silu[:, i % 2, :], bank[2 * (i % 2)][:, :], ACT.Silu).then_inc(silu_ready, 1)
                over(act, FC, RING, one)

            @block.vector
            def _(dve):
                def one(j, i):
                    dve.wait_ge(w.used, j * RING + (w.at + i + 1))
                    dve.wait_ge(silu_ready, j * RING + (i + 1))
                    dve.tensor_tensor(hidden[:, j * RING + i, :], silu[:, i % 2, :], bank[2 * (i % 2) + 1][:, :],
                                      ALU.mult).then_inc(hidden_ready, 1)
                over(dve, FC, RING, one)
                for m_ in range(DC):
                    if m_ < DC - 1:
                        dve.wait_ge(down_done, m_ + 1)
                    else:
                        dve.wait_ge(w.used, w.at + U_GATE_UP + U_DOWN)
                    dve.tensor_tensor(x[:, m_, :], x[:, m_, :], bank[4 + m_ % 2][:, :], ALU.add).then_inc(added, 1)
    w.at += U_GATE_UP + U_DOWN



def out_stage(nc, c, w, o, x, name):
    with ExitStack() as ctx:
        chunk_done, added = c.semaphores(name, ("chunk_done", "added"))
        bank = c.bank
        with nc.Block() as block:
            @block.sync
            def _(sp):
                w.feed(sp, U_OUT)

            @block.tensor
            def _(pe):
                for m_ in range(DC):
                    unit = w.arrived(pe, 0, m_ // 2) if m_ % 2 == 0 else unit
                    for k in range(DC):
                        b = (m_ % 2 * DC + k) * P
                        m = pe.matmul(bank[m_][:, :], unit[:, b:b + P], o[:, k, :], start=(k == 0), stop=(k == DC - 1))
                    m.then_inc((chunk_done, w.used)[m_ % 2], 1)

            @block.vector
            def _(dve):
                for m_ in range(DC):
                    if m_ % 2 == 0:
                        dve.wait_ge(chunk_done, m_ // 2 + 1)
                    else:
                        dve.wait_ge(w.used, w.at + m_ // 2 + 1)
                    dve.tensor_tensor(x[:, m_, :], x[:, m_, :], bank[m_][:, :], ALU.add).then_inc(added, 1)
    w.at += U_OUT


def project_a_stage(nc, c, w, h, q, k_, v):
    KVC = 2
    chunk_done, copied, v_done, v_copied = c.semaphores("proj_a", ("chunk_done", "copied", "v_done", "v_copied"))
    bank = c.bank
    with nc.Block() as block:
        @block.sync
        def _(sp):
            w.feed(sp, U_QKV_A)

        @block.tensor
        def _(pe):
            for m_ in range(DC + KVC):
                if m_ % 2 == 0:
                    unit = w.arrived(pe, 0, m_ // 2)
                if m_ >= 4:
                    pe.wait_ge(copied, m_ - 3)
                for k in range(DC):
                    b = (m_ % 2 * DC + k) * P
                    m = pe.matmul(bank[m_ % 4][:, :], unit[:, b:b + P], h[:, k, :], start=(k == 0), stop=(k == DC - 1))
                m.then_inc((chunk_done, w.used)[m_ % 2], 1)
            unit = w.arrived(pe, 0, U_QKV_A - 1)
            for t in range(TT):
                for k in range(DC):
                    m = pe.matmul(bank[4 + t][:, 0:2 * P], h[:, k, t * P:(t + 1) * P], unit[:, 2 * k * P:2 * (k + 1) * P],
                                  start=(k == 0), stop=(k == DC - 1))
                m.then_inc(v_done if t < TT - 1 else w.used, 1)

        @block.scalar
        def _(act):
            for m_ in range(DC + KVC):
                if m_ % 2 == 0:
                    act.wait_ge(chunk_done, m_ // 2 + 1)
                else:
                    act.wait_ge(w.used, w.at + m_ // 2 + 1)
                if m_ < DC:
                    act.mul(q[:, m_, :], bank[m_ % 4][:, :], DH ** -0.5).then_inc(copied, 1)
                else:
                    act.copy(k_[:, m_ - DC, :], bank[m_ % 4][:, :]).then_inc(copied, 1)

        @block.vector
        def _(dve):
            for t in range(TT):
                if t < TT - 1:
                    dve.wait_ge(v_done, t + 1)
                else:
                    dve.wait_ge(w.used, w.at + U_QKV_A)
                dve.tensor_copy(v[:, t, :], bank[4 + t][:, 0:2 * P]).then_inc(v_copied, 1)
    w.at += U_QKV_A


class Item:

    def __init__(self, head, half, slope, dist, scores, values, out, pair=0):
        self.head, self.half, self.slope, self.dist, self.scores, self.values, self.out, self.pair = (
            head, half, slope, dist, scores, values, out, pair)
        self.keys = dist.shape[-1]


def attention_stage(nc, c, w, items, name, sink, project=None):
    N = len(items)
    WIDE = max(i.keys for i in items)
    LAG = 2
    SB = LAG + 1
    with ExitStack() as ctx:
        def sb(n, shape):
            return ctx.enter_context(nc.sbuf_tensor(f"{name}_{n}", shape, F32))
        bias = sb("bias", [P, 2, WIDE])
        prob = sb("prob", [P, SB, WIDE])
        probT = sb("probT", [P, 2, WIDE])
        diag = sb("diag", [P, 2, P])
        top = sb("top", [P, N])
        negtop = sb("negtop", [P, N])
        den = sb("den", [P, N])
        sunk = sb("sunk", [P, N])
        total = sb("total", [P, N])
        rden = sb("rden", [P, N])
        (bias_ready, scores_done, biased, negtop_ready, prob_ready, sunk_ready, total_ready, rden_ready, diag_ready,
         turned, probT_ready, out_done, out_copied, pair_chunk_done, pair_chunk_copied) = c.semaphores(name, (
             "bias_ready", "scores_done", "biased", "negtop_ready", "prob_ready", "sunk_ready", "total_ready",
             "rden_ready", "diag_ready", "turned", "probT_ready", "out_done", "out_copied", "pair_chunk_done",
             "pair_chunk_copied"))
        S = [c.wide[0], c.wide[1]]
        PT = c.wide[2]
        O = c.bank[6]
        per = project.chunks if project else 0
        pairs = project.pairs if project else 0
        in_pair = N // pairs if pairs else N + 1

        def chunk_after(i):
            if not project:
                return None
            pair, j = i // in_pair + 1, i % in_pair
            return (pair, j) if pair < pairs and j < per else None

        with nc.Block() as block:
            if project:
                @block.sync
                def _(sp):
                    w.feed(sp, project.units)

            @block.gpsimd
            def _(pool):
                for i, it in enumerate(items):
                    if i >= 2:
                        pool.wait_ge(biased, i - 1)
                    pool.tensor_scalar(bias[:, i % 2, 0:it.keys], it.dist, -it.slope, None, ALU.mult).then_inc(bias_ready, 1)

            @block.tensor
            def _(pe):
                def pair_chunk(pair, j):
                    n = pair * per + j
                    if n >= 1:
                        pe.wait_ge(pair_chunk_copied, n)
                    unit = w.arrived(pe, 0, n // 2) if True else None
                    for k in range(DC):
                        b = (n % 2 * DC + k) * P
                        m = pe.matmul(c.bank[7][:, :], unit[:, b:b + P], project.h[:, k, :], start=(k == 0), stop=(k == DC - 1))
                    m.then_inc((pair_chunk_done, w.used)[n % 2], 1)

                def transposes(i):
                    it = items[i]
                    pe.wait_ge(prob_ready, i + 1)
                    pe.wait_ge(diag_ready, i + 1)
                    if i >= 1:
                        pe.wait_ge(probT_ready, i)
                    for t in range(it.keys // P):
                        m = pe.matmul(PT[:, t * P:(t + 1) * P], prob[:, i % SB, t * P:(t + 1) * P], diag[:, i % 2, :],
                                      start=True, stop=True)
                    m.then_inc(turned, 1)

                def values(i):
                    it = items[i]
                    pe.wait_ge(probT_ready, i + 1)
                    if i >= 1:
                        pe.wait_ge(out_copied, i)
                    n = it.keys // P
                    for t in range(n):
                        m = pe.matmul(O[it.half * DH:(it.half + 1) * DH, 0:P], it.values[t], probT[:, i % 2, t * P:(t + 1) * P],
                                      start=(t == 0), stop=(t == n - 1))
                    m.then_inc(out_done, 1)

                for j in range(per):
                    pair_chunk(0, j)
                for i in range(N + LAG + 1):
                    if i < N:
                        it = items[i]
                        if project and i % in_pair == 0:
                            pe.wait_ge(pair_chunk_copied, (i // in_pair + 1) * per)
                        if i >= 2:
                            pe.wait_ge(biased, i - 1)
                        for lhs, rhs, at in it.scores:
                            m = pe.matmul(S[i % 2][:, at:at + rhs.shape[-1]], lhs, rhs, start=True, stop=True)
                        m.then_inc(scores_done, 1)
                    if LAG + 1 <= i:
                        values(i - LAG - 1)
                    if i < N and chunk_after(i):
                        pair_chunk(*chunk_after(i))
                    if LAG <= i < N + LAG:
                        transposes(i - LAG)

            @block.vector
            def _(dve):
                def scale_of(i):
                    dve.wait_ge(prob_ready, i + 1)
                    if sink is not None:
                        dve.wait_ge(sunk_ready, i + 1)
                        dve.tensor_tensor(total[:, i:i + 1], den[:, i:i + 1], sunk[:, i:i + 1], ALU.add).then_inc(total_ready, 1)
                        dve.wait_ge(total_ready, i + 1)
                    src = den if sink is None else total
                    dve.reciprocal(rden[:, i:i + 1], src[:, i:i + 1]).then_inc(rden_ready, 1)
                    dve.wait_ge(rden_ready, i + 1)
                    if i >= 2:
                        dve.wait_ge(turned, i - 1)
                    dve.tensor_scalar(diag[:, i % 2, :], c.ident[:, :], rden[:, i:i + 1], None, ALU.mult).then_inc(diag_ready, 1)

                def copy_out(i):
                    it = items[i]
                    dve.wait_ge(out_done, i + 1)
                    dve.tensor_copy(it.out, O[it.half * DH:(it.half + 1) * DH, 0:P]).then_inc(out_copied, 1)

                for j in range(per):
                    if j % 2:
                        project.copy(dve, w, 0, j, pair_chunk_done, pair_chunk_copied)
                for i in range(N + LAG + 1):
                    if i < N:
                        it = items[i]
                        dve.wait_ge(scores_done, i + 1)
                        dve.wait_ge(bias_ready, i + 1)
                        if i >= SB:
                            dve.wait_ge(turned, i - SB + 1)
                        dve.tensor_tensor_reduce(prob[:, i % SB, 0:it.keys], S[i % 2][:, 0:it.keys], bias[:, i % 2, 0:it.keys],
                                                 1.0, -3e38, ALU.add, ALU.max, top[:, i:i + 1]).then_inc(biased, 1)
                        dve.wait_ge(biased, i + 1)
                        dve.tensor_scalar(negtop[:, i:i + 1], top[:, i:i + 1], -1.0, None, ALU.mult).then_inc(negtop_ready, 1)
                    if i >= 1 and i <= N:
                        scale_of(i - 1)
                    if i >= LAG + 1:
                        copy_out(i - LAG - 1)
                    if i < N and chunk_after(i) and chunk_after(i)[1] % 2:
                        project.copy(dve, w, *chunk_after(i), pair_chunk_done, pair_chunk_copied)

            @block.scalar
            def _(act):
                for j in range(per):
                    if j % 2 == 0:
                        project.copy(act, w, 0, j, pair_chunk_done, pair_chunk_copied)
                for i in range(N + LAG):
                    if i < N:
                        it = items[i]
                        act.wait_ge(negtop_ready, i + 1)
                        if sink is not None:
                            act.activation(sunk[:, i:i + 1], sink[:, it.head:it.head + 1], ACT.Exp,
                                           bias=negtop[:, i:i + 1]).then_inc(sunk_ready, 1)
                        act.activation(prob[:, i % SB, 0:it.keys], prob[:, i % SB, 0:it.keys], ACT.Exp,
                                       bias=negtop[:, i:i + 1], accum_out=den[:, i:i + 1]).then_inc(prob_ready, 1)
                    if i < N and chunk_after(i) and chunk_after(i)[1] % 2 == 0:
                        project.copy(act, w, *chunk_after(i), pair_chunk_done, pair_chunk_copied)
                    if i >= LAG:
                        n = i - LAG
                        act.wait_ge(turned, n + 1)
                        if n >= 2:
                            act.wait_ge(out_done, n - 1)
                        act.copy(probT[:, n % 2, 0:items[n].keys], PT[:, 0:items[n].keys]).then_inc(probT_ready, 1)
    if project:
        w.at += project.units


def slopes():
    return [2.0 ** (-8.0 * (h + 1) / HEADS) for h in range(HEADS)]


def attention_a_items(q, k_, v, dist, o):
    items = []
    for m in range(DC):
        for half in range(2):
            head = m // 4 * 8 + m % 4 + 4 * half
            kv = m // 4 * 2 + half
            rows = slice(half * DH, (half + 1) * DH)
            for b in range(TT):
                first, last = max(0, b - 1), min(TT, b + 2)
                off = (first - b + 1) * P
                keys = (last - first) * P
                items.append(Item(head, half, slopes()[head], dist[:, off:off + keys],
                                  [(q[rows, m, b * P:(b + 1) * P], k_[rows, m // 4, first * P:last * P], 0)],
                                  [v[:, t, kv * DH:(kv + 1) * DH] for t in range(first, last)],
                                  o[rows, m, b * P:(b + 1) * P]))
    return items


def attention_b_items(qk, v, dist, o):
    items = []
    for m in range(DC):
        for half in range(2):
            rows = slice(half * DH, (half + 1) * DH)
            buf = qk[m % 2]
            cols = slice((2 * m + half) * DH, (2 * m + half + 1) * DH)
            for r in range(TT):
                tile = slice(r * P, (r + 1) * P)
                items.append(Item(2 * m + half, half, slopes()[2 * m + half], dist[:, r, :],
                                  [(buf[rows, 0, tile], buf[rows, 1, :], 0), (buf[rows, 2, tile], buf[rows, 3, tile], T),
                                   (buf[rows, 4, tile], buf[rows, 5, tile], T + P)],
                                  [v[:, 0, t, cols] for t in range(TT)] + [v[:, 1, r, cols], v[:, 2, r, cols]],
                                  o[rows, m, :].rearrange("p (i r) -> p r i", r=4)[:, r, :]))
    return items


class ProjectB:
    chunks, pairs, units = 6, DC, U_QK_B * DC

    def __init__(self, c, h, qk):
        self.c, self.h, self.qk = c, h, qk

    def copy(self, eng, w, pair, j, done, copied):
        n = pair * self.chunks + j
        if n % 2 == 0:
            eng.wait_ge(done, n // 2 + 1)
        else:
            eng.wait_ge(w.used, w.at + n // 2 + 1)
        src, dst = self.c.bank[7][:, :], self.qk[pair % 2][:, j, :]
        if j != 1:
            src = src.rearrange("p (i r) -> p r i", r=4)
            dst = dst.rearrange("p (r i) -> p r i", r=4)
        if j % 2 == 0:
            eng.mul(dst, src, DH ** -0.5).then_inc(copied, 1)
        else:
            eng.tensor_copy(dst, src).then_inc(copied, 1)


def values_b_stage(nc, c, w, h, v):
    copied_act, copied_dve = c.semaphores("v_b", ("copied_act", "copied_dve"))
    with nc.Block() as block:
        @block.sync
        def _(sp):
            w.feed(sp, U_V_B)

        @block.tensor
        def _(pe):
            for n in range(6):
                g = n // 2
                if n >= 2:
                    pe.wait_ge(copied_act, 2 * (n - 1))
                    pe.wait_ge(copied_dve, 2 * (n - 1))
                for k in range(DC):
                    if k % 4 == 0:
                        unit = w.arrived(pe, 0, 2 * n + k // 4)
                    for t in range(TT):
                        hk = h[:, k, :]
                        lhs = hk[:, t * P:(t + 1) * P] if g == 0 else hk.rearrange("p (i r) -> p r i", r=4)[:, t, :]
                        m = pe.matmul(c.bank[n % 2 * 4 + t][:, :], lhs, unit[:, k % 4 * T:(k % 4 + 1) * T],
                                      start=(k == 0), stop=(k == DC - 1))
                    if k % 4 == 3:
                        m.then_inc(w.used, 1)

        @block.scalar
        def _(act):
            for n in range(6):
                act.wait_ge(w.used, w.at + 2 * n + 2)
                for t in range(2):
                    act.copy(v[:, n // 2, t, n % 2 * T:(n % 2 + 1) * T], c.bank[n % 2 * 4 + t][:, :]).then_inc(copied_act, 1)

        @block.vector
        def _(dve):
            for n in range(6):
                dve.wait_ge(w.used, w.at + 2 * n + 2)
                for t in range(2, 4):
                    dve.tensor_copy(v[:, n // 2, t, n % 2 * T:(n % 2 + 1) * T], c.bank[n % 2 * 4 + t][:, :]).then_inc(copied_dve, 1)
    w.at += U_V_B



DM = 512
MC = DM // P
NH = 8
CTX = 256
TA = CTX + T
TAT = TA // P
GRID_W = 64
ROWS = T // GRID_W
CONV_CHUNKS = 5 * MC
DECAY = float(np.exp(-0.5))
LN_EPS = 1e-6
GN_EPS = 64e-5
ALPHA = 2.0 ** 0.25
U_ADA = 6 * DC * DC // BLOCKS
U_IN = 16
U_IN_COLUMNS = 14
U_OUT2 = DC * DC // BLOCKS
E_GROUPS, E_EACH = 4, 8
EXPERTS = E_GROUPS * E_EACH
D_EXPERT = 512
EC = D_EXPERT // P
U_EXPERT = 6


def ada_stage(nc, c, w, cond, mod, mod1, bias):
    act_ready, summed, mod_ready, mod1_ready = c.semaphores("ada", ("act_ready", "summed", "mod_ready", "mod1_ready"))
    n_out = 6 * DC
    out = c.bank[0][:, 0:2 * n_out].rearrange("p (m s) -> p m s", s=2)
    with nc.Block() as block:
        @block.sync
        def _(sp):
            w.feed(sp, U_ADA)

        @block.scalar
        def _(act):
            act.activation(cond[:, :, :], cond[:, :, :], ACT.Silu).then_inc(act_ready, 1)

        @block.tensor
        def _(pe):
            pe.wait_ge(act_ready, 1)

            def one(j, i):
                unit = w.arrived(pe, j, i)
                for half in range(2):
                    for k in range(DC):
                        b = (half * DC + k) * P
                        m = pe.matmul(c.bank[0][:, bass.ds(j * (4 * RING) + (4 * i + 2 * half), 2)], unit[:, b:b + P],
                                      cond[:, k, :], start=(k == 0), stop=(k == DC - 1))
                m.then_inc(w.used, 1)
            over(pe, U_ADA, RING, one)

        @block.vector
        def _(dve):
            dve.wait_ge(w.used, w.at + U_ADA)
            dve.tensor_tensor(mod[:, :, :], out, bias.unsqueeze(2).broadcast_to([P, n_out, 2]), ALU.add).then_inc(mod_ready, 1)
            dve.wait_ge(mod_ready, 1)
            dve.tensor_scalar(mod1[:, :, :], mod[:, :, :], 1.0, None, ALU.add).then_inc(mod1_ready, 1)
    w.at += U_ADA


def layer_norm_stage(nc, c, src, dst, n, scale, shift, name, room=None):
    with ExitStack() as ctx:
        if room is None:
            room = ctx.enter_context(nc.sbuf_tensor(f"{name}_room", [P, (DC + 3) * n], F32))
        sq = room[:, 0:DC * n].rearrange("p (k t) -> p k t", t=n)
        st = room[:, DC * n:(DC + 3) * n].rearrange("p (k t) -> p k t", t=n)
        summed, mean_ready, centered, squared, square_summed, var_ready, root_ready, rstd_ready, scaled, done = c.semaphores(
            name, ("summed", "mean_ready", "centered", "squared", "square_summed", "var_ready", "root_ready",
                   "rstd_ready", "scaled", "done"))
        with nc.Block() as block:
            @block.tensor
            def _(pe):
                for k in range(DC):
                    m = pe.matmul(c.bank[0][:, 0:n], c.ones[:, :], src[:, k, :], start=(k == 0), stop=(k == DC - 1))
                m.then_inc(summed, 1)
                for k in range(DC):
                    pe.wait_ge(squared, k + 1)
                    m = pe.matmul(c.bank[1][:, 0:n], c.ones[:, :], sq[:, k, :], start=(k == 0), stop=(k == DC - 1))
                m.then_inc(square_summed, 1)

            @block.vector
            def _(dve):
                dve.wait_ge(summed, 1)
                dve.tensor_scalar(st[:, 0, :], c.bank[0][:, 0:n], 1.0 / D, None, ALU.mult).then_inc(mean_ready, 1)
                dve.wait_ge(mean_ready, 1)
                for k in range(DC):
                    dve.tensor_tensor(src[:, k, :], src[:, k, :], st[:, 0, :], ALU.subtract).then_inc(centered, 1)
                dve.wait_ge(square_summed, 1)
                dve.tensor_scalar(st[:, 1, :], c.bank[1][:, 0:n], 1.0 / D, LN_EPS, ALU.mult, ALU.add).then_inc(var_ready, 1)
                dve.wait_ge(root_ready, 1)
                dve.reciprocal(st[:, 1, :], st[:, 2, :]).then_inc(rstd_ready, 1)
                dve.wait_ge(rstd_ready, 1)
                dve.wait_ge(centered, DC)
                for k in range(DC):
                    dve.tensor_tensor(src[:, k, :], src[:, k, :], st[:, 1, :], ALU.mult).then_inc(scaled, 1)

            @block.scalar
            def _(act):
                for k in range(DC):
                    act.wait_ge(centered, k + 1)
                    act.activation(sq[:, k, :], src[:, k, :], ACT.Square).then_inc(squared, 1)
                act.wait_ge(var_ready, 1)
                act.activation(st[:, 2, :], st[:, 1, :], ACT.Sqrt).then_inc(root_ready, 1)
                for k in range(DC):
                    act.wait_ge(scaled, k + 1)
                    act.activation(dst[:, k, :], src[:, k, :], ACT.Identity, bias=shift(k), scale=scale(k)).then_inc(done, 1)



class Mixed:
    pass


def project_in_stage(nc, c, w, h, u, pads):
    items = [("conv", m) for m in range(CONV_CHUNKS)] + [("lw", 0), ("la", 0), ("lg", 0), ("li", 0), ("lf", 0)]
    items += [("mo", m) for m in range(MC)]
    chunk_of = []
    for kind, m in items:
        chunk_of.append(chunk_of[-1] + (kind != "lf") if chunk_of else 0)
    chunk_done, copied, convolved, v_copied_act, v_copied_dve, silu_done = c.semaphores(
        "proj_in", ("chunk_done", "copied", "convolved", "v_copied_act", "v_copied_dve", "silu_done"))
    ends = [i + 1 == len(items) or chunk_of[i + 1] != chunk_of[i] for i in range(len(items))]
    ends = [e and chunk_of[i] % 2 == 1 for i, e in enumerate(ends)]
    CONV = 12

    def complete(eng, n):
        if ends[n]:
            eng.wait_ge(w.used, w.at + chunk_of[n] // 2 + 1)
        else:
            eng.wait_ge(chunk_done, sum(not e for e in ends[:n + 1]))

    def lat(n):
        return c.wide[n % 4][:, 0:T]

    def con(n):
        return c.wide[n % 4][:, T:TA]

    with nc.Block() as block:
        @block.sync
        def _(sp):
            w.feed(sp, U_IN)

        @block.tensor
        def _(pe):
            for n, (kind, m) in enumerate(items):
                q = chunk_of[n]
                if kind != "lf" and q % 2 == 0:
                    unit = w.arrived(pe, 0, q // 2)
                if n >= 4:
                    pe.wait_ge(copied, n - 3)
                first = P // 2 if kind == "lf" else 0
                wide = P // 2 if kind in ("la", "li", "lf") else P
                parts = [(lat(n), slice(CTX, TA))] + ([(con(n), slice(0, CTX))] if kind not in ("mo", "lg") else [])
                for dst, toks in parts:
                    for k in range(DC):
                        b = (q % 2 * DC + k) * P + first
                        mm = pe.matmul(dst[0:wide, :], unit[:, b:b + wide], h[:, k, toks], start=(k == 0), stop=(k == DC - 1))
                mm.then_inc(w.used if ends[n] else chunk_done, 1)
            pe.wait_ge(copied, len(items))
            for k in range(DC):
                if k % 4 == 0:
                    unit = w.arrived(pe, 0, U_IN_COLUMNS + k // 4)
                for t in range(TAT):
                    mm = pe.matmul(c.bank[t][:, :], h[:, k, t * P:(t + 1) * P], unit[:, k % 4 * DM:(k % 4 + 1) * DM],
                                   start=(k == 0), stop=(k == DC - 1))
                if k % 4 == 3:
                    mm.then_inc(w.used, 1)

        @block.scalar
        def _(act):
            def silu(m):
                act.wait_ge(convolved, CONV * (m + 1))
                act.activation(u.conv[:, m, :], u.conv[:, m, :], ACT.Silu).then_inc(silu_done, 1)

            for n, (kind, m) in enumerate(items):
                complete(act, n)
                if kind == "conv":
                    grid, seq = pads[m % 2]
                    if m >= 2:
                        act.wait_ge(convolved, CONV * (m - 1))
                    act.copy(seq[:, 1:CTX + 1], con(n))
                    act.copy(grid[:, 1:ROWS + 1, 1:GRID_W + 1], lat(n).rearrange("p (r x) -> p r x", x=GRID_W)).then_inc(copied, 1)
                    if 3 <= m < 3 + 2 * MC:
                        silu(m - 3)
                elif kind == "lw":
                    act.activation(u.lw[:, CTX:TA], lat(n), ACT.Tanh)
                    act.activation(u.lw[:, 0:CTX], con(n), ACT.Tanh).then_inc(copied, 1)
                elif kind == "la":
                    act.copy(u.la[:, CTX:TA], lat(n)[0:64, :])
                    act.copy(u.la[:, 0:CTX], con(n)[0:64, :]).then_inc(copied, 1)
                elif kind == "lg":
                    act.activation(u.lg[:, :], lat(n), ACT.Sigmoid).then_inc(copied, 1)
                elif kind in ("li", "lf"):
                    dst, b = (u.li, u.bias[0:64, 0:1]) if kind == "li" else (u.lf, u.bias[0:64, 1:2])
                    act.activation(dst[:, CTX:TA], lat(n)[0:64, :], ACT.Identity, bias=b)
                    act.activation(dst[:, 0:CTX], con(n)[0:64, :], ACT.Identity, bias=b).then_inc(copied, 1)
                else:
                    act.activation(u.mo[:, m, :], lat(n), ACT.Sigmoid).then_inc(copied, 1)
            act.wait_ge(w.used, w.at + U_IN)
            for t in range(3):
                act.copy(u.v1[:, t, :, 0:DH], c.bank[t].rearrange("p (h e) -> p h e", e=DH)).then_inc(v_copied_act, 1)

        @block.vector
        def _(dve):
            for m in range(CONV_CHUNKS):
                grid, seq = pads[m % 2]
                dve.wait_ge(copied, m + 1)
                at = CONV * m
                go = u.conv[:, m, CTX:TA].rearrange("p (r x) -> p r x", x=GRID_W)
                so = u.conv[:, m, 0:CTX]

                def weight(dy, dx):
                    col = COLS["conv"] + (3 * dy + dx) * CONV_CHUNKS + m
                    return c.cols[:, col:col + 1]

                def shifted(dy, dx):
                    return grid[:, dy:dy + ROWS, dx:dx + GRID_W]

                dve.tensor_scalar(go, shifted(0, 0), weight(0, 0), None, ALU.mult).then_inc(convolved, 1)
                dve.tensor_scalar(so, seq[:, 0:CTX], weight(1, 0), None, ALU.mult).then_inc(convolved, 1)
                step = 2
                for tap in range(1, 9):
                    dy, dx = tap // 3, tap % 3
                    dve.wait_ge(convolved, at + step - (1 if tap <= 3 else 0))
                    dve.scalar_tensor_tensor(out=go, in0=shifted(dy, dx), scalar=weight(dy, dx), in1=go,
                                             op0=ALU.mult, op1=ALU.add).then_inc(convolved, 1)
                    step += 1
                    if tap <= 2:
                        dve.wait_ge(convolved, at + step - 1)
                        dve.scalar_tensor_tensor(out=so, in0=seq[:, tap:tap + CTX], scalar=weight(1, tap), in1=so,
                                                 op0=ALU.mult, op1=ALU.add).then_inc(convolved, 1)
                        step += 1
                assert step == CONV
            dve.wait_ge(w.used, w.at + U_IN)
            for t in range(3, TAT):
                dve.tensor_copy(u.v1[:, t, :, 0:DH], c.bank[t].rearrange("p (h e) -> p h e", e=DH)).then_inc(v_copied_dve, 1)
    w.at += U_IN



ORDER = ([0, 1, 2, 3, 4, 5], [1, 0, 5, 4, 3, 2])
SIDE = (0, 32)
GR = 40


def chain_of(eng, sem):
    count = [0]

    def step(ins, wait=True):
        ins.then_inc(sem, 1)
        count[0] += 1
        if wait:
            eng.wait_ge(sem, count[0])
        return count[0]
    return step


def gates_stage(nc, c, u, g):
    dve_step, neg_ready, exp_ready, ln_ready, pre_ready, post_ready, turned, cols_copied, spread, spread_copied = c.semaphores(
        "gates", ("dve_step", "neg_ready", "exp_ready", "ln_ready", "pre_ready", "post_ready", "turned", "cols_copied",
                  "spread", "spread_copied"))
    R = slice(0, GR)

    def tiles(x):
        return x[R, :].rearrange("p (j t) -> p j t", t=P)

    with ExitStack() as ctx:
        def sb(n, shape):
            return ctx.enter_context(nc.sbuf_tensor(f"gates_{n}", shape, F32))
        low, arg, m, b = (g.temps[:, n, :] for n in range(4))
        small, reset = sb("small", [GR, 2, TAT]), g.reset
        with nc.Block() as block:
            @block.vector
            def _(dve):
                step = chain_of(dve, dve_step)
                step(dve.memset(reset[:, :], 1.0))
                step(dve.memset(reset[0:32, 0:TA:P], 0.0))
                step(dve.memset(reset[32:GR, P - 1:TA:P], 0.0))
                step(dve.tensor_scalar(low[:, :], u.lf[R, :], 0.0, None, ALU.min))
                dve.scalar_tensor_tensor(out=arg[:, :], in0=low[:, :], scalar=2.0, in1=u.lf[R, :], op0=ALU.mult,
                                         op1=ALU.subtract).then_inc(neg_ready, 1)
                dve.wait_ge(ln_ready, 1)
                step(dve.tensor_tensor(low[:, :], low[:, :], arg[:, :], ALU.subtract))
                for side, rev in ((slice(0, 32), False), (slice(32, GR), True)):
                    if not rev:
                        step(dve.tensor_tensor_scan(m[side, :], low[side, :], u.li[side, :], 0.0, ALU.add, ALU.max))
                        step(dve.tensor_tensor_scan(b[side, :], reset[side, :], low[side, :], 0.0, ALU.mult, ALU.add))
                    else:
                        for lo, hi, init in ((0, CTX, 0.0), (CTX, TA, m[side, 0:1])):
                            def back(x):
                                return x[side, lo:hi][:, ::-1]
                            step(dve.tensor_tensor_scan(back(m), back(low), back(u.li), init, ALU.add, ALU.max))
                            step(dve.tensor_tensor_scan(back(b), back(reset), back(low), 0.0, ALU.mult, ALU.add))
                step(dve.tensor_tensor(g.bm[:, :], b[:, :], m[:, :], ALU.subtract))
                step(dve.tensor_tensor(g.rows[:, 0, :], u.li[R, :], b[:, :], ALU.subtract))
                step(dve.memset(small[:, :, :], 0.0))
                for d in range(2):
                    side = slice(SIDE[d], SIDE[d] + 8)
                    end = 0 if d else P - 1
                    step(dve.tensor_copy(small[side, 1, :], g.bm[side, end:TA:P]))
                    for before, tile in zip(ORDER[d], ORDER[d][1:]):
                        at = before * P + end
                        step(dve.tensor_copy(small[side, 0, tile:tile + 1], m[side, at:at + 1]))
                step(dve.tensor_tensor(tiles(g.inter), tiles(g.bm), small[:, 0, :].unsqueeze(2).broadcast_to([GR, TAT, P]), ALU.add))
                step(dve.tensor_tensor(g.rows[:, 1, :].rearrange("p (j t) -> p j t", t=P),
                                       g.rows[:, 0, :].rearrange("p (j t) -> p j t", t=P),
                                       small[:, 1, :].unsqueeze(2).broadcast_to([GR, TAT, P]), ALU.add))
                dve.tensor_scalar(g.rows[:, 2, :], m[:, :], -1.0, None, ALU.mult).then_inc(pre_ready, 1)
                dve.wait_ge(turned, 3 * TAT)
                dve.tensor_copy(g.cols[:, 0:9, :], c.bank[0][:, 0:9 * GR].rearrange("p (n r) -> p n r", r=GR)).then_inc(cols_copied, 1)
                dve.tensor_copy(g.cols[:, 9:18, :], c.bank[1][:, 0:9 * GR].rearrange("p (n r) -> p n r", r=GR)).then_inc(cols_copied, 1)
                for d in range(2):
                    for mm in range(MC):
                        n = d * MC + mm
                        dve.wait_ge(spread, n + 1)
                        dve.scalar_tensor_tensor(out=g.qi[:, d, mm, :], in0=u.conv[:, mm, CTX:TA], scalar=DH ** -0.5,
                                                 in1=c.wide[2 + n % 2][:, 0:T], op0=ALU.mult, op1=ALU.mult)
                        ends = slice(0, TAT)
                        dve.tensor_copy(g.decay[:, d, mm, :], c.wide[2 + n % 2][:, T:T + TAT]).then_inc(spread_copied, 1)

            @block.scalar
            def _(act):
                act.wait_ge(neg_ready, 1)
                act.activation(arg[:, :], arg[:, :], ACT.Exp).then_inc(exp_ready, 1)
                act.wait_ge(exp_ready, 1)
                act.activation(arg[:, :], arg[:, :], ACT.Ln, bias=1.0).then_inc(ln_ready, 1)
                act.wait_ge(pre_ready, 1)
                act.activation(g.inter[:, :], g.inter[:, :], ACT.Exp).then_inc(post_ready, 1)
                act.activation(g.rows[:, 1:3, :], g.rows[:, 1:3, :], ACT.Exp).then_inc(post_ready, 1)

            @block.tensor
            def _(pe):
                pe.wait_ge(post_ready, 2)
                pe.wait_ge(pre_ready, 1)
                for n in range(3 * TAT):
                    a, t = n // TAT, n % TAT
                    pe.matmul(c.bank[n // 9][:, n % 9 * GR:(n % 9 + 1) * GR], g.rows[:, a, t * P:(t + 1) * P],
                              c.ident[0:GR, 0:GR], start=True, stop=True).then_inc(turned, 1)
                for d in range(2):
                    for mm in range(MC):
                        n = d * MC + mm
                        if n >= 2:
                            pe.wait_ge(spread_copied, n - 1)
                        pe.matmul(c.wide[2 + n % 2][:, 0:T], u.pair[:, n, :], g.inter[:, CTX:TA], start=True, stop=True)
                        end = 0 if d else P - 1
                        pe.matmul(c.wide[2 + n % 2][:, T:T + TAT], u.pair[:, n, :], g.inter[:, end:TA:P],
                                  start=True, stop=True).then_inc(spread, 1)


def mlstm_stage(nc, c, u, g, hsum):
    with ExitStack() as ctx:
        def sb(n, shape):
            return ctx.enter_context(nc.sbuf_tensor(f"ml_{n}", shape, F32))
        ktm, kw, expo = g.ktm, g.kw, g.expo
        sc, hout = g.sc, g.hout
        state = sb("state", [P, 2, MC, DH + 1])
        small = sb("small", [P, 3, 2, 4])
        (k_turned, k_copied, kw_ready, gain_done, state_step, bm_spread, masked, exp_ready, qk_done, sc_ready, out_done,
         den_step, h_ready, h_added) = c.semaphores("ml", (
             "k_turned", "k_copied", "kw_ready", "gain_done", "state_step", "bm_spread", "masked", "exp_ready", "qk_done",
             "sc_ready", "out_done", "den_step", "h_ready", "h_added"))
        steps = [(d, p, ORDER[d][p]) for p in range(TAT) for d in range(2)]
        groups = [(n, d, t, q) for n, (d, p, t) in enumerate(steps) if t >= 2 for q in range(2)]
        first_of = {}
        for i, (n, *_ ) in enumerate(groups):
            first_of.setdefault(n, i)
        BM, QK, OUT, GAIN = c.bank[0:2], c.bank[2:4], c.bank[4:6], c.bank[6:8]
        with nc.Block() as block:
            @block.tensor
            def _(pe):
                for t in range(TAT):
                    if t >= 2:
                        pe.wait_ge(k_copied, t - 1)
                    for m in range(MC):
                        mm = pe.matmul(c.bank[t % 2][:, m * P:(m + 1) * P], u.conv[:, MC + m, t * P:(t + 1) * P], c.ident[:, :],
                                       start=True, stop=True)
                    mm.then_inc(k_turned, 1)
                pe.wait_ge(k_copied, TAT)
                for n, (d, p, t) in enumerate(steps):
                    if t >= 2:
                        for q in range(2):
                            i = first_of[n] + q
                            if i >= 2:
                                pe.wait_ge(masked, 4 * (i - 1))
                                pe.wait_ge(sc_ready, i - 1)
                            for e in range(4):
                                mm = pe.matmul(BM[i % 2][:, e * P:(e + 1) * P], c.ident[0:GR, SIDE[d] + 2 * e + q:SIDE[d] + 2 * e + q + 1].broadcast_to([GR, P]),
                                               g.bm[:, t * P:(t + 1) * P], start=True, stop=True)
                            mm.then_inc(bm_spread, 1)
                            for e in range(4):
                                head = 2 * e + q
                                rows = slice(head % 2 * DH, head % 2 * DH + DH)
                                mm = pe.matmul(QK[i % 2][:, e * P:(e + 1) * P], u.conv[rows, MC + head // 2, t * P:(t + 1) * P],
                                               u.conv[rows, head // 2, t * P:(t + 1) * P], start=True, stop=True)
                            mm.then_inc(qk_done, 1)
                        for q in range(2):
                            i = first_of[n] + q
                            pe.wait_ge(sc_ready, i + 1)
                            pe.wait_ge(state_step, 2 * n)
                            if i >= 2:
                                pe.wait_ge(h_ready, i - 1)
                            for e in range(4):
                                head = 2 * e + q
                                rows = slice(head % 2 * DH, head % 2 * DH + DH)
                                dst = OUT[i % 2][:, e * (DH + 1):(e + 1) * (DH + 1)]
                                pe.matmul(dst, sc[:, i % 2, e, :], u.v1[:, t, head, :], start=True, stop=False)
                                lt = (t - 2) * P
                                mm = pe.matmul(dst, g.qi[rows, d, head // 2, lt:lt + P], state[rows, d, head // 2, :],
                                               start=False, stop=True)
                            mm.then_inc(out_done, 1)
                    if p < TAT - 1:
                        pe.wait_ge(kw_ready, n + 1)
                        if n >= 2:
                            pe.wait_ge(state_step, 2 * n)
                        for head in range(NH):
                            rows = slice(head % 2 * DH, head % 2 * DH + DH)
                            m = head // 2
                            mm = pe.matmul(GAIN[n % 2][rows, m * (DH + 1):(m + 1) * (DH + 1)], kw[:, n % 2, head * DH:(head + 1) * DH],
                                           u.v1[:, t, head, :], start=True, stop=True)
                        mm.then_inc(gain_done, 1)

            @block.scalar
            def _(act):
                for t in range(TAT):
                    act.wait_ge(k_turned, t + 1)
                    act.copy(ktm[:, t, :], c.bank[t % 2][:, :]).then_inc(k_copied, 1)
                for i, (n, d, t, q) in enumerate(groups):
                    act.wait_ge(masked, 4 * (i + 1))
                    act.activation(expo[:, i % 2, :, :], expo[:, i % 2, :, :], ACT.Exp).then_inc(exp_ready, 1)

            @block.vector
            def _(dve):
                dve.memset(state[:, :, :, :], 0.0).then_inc(state_step, 1)
                dve.memset(hsum[:, :, :], 0.0).then_inc(state_step, 1)
                dve.wait_ge(state_step, 2)

                for n, (d, p, t) in enumerate(steps):
                    if p < TAT - 1:
                        dve.wait_ge(k_copied, TAT)
                        if n >= 2:
                            dve.wait_ge(gain_done, n - 1)
                        wts = g.cols[:, TAT + t, SIDE[d]:SIDE[d] + 8]
                        dve.tensor_tensor(kw[:, n % 2, :].rearrange("p (h e) -> p h e", e=DH),
                                          ktm[:, t, :].rearrange("p (h e) -> p h e", e=DH),
                                          wts.unsqueeze(2).broadcast_to([P, NH, DH]), ALU.mult).then_inc(kw_ready, 1)
                    if t >= 2:
                        for q in range(2):
                            i = first_of[n] + q
                            if i >= 2:
                                dve.wait_ge(sc_ready, i - 1)
                            dve.wait_ge(bm_spread, i + 1)
                            for e in range(4):
                                row = SIDE[d] + 2 * e + q
                                dve.scalar_tensor_tensor(out=expo[:, i % 2, e, :], in0=BM[i % 2][:, e * P:(e + 1) * P],
                                                         scalar=g.cols[:, t, row:row + 1], in1=u.never[:, d, :], op0=ALU.add,
                                                         op1=ALU.add).then_inc(masked, 1)
                        for q in range(2):
                            i = first_of[n] + q
                            dve.wait_ge(exp_ready, i + 1)
                            dve.wait_ge(qk_done, i + 1)
                            if i >= 2:
                                dve.wait_ge(out_done, i - 1)
                            dve.scalar_tensor_tensor(out=sc[:, i % 2, :, :].rearrange("p e t -> p (e t)"),
                                                     in0=QK[i % 2], scalar=DH ** -0.5,
                                                     in1=expo[:, i % 2, :, :].rearrange("p e t -> p (e t)"),
                                                     op0=ALU.mult, op1=ALU.mult).then_inc(sc_ready, 1)
                        for q in range(2):
                            i = first_of[n] + q
                            o = OUT[i % 2][:, 0:4 * (DH + 1)].rearrange("p (h e) -> p h e", e=DH + 1)
                            rows = slice(SIDE[d] + q, SIDE[d] + NH, 2)
                            dve.wait_ge(out_done, i + 1)
                            dve.tensor_tensor(small[:, 0, i % 2, :], o[:, :, DH], g.cols[:, 2 * TAT + t, rows], ALU.max).then_inc(den_step, 1)
                            dve.wait_ge(den_step, 3 * i + 1)
                            dve.scalar_tensor_tensor(out=small[:, 1, i % 2, :], in0=o[:, :, DH], scalar=-1.0,
                                                     in1=small[:, 0, i % 2, :], op0=ALU.mult, op1=ALU.max).then_inc(den_step, 1)
                            dve.wait_ge(den_step, 3 * i + 2)
                            dve.reciprocal(small[:, 2, i % 2, :], small[:, 1, i % 2, :]).then_inc(den_step, 1)
                            dve.wait_ge(den_step, 3 * i + 3)
                            dve.tensor_tensor(hout[:, i % 2, :, :], o[:, :, 0:DH],
                                              small[:, 2, i % 2, :].unsqueeze(2).broadcast_to([P, 4, DH]),
                                              ALU.mult).then_inc(h_ready, 1)
                            dve.wait_ge(h_ready, i + 1)
                            hs = hsum[:, t - 2, :].rearrange("p (m a e) -> p a m e", a=2, e=DH)[:, q, :, :]
                            dve.tensor_tensor(hs, hs, hout[:, i % 2, :, :], ALU.add).then_inc(h_added, 1)
                            dve.wait_ge(h_added, i + 1)
                    if p < TAT - 1:
                        dve.wait_ge(gain_done, n + 1)
                        dve.tensor_tensor(state[:, d, :, :], state[:, d, :, :],
                                          g.decay[:, d, :, t:t + 1].broadcast_to([P, MC, DH + 1]), ALU.mult).then_inc(state_step, 1)
                        dve.wait_ge(state_step, 2 * n + 3)
                        dve.tensor_tensor(state[:, d, :, :], state[:, d, :, :],
                                          GAIN[n % 2][:, 0:MC * (DH + 1)].rearrange("p (m e) -> p m e", e=DH + 1),
                                          ALU.add).then_inc(state_step, 1)



LEVELS = 7


def rwkv_common_stage(nc, c, u, r, lowrank):
    with ExitStack() as ctx:
        def sb(n, shape):
            return ctx.enter_context(nc.sbuf_tensor(f"rc_{n}", shape, F32))
        grown, kap, sq, t1, rk = sb("grown", [P, TA]), sb("kap", [P, TA]), sb("sq", [P, TA]), sb("t1", [P, TA]), sb("rk", [P, 3, T])
        one_ka = sb("one_ka", [P, MC])
        (dve_step, a_done, a_ready, kap_ready, sq_ready, sum_done, safe_ready, root_ready, g_done, g_ready, bonus_ready,
         bonus_done, turned, v_copied, m_done) = c.semaphores("rc", (
             "dve_step", "a_done", "a_ready", "kap_ready", "sq_ready", "sum_done", "safe_ready", "root_ready", "g_done",
             "g_ready", "bonus_ready", "bonus_done", "turned", "v_copied", "m_done"))
        col = lambda name, m: c.cols[:, COLS[name] + m:COLS[name] + m + 1]
        with nc.Block() as block:
            @block.tensor
            def _(pe):
                for m in range(MC):
                    ms = slice(m * P, (m + 1) * P)
                    if m >= 1:
                        pe.wait_ge(m_done, m)
                        pe.wait_ge(a_ready, m)
                        pe.wait_ge(g_ready, m)
                    pe.matmul(c.wide[0][:, 0:T], lowrank[0:64, 1, ms], u.la[:, CTX:TA], start=True, stop=True)
                    pe.matmul(c.wide[0][:, T:TA], lowrank[0:64, 1, ms], u.la[:, 0:CTX], start=True, stop=True).then_inc(a_done, 1)
                    pe.matmul(c.bank[4][:, :], lowrank[:, 2, ms], u.lg[:, :], start=True, stop=True).then_inc(g_done, 1)
                    pe.wait_ge(sq_ready, m + 1)
                    pe.matmul(c.wide[1][:, 0:T], c.same[:, :], sq[:, CTX:TA], start=True, stop=True)
                    pe.matmul(c.wide[1][:, T:TA], c.same[:, :], sq[:, 0:CTX], start=True, stop=True).then_inc(sum_done, 1)
                    pe.wait_ge(bonus_ready, m + 1)
                    pe.matmul(c.bank[5][:, :], c.same[:, :], rk[:, 2, :], start=True, stop=True).then_inc(bonus_done, 1)
                for t in range(TAT):
                    if t >= 2:
                        pe.wait_ge(v_copied, t - 1)
                    for m in range(MC):
                        mm = pe.matmul(c.bank[6 + t % 2][:, m * P:(m + 1) * P], u.conv[:, 4 * MC + m, t * P:(t + 1) * P],
                                       c.ident[:, :], start=True, stop=True)
                    mm.then_inc(turned, 1)

            @block.scalar
            def _(act):
                for m in range(MC):
                    act.wait_ge(a_done, m + 1)
                    if m >= 1:
                        act.wait_ge(m_done, m)
                    act.activation(r.a[:, m, CTX:TA], c.wide[0][:, 0:T], ACT.Sigmoid, bias=col("r_a0", m))
                    act.activation(r.a[:, m, 0:CTX], c.wide[0][:, T:TA], ACT.Sigmoid, bias=col("r_a0", m)).then_inc(a_ready, 1)
                    act.wait_ge(g_done, m + 1)
                    act.copy(r.g[:, m, :], c.bank[4][:, :]).then_inc(g_ready, 1)
                    act.wait_ge(kap_ready, m + 1)
                    act.activation(sq[:, :], kap[:, :], ACT.Square).then_inc(sq_ready, 1)
                    act.wait_ge(safe_ready, m + 1)
                    act.activation(t1[:, :], t1[:, :], ACT.Sqrt).then_inc(root_ready, 1)
                for t in range(TAT):
                    act.wait_ge(turned, t + 1)
                    act.copy(r.vtm[:, t, :], c.bank[6 + t % 2][:, :]).then_inc(v_copied, 1)

            @block.vector
            def _(dve):
                step = chain_of(dve, dve_step)
                step(dve.tensor_scalar(one_ka[:, :], c.cols[:, COLS["r_ka"]:COLS["r_ka"] + MC], -1.0, 1.0, ALU.mult, ALU.add))
                for m in range(MC):
                    rr, rkk, rv = u.conv[:, 2 * MC + m, :], u.conv[:, 3 * MC + m, :], u.conv[:, 4 * MC + m, :]
                    dve.tensor_scalar(kap[:, :], rkk, col("r_kk", m), None, ALU.mult).then_inc(kap_ready, 1)
                    dve.wait_ge(a_ready, m + 1)
                    step(dve.tensor_scalar(grown[:, :], r.a[:, m, :], col("r_ka", m), one_ka[:, m:m + 1], ALU.mult, ALU.add))
                    step(dve.tensor_tensor(r.kmod[:, m, :], grown[:, :], rkk, ALU.mult))
                    step(dve.tensor_tensor(rk[:, 0, :], rr[:, CTX:TA], r.kmod[:, m, CTX:TA], ALU.mult))
                    dve.tensor_scalar(rk[:, 2, :], rk[:, 0, :], col("r_bonus", m), None, ALU.mult).then_inc(bonus_ready, 1)
                    dve.wait_ge(sum_done, m + 1)
                    step(dve.tensor_scalar(t1[:, CTX:TA], c.wide[1][:, 0:T], 1e-24, None, ALU.max))
                    dve.tensor_scalar(t1[:, 0:CTX], c.wide[1][:, T:TA], 1e-24, None, ALU.max).then_inc(safe_ready, 1)
                    dve.wait_ge(root_ready, m + 1)
                    step(dve.reciprocal(t1[:, :], t1[:, :]))
                    step(dve.tensor_tensor(r.kh[:, m, :], kap[:, :], t1[:, :], ALU.mult))
                    step(dve.scalar_tensor_tensor(out=r.a[:, m, :], in0=r.a[:, m, :], scalar=-1.0, in1=r.kh[:, m, :],
                                                  op0=ALU.mult, op1=ALU.mult))
                    dve.wait_ge(bonus_done, m + 1)
                    dve.tensor_tensor(r.bonus[:, m, :], c.bank[5][:, :], rv[:, CTX:TA], ALU.mult).then_inc(m_done, 1)


def rwkv_factors_stage(nc, c, u, r, f, lowrank, d):
    mid = 64 if d else 63
    end = 0 if d else P - 1
    with ExitStack() as ctx:
        def sb(n, shape):
            return ctx.enter_context(nc.sbuf_tensor(f"rf{d}_{n}", shape, F32))
        sg, cum = r.room, sb("cum", [P, 2, TA])
        e = u.conv[:, 4 * MC:4 * MC + 3, :]
        out = sb("out", [P, 2, TAT, 4, P])
        reset = u.conv[:, 4 * MC + 3, :]
        mids, last = sb("mids", [P, MC, TAT]), sb("last", [P, MC, TAT])
        dve_step, z_done, sg_ready, s_ready, exp_ready, m_done, edge_ready, gain_ready, stored = c.semaphores(f"rf{d}", (
            "dve_step", "z_done", "sg_ready", "s_ready", "exp_ready", "m_done", "edge_ready", "gain_ready", "stored"))
        rows = slice(64 * d, 64 * d + 64)

        def tiles(x):
            return x.rearrange("p (j t) -> p j t", t=P)
        with nc.Block() as block:
            @block.sync
            def _(sp):
                for m in range(MC):
                    sp.wait_ge(m_done, m + 1)
                    sp.dma_start(f.scratch[d, :, :, m].rearrange("t p a x -> p t a x"), out[:, m % 2, :, :, :]).then_inc(stored, 16)
                    sp.wait_ge(stored, 16 * (m + 1))

            @block.tensor
            def _(pe):
                for m in range(MC):
                    if m >= 2:
                        pe.wait_ge(sg_ready, m - 1)
                    z = c.wide[m % 2]
                    pe.matmul(z[:, 0:T], lowrank[rows, 0, m * P:(m + 1) * P], u.lw[rows, CTX:TA], start=True, stop=True)
                    pe.matmul(z[:, T:TA], lowrank[rows, 0, m * P:(m + 1) * P], u.lw[rows, 0:CTX], start=True, stop=True).then_inc(z_done, 1)

            @block.scalar
            def _(act):
                def sigmoid(m):
                    b = c.cols[:, COLS["r_w0"] + d * MC + m:COLS["r_w0"] + d * MC + m + 1]
                    act.wait_ge(z_done, m + 1)
                    if m >= 2:
                        act.wait_ge(m_done, m - 1)
                    act.activation(sg[:, m % 2, CTX:TA], c.wide[m % 2][:, 0:T], ACT.Sigmoid, bias=b)
                    act.activation(sg[:, m % 2, 0:CTX], c.wide[m % 2][:, T:TA], ACT.Sigmoid, bias=b).then_inc(sg_ready, 1)

                sigmoid(0)
                sigmoid(1)
                for m in range(MC):
                    act.wait_ge(s_ready, m + 1)
                    if m >= 1:
                        act.wait_ge(m_done, m)
                    act.activation(e[:, 0, :], sg[:, m % 2, :], ACT.Exp, scale=DECAY)
                    act.activation(e[:, 1, :], cum[:, m % 2, :], ACT.Exp, scale=-DECAY)
                    act.activation(e[:, 2, :], cum[:, m % 2, :], ACT.Exp, scale=DECAY).then_inc(exp_ready, 1)
                    if m + 2 < MC:
                        act.wait_ge(m_done, m + 1)
                        sigmoid(m + 2)
                act.wait_ge(edge_ready, 1)
                act.activation(f.gain[:, d, :, :], f.gain[:, d, :, :], ACT.Exp, scale=-DECAY).then_inc(gain_ready, 1)

            @block.vector
            def _(dve):
                step = chain_of(dve, dve_step)
                step(dve.memset(reset[:, :], 1.0))
                first = P - 1 if d else 0
                step(dve.memset(reset[:, first:TA:P], 0.0))
                for m in range(MC):
                    s_, q = sg[:, m % 2, :], cum[:, m % 2, :]
                    dve.wait_ge(sg_ready, m + 1)
                    if d == 0:
                        step(dve.tensor_tensor_scan(q, reset[:, :], s_, 0.0, ALU.mult, ALU.add))
                    else:
                        step(dve.tensor_tensor_scan(q[:, ::-1], reset[:, ::-1], s_[:, ::-1], 0.0, ALU.mult, ALU.add))
                    step(dve.tensor_copy(mids[:, m, :], q[:, mid:TA:P]))
                    step(dve.tensor_copy(last[:, m, :], q[:, end:TA:P]))
                    dve.tensor_tensor(tiles(q), tiles(q), mids[:, m, :].unsqueeze(2).broadcast_to([P, TAT, P]), ALU.subtract).then_inc(s_ready, 1)
                    dve.wait_ge(exp_ready, m + 1)
                    step(dve.tensor_tensor(e[:, 0, :], e[:, 0, :], e[:, 1, :], ALU.mult))
                    if m >= 2:
                        dve.wait_ge(stored, 16 * (m - 1))
                    dve.tensor_tensor(out[:, m % 2, :, 0, :], tiles(r.kh[:, m, :]), tiles(e[:, 0, :]), ALU.mult)
                    dve.tensor_tensor(out[:, m % 2, :, 1, :], tiles(u.conv[:, 2 * MC + m, :]), tiles(e[:, 1, :]), ALU.mult)
                    dve.tensor_tensor(out[:, m % 2, :, 2, :], tiles(r.a[:, m, :]), tiles(e[:, 2, :]), ALU.mult)
                    dve.tensor_tensor(out[:, m % 2, :, 3, :], tiles(r.kmod[:, m, :]), tiles(e[:, 2, :]), ALU.mult).then_inc(m_done, 1)
                step(dve.tensor_tensor(f.gain[:, d, :, :], last[:, :, :], mids[:, :, :], ALU.subtract))
                for now, then in zip(ORDER[d], ORDER[d][1:]):
                    step(dve.tensor_tensor(f.gain[:, d, :, now:now + 1], f.gain[:, d, :, now:now + 1], mids[:, :, then:then + 1], ALU.add))
                dve.tensor_copy(last[:, 0, 0:1], mids[:, 0, 0:1]).then_inc(edge_ready, 1)


def rwkv_stage(nc, c, r, f, masks, ysum, d):
    with ExitStack() as ctx:
        def sb(n, shape, dt=F32):
            return ctx.enter_context(nc.sbuf_tensor(f"rw{d}_{n}", shape, dt))
        G = sb("G", [P, 2, NH, 4 * P])
        X = sb("X", [P, NH, P])
        XT = sb("XT", [P, 2, NH, P])
        Q = sb("Q", [P, NH, P])
        tm = sb("tm", [P, 2, 2, DM])
        F = sb("F", [P, 2, MC, 4, P])
        base = sb("base", [P, NH, DH])
        U = sb("U", [P, NH, DH])
        S = sb("S", [P, MC, DH])
        S2 = sb("S2", [P, MC, DH])
        (pair_done, pair_masked, au_done, x0_ready, tm_done, tm_copied, q_done, q_ready, x_done, xt_done, x_ready, base_done, base_ready,
         u_done, u_ready, y_done, y_added, gain_done, state_step, x_step, loaded0, loaded1) = c.semaphores(f"rw{d}", (
             "pair_done", "pair_masked", "au_done", "x0_ready", "tm_done", "tm_copied", "q_done", "q_ready", "x_done", "xt_done",
             "x_ready", "base_done", "base_ready", "u_done", "u_ready", "y_done", "y_added", "gain_done", "state_step", "x_step", "loaded0", "loaded1"))
        order = ORDER[d]
        loaded = (loaded0, loaded1)
        QB, XB, XTB = [c.bank[0], c.bank[3]], [c.bank[1], c.bank[4]], [c.bank[2], c.bank[5]]
        side = [c.bank[6], c.bank[7]]
        pair_mask, first_u, first_t = masks.pair[:, d, :], masks.first[:, d, :], masks.first[:, 1 - d, :]
        level, level_t = masks.level[:, d, :, :], masks.level[:, 1 - d, :, :]

        def heads(g):
            return range(g, NH, 2)

        def place(h):
            return h % 2 * 4 + h // 2

        def rows_of(head):
            return slice(head % 2 * DH, head % 2 * DH + DH)

        with nc.Block() as block:
            @block.sync
            def _(sp):
                for p, t in enumerate(order):
                    if p >= 2:
                        sp.wait_ge(state_step, 3 * (p - 2) + 4)
                    sp.dma_start(F[:, p % 2, :, :, :], f.scratch[d, t]).then_inc(loaded[p % 2], 16)

            @block.tensor
            def _(pe):
                def pairs(p):
                    t = order[p]
                    pe.wait_ge(loaded[p % 2], 16 * (p // 2 + 1))
                    for h in range(NH):
                        rows, m = rows_of(h), h // 2
                        if p * NH + h >= 2:
                            pe.wait_ge(pair_masked, p * NH + h - 1)
                        if p >= 2 and h < 2:
                            pe.wait_ge(state_step, 3 * (p - 2) + 4)
                            pe.wait_ge(y_added, 2 * (p - 3)) if p > 3 else None
                        dst = side[h % 2]
                        ar, b, k = F[rows, p % 2, m, 0:2, :].rearrange("p a t -> p (a t)"), F[rows, p % 2, m, 2, :], F[rows, p % 2, m, 3, :]
                        pe.matmul(dst[:, 0:2 * P], b, ar, start=True, stop=True)
                        pe.matmul(dst[:, 2 * P:4 * P], k, ar, start=True, stop=True).then_inc(pair_done, 1)
                    for g in range(2):
                        if p >= 1:
                            pe.wait_ge(x_ready, 2 * (LEVELS - 1) * p)
                        for e, h in enumerate(heads(g)):
                            rows, m = rows_of(h), h // 2
                            mm = pe.matmul(QB[g][:, e * P:(e + 1) * P], F[rows, p % 2, m, 0, :], F[rows, p % 2, m, 2, :], start=True, stop=True)
                        mm.then_inc(au_done, 1)
                    for a in range(2):
                        pe.wait_ge(pair_masked, (p + 1) * NH - 1 + a)
                        for m in range(MC):
                            mm = pe.matmul(side[a][:, m * P:(m + 1) * P], F[:, p % 2, m, 2 + a, :], c.ident[:, :], start=True, stop=True)
                        mm.then_inc(tm_done, 1)

                def level_step(p, k):
                    for g in range(2):
                        n = 2 * (LEVELS - 1) * p + 2 * (k - 1) + g
                        if k == 1:
                            pe.wait_ge(x0_ready, 2 * p + g + 1)
                        else:
                            pe.wait_ge(x_ready, n - 1)
                        for e, h in enumerate(heads(g)):
                            mm = pe.matmul(QB[g][:, e * P:(e + 1) * P], G[:, p % 2, place(h), 0:P], X[:, place(h), :], start=True, stop=True)
                        mm.then_inc(q_done, 1)
                    for g in range(2):
                        n = 2 * (LEVELS - 1) * p + 2 * (k - 1) + g
                        pe.wait_ge(q_ready, n + 1)
                        for e, h in enumerate(heads(g)):
                            mm = pe.matmul(XTB[g][:, e * P:(e + 1) * P], Q[:, place(h), :], XT[:, p % 2, place(h), :], start=True, stop=True)
                        mm.then_inc(xt_done, 1)
                        if k < LEVELS - 1:
                            for e, h in enumerate(heads(g)):
                                mm = pe.matmul(XB[g][:, e * P:(e + 1) * P], XT[:, p % 2, place(h), :], Q[:, place(h), :], start=True, stop=True)
                            mm.then_inc(x_done, 1)

                def chain(p, part):
                    t = order[p]
                    if part == 0:
                        pe.wait_ge(tm_copied, 2 * min(p + 2, TAT))
                        pe.wait_ge(state_step, 3 * p + 1)
                        for h in range(NH):
                            rows, m = rows_of(h), h // 2
                            dst = side[h % 2][:, m * DH:(m + 1) * DH]
                            pe.matmul(dst, F[rows, p % 2, m, 0, :], S[rows, m, :], start=True, stop=False)
                            mm = pe.matmul(dst, G[:, p % 2, place(h), 2 * P:3 * P], r.vtm[:, t, h * DH:(h + 1) * DH], start=False, stop=True)
                        mm.then_inc(base_done, 1)
                    elif part == 1:
                        pe.wait_ge(base_ready, 2 * p + 2)
                        pe.wait_ge(x_ready, 2 * (LEVELS - 1) * (p + 1))
                        for h in range(NH):
                            mm = pe.matmul(side[h % 2][:, h // 2 * DH:(h // 2 + 1) * DH], XT[:, p % 2, place(h), :], base[:, place(h), :], start=True, stop=True)
                        mm.then_inc(u_done, 1)
                    else:
                        pe.wait_ge(u_ready, 2 * p + 2)
                        if t >= 2:
                            for h in range(NH):
                                rows, m, hs = rows_of(h), h // 2, slice(h * DH, (h + 1) * DH)
                                dst = side[h % 2][:, m * DH:(m + 1) * DH]
                                pe.matmul(dst, F[rows, p % 2, m, 1, :], S[rows, m, :], start=True, stop=False)
                                pe.matmul(dst, G[:, p % 2, place(h), P:2 * P], U[:, place(h), :], start=False, stop=False)
                                mm = pe.matmul(dst, G[:, p % 2, place(h), 3 * P:4 * P], r.vtm[:, t, hs], start=False, stop=True)
                            mm.then_inc(y_done, 1)
                        if p < TAT - 1:
                            for h in range(NH):
                                rows, m, hs = rows_of(h), h // 2, slice(h * DH, (h + 1) * DH)
                                dst = side[h % 2][rows, (MC + m) * DH:(MC + m + 1) * DH]
                                pe.matmul(dst, tm[:, p % 2, 0, hs], U[:, place(h), :], start=True, stop=False)
                                mm = pe.matmul(dst, tm[:, p % 2, 1, hs], r.vtm[:, t, hs], start=False, stop=True)
                            mm.then_inc(gain_done, 1)

                for p in range(TAT + 1):
                    if p < TAT:
                        pairs(p)
                        for k in range(1, LEVELS):
                            level_step(p, k)
                            if p >= 1 and k <= 3:
                                chain(p - 1, k - 1)
                    else:
                        for part in range(3):
                            chain(p - 1, part)

            @block.vector
            def _(dve):
                dve.memset(S[:, :, :], 0.0).then_inc(state_step, 1)
                def start(p):
                    for h in range(NH):
                        dve.wait_ge(pair_done, p * NH + h + 1)
                        if p >= 2:
                            dve.wait_ge(state_step, 3 * (p - 2) + 4)
                        dve.tensor_tensor(G[:, p % 2, place(h), :].rearrange("p (a t) -> p a t", a=2), side[h % 2].rearrange("p (a t) -> p a t", a=2),
                                          pair_mask.unsqueeze(1).broadcast_to([P, 2, 2 * P]), ALU.mult).then_inc(pair_masked, 1)
                    for g in range(2):
                        hs = slice(4 * g, 4 * g + 4)
                        dve.wait_ge(au_done, 2 * p + g + 1)
                        dve.wait_ge(pair_masked, p * NH + NH)
                        dve.tensor_tensor(X[:, hs, :], QB[g].rearrange("p (h t) -> p h t", h=4),
                                          first_u.unsqueeze(1).broadcast_to([P, 4, P]), ALU.mult).then_inc(x_step, 1)
                        dve.tensor_tensor(XT[:, p % 2, hs, :], G[:, p % 2, hs, 0:P],
                                          first_t.unsqueeze(1).broadcast_to([P, 4, P]), ALU.mult).then_inc(x_step, 1)
                        dve.wait_ge(x_step, 4 * p + 2 * g + 2)
                        dve.tensor_tensor(X[:, hs, :], X[:, hs, :], c.ident[:, :].unsqueeze(1).broadcast_to([P, 4, P]), ALU.add)
                        dve.tensor_tensor(XT[:, p % 2, hs, :], XT[:, p % 2, hs, :], c.ident[:, :].unsqueeze(1).broadcast_to([P, 4, P]),
                                          ALU.add).then_inc(x0_ready, 1)

                def grow(p, k):
                    for g in range(2):
                        hs = slice(4 * g, 4 * g + 4)
                        n = 2 * (LEVELS - 1) * p + 2 * (k - 1) + g
                        dve.wait_ge(xt_done, n + 1)
                        if k < LEVELS - 1:
                            dve.wait_ge(x_done, 2 * (LEVELS - 2) * p + 2 * (k - 1) + g + 1)
                            dve.copy_predicated(X[:, hs, :], level[:, k, :].unsqueeze(1).broadcast_to([P, 4, P]),
                                                XB[g].rearrange("p (h t) -> p h t", h=4))
                        dve.copy_predicated(XT[:, p % 2, hs, :], level_t[:, k, :].unsqueeze(1).broadcast_to([P, 4, P]),
                                            XTB[g].rearrange("p (h t) -> p h t", h=4)).then_inc(x_ready, 1)

                def finish(p):
                    t = order[p]
                    if t >= 2:
                        dve.wait_ge(y_done, sum(q >= 2 for q in order[:p + 1]))
                        if p < TAT - 1:
                            dve.wait_ge(gain_done, p + 1)
                        for g in range(2):
                            y = ysum[:, t - 2, :].rearrange("p (m a e) -> p a m e", a=2, e=DH)[:, g, :, :]
                            part = side[g][:, 0:MC * DH].rearrange("p (m e) -> p m e", e=DH)
                            if d == 0:
                                dve.tensor_copy(y, part).then_inc(y_added, 1)
                            else:
                                dve.tensor_tensor(y, y, part, ALU.add).then_inc(y_added, 1)
                    if p < TAT - 1:
                        dve.wait_ge(gain_done, p + 1)
                        for g in range(2):
                            half = slice(g * DH, (g + 1) * DH)
                            dve.tensor_tensor(S2[half, :, :], S[half, :, :], side[g][half, MC * DH:2 * MC * DH].rearrange("p (m e) -> p m e", e=DH),
                                              ALU.add).then_inc(state_step, 1)
                        dve.wait_ge(state_step, 3 * p + 3)
                        dve.tensor_tensor(S[:, :, :], S2[:, :, :], f.gain[:, d, :, t:t + 1].broadcast_to([P, MC, DH]), ALU.mult).then_inc(state_step, 1)

                for p in range(TAT + 1):
                    if p < TAT:
                        start(p)
                        for k in range(1, LEVELS):
                            grow(p, k)
                            if p >= 1 and k == 3:
                                finish(p - 1)
                    else:
                        finish(p - 1)

            @block.scalar
            def _(act):
                def mover(p, k):
                    for g in range(2):
                        hs = slice(4 * g, 4 * g + 4)
                        n = 2 * (LEVELS - 1) * p + 2 * (k - 1) + g
                        act.wait_ge(q_done, n + 1)
                        if n >= 2:
                            act.wait_ge(x_ready, n - 1)
                        act.copy(Q[:, hs, :], QB[g].rearrange("p (h t) -> p h t", h=4)).then_inc(q_ready, 1)

                def carry(p, part):
                    if part == 0:
                        act.wait_ge(base_done, p + 1)
                        for g in range(2):
                            act.copy(base[:, 4 * g:4 * g + 4, :], side[g][:, 0:MC * DH].rearrange("p (m e) -> p m e", e=DH)).then_inc(base_ready, 1)
                    elif part == 1:
                        act.wait_ge(u_done, p + 1)
                        for g in range(2):
                            act.copy(U[:, 4 * g:4 * g + 4, :], side[g][:, 0:MC * DH].rearrange("p (m e) -> p m e", e=DH)).then_inc(u_ready, 1)

                for p in range(TAT + 1):
                    if p < TAT:
                        for a in range(2):
                            act.wait_ge(tm_done, 2 * p + a + 1)
                            if p >= 2:
                                act.wait_ge(state_step, 3 * (p - 2) + 4)
                            act.copy(tm[:, p % 2, a, :], side[a]).then_inc(tm_copied, 1)
                        for k in range(1, LEVELS):
                            mover(p, k)
                            if p >= 1 and k <= 3:
                                carry(p - 1, k - 1)
                    else:
                        for part in range(3):
                            carry(p - 1, part)



def head_norm_stage(nc, c, hsum, ysum, mo, g, bonus, mixed):
    with ExitStack() as ctx:
        def sb(n, shape):
            return ctx.enter_context(nc.sbuf_tensor(f"hn_{n}", shape, F32))
        sq = sb("sq", [P, DM])
        st = sb("st", [P, 8, 4, NH])
        tmp = sb("tmp", [P, 2, T])
        dve_step, var_ready, root_ready, normed, turned, scaled, mixed_ready = c.semaphores("hn", (
            "dve_step", "var_ready", "root_ready", "normed", "turned", "scaled", "mixed_ready"))
        pieces = [(hsum, t, LN_EPS) for t in range(TT)] + [(ysum, t, GN_EPS) for t in range(TT)]

        def by_head(x):
            return x.rearrange("p (h e) -> p h e", e=DH)
        with nc.Block() as block:
            @block.vector
            def _(dve):
                step = chain_of(dve, dve_step)
                for n, (src, t, eps) in enumerate(pieces):
                    x = by_head(src[:, t, :])
                    step(dve.tensor_reduce(st[:, n, 0, :], x, AX.X, ALU.add))
                    step(dve.tensor_scalar(st[:, n, 0, :], st[:, n, 0, :], 1.0 / DH, None, ALU.mult))
                    step(dve.tensor_tensor(x, x, st[:, n, 0, :].unsqueeze(2).broadcast_to([P, NH, DH]), ALU.subtract))
                    step(dve.tensor_tensor(sq[:, :], src[:, t, :], src[:, t, :], ALU.mult))
                    step(dve.tensor_reduce(st[:, n, 1, :], by_head(sq[:, :]), AX.X, ALU.add))
                    dve.tensor_scalar(st[:, n, 1, :], st[:, n, 1, :], 1.0 / DH, eps, ALU.mult, ALU.add).then_inc(var_ready, 1)
                for n, (src, t, eps) in enumerate(pieces):
                    x = by_head(src[:, t, :])
                    dve.wait_ge(root_ready, n + 1)
                    step(dve.reciprocal(st[:, n, 3, :], st[:, n, 2, :]))
                    dve.tensor_tensor(x, x, st[:, n, 3, :].unsqueeze(2).broadcast_to([P, NH, DH]), ALU.mult).then_inc(normed, 1)
                for k in range(2 * MC):
                    m = k % MC
                    dve.wait_ge(turned, k + 1)
                    if k < MC:
                        dve.scalar_tensor_tensor(out=mixed[:, k, :], in0=c.bank[k][:, :], scalar=c.cols[:, COLS["m_norm_w"] + m:COLS["m_norm_w"] + m + 1],
                                                 in1=mo[:, m, :], op0=ALU.mult, op1=ALU.mult).then_inc(mixed_ready, 1)
                    else:
                        step(dve.tensor_scalar(tmp[:, k % 2, :], c.bank[k][:, :], c.cols[:, COLS["r_norm_w"] + m:COLS["r_norm_w"] + m + 1],
                                               c.cols[:, COLS["r_norm_b"] + m:COLS["r_norm_b"] + m + 1], ALU.mult, ALU.add))
                        step(dve.tensor_tensor(tmp[:, k % 2, :], tmp[:, k % 2, :], bonus[:, m, :], ALU.add))
                        dve.tensor_tensor(mixed[:, k, :], tmp[:, k % 2, :], g[:, m, :], ALU.mult).then_inc(mixed_ready, 1)

            @block.scalar
            def _(act):
                for n in range(2 * TT):
                    act.wait_ge(var_ready, n + 1)
                    act.activation(st[:, n, 2, :], st[:, n, 1, :], ACT.Sqrt).then_inc(root_ready, 1)

            @block.tensor
            def _(pe):
                for k in range(2 * MC):
                    src, m = (hsum, k) if k < MC else (ysum, k - MC)
                    pe.wait_ge(normed, TT if k < MC else 2 * TT)
                    for t in range(TT):
                        mm = pe.matmul(c.bank[k][:, t * P:(t + 1) * P], src[:, t, m * P:(m + 1) * P], c.ident[:, :], start=True, stop=True)
                    mm.then_inc(turned, 1)


def residual_stage(nc, c, w, o, x, gate):
    chunk_done, grown, added = c.semaphores("res", ("chunk_done", "grown", "added"))
    with nc.Block() as block:
        @block.sync
        def _(sp):
            w.feed(sp, U_OUT2)

        @block.scalar
        def _(act):
            for m in range(DC):
                act.mul(x[:, m, :], x[:, m, :], ALPHA).then_inc(grown, 1)

        @block.tensor
        def _(pe):
            for m in range(DC):
                unit = w.arrived(pe, 0, m // 2) if m % 2 == 0 else unit
                for k in range(DC):
                    b = (m % 2 * DC + k) * P
                    mm = pe.matmul(c.bank[m][:, :], unit[:, b:b + P], o[:, k, :], start=(k == 0), stop=(k == DC - 1))
                mm.then_inc((chunk_done, w.used)[m % 2], 1)

        @block.vector
        def _(dve):
            for m in range(DC):
                if m % 2 == 0:
                    dve.wait_ge(chunk_done, m // 2 + 1)
                else:
                    dve.wait_ge(w.used, w.at + m // 2 + 1)
                dve.wait_ge(grown, m + 1)
                dve.scalar_tensor_tensor(out=x[:, m, :], in0=c.bank[m][:, :], scalar=gate(m), in1=x[:, m, :],
                                         op0=ALU.mult, op1=ALU.add).then_inc(added, 1)
    w.at += U_OUT2



def router_stage(nc, c, h, rt, rt_bias, iota, wt):
    NR = E_GROUPS + EXPERTS
    with ExitStack() as ctx:
        def sb(n, shape, dt=F32):
            return ctx.enter_context(nc.sbuf_tensor(f"rt_{n}", shape, dt))
        L = sb("L", [P, TT, NR])
        lg8, top, idx, idxf = sb("lg8", [P, TT, 8]), sb("top", [P, TT, 8]), sb("idx", [P, TT, 8], U32), sb("idxf", [P, TT, 8])
        eg, sums = sb("eg", [P, TT, E_GROUPS]), sb("sums", [P, TT, 8])
        oh, pick, own = sb("oh", [P, TT, E_GROUPS]), sb("pick", [P, TT, E_GROUPS, E_EACH]), sb("own", [P, TT, E_EACH])
        both = sb("both", [P, 2, TT, E_EACH])
        dve_step, logits_done, shifted, exp_ready, gap_ready, odds_ready = c.semaphores("rt", (
            "dve_step", "logits_done", "shifted", "exp_ready", "gap_ready", "odds_ready"))
        with nc.Block() as block:
            @block.tensor
            def _(pe):
                for t in range(TT):
                    dst = c.bank[t][:, 0:NR]
                    for k in range(DC):
                        pe.matmul(dst, h[:, k, t * P:(t + 1) * P], rt[:, k, :], start=(k == 0), stop=False)
                    mm = pe.matmul(dst, c.ones[0:1, :], rt_bias[0:1, :], start=False, stop=True)
                mm.then_inc(logits_done, 1)

            @block.vector
            def _(dve):
                step = chain_of(dve, dve_step)
                dve.wait_ge(logits_done, 1)
                for t in range(TT):
                    step(dve.tensor_copy(L[:, t, :], c.bank[t][:, 0:NR]))
                step(dve.memset(lg8[:, :, :], -3e38))
                step(dve.tensor_copy(lg8[:, :, 0:E_GROUPS], L[:, :, 0:E_GROUPS]))
                for t in range(TT):
                    step(dve.max(top[:, t, :], lg8[:, t, :]))
                    step(dve.max_index(idx[:, t, :], top[:, t, :], lg8[:, t, :]))
                step(dve.tensor_copy(idxf[:, :, :], idx[:, :, :]))
                dve.tensor_tensor(eg[:, :, :], L[:, :, 0:E_GROUPS], top[:, :, 0:1].broadcast_to([P, TT, E_GROUPS]), ALU.subtract).then_inc(shifted, 1)
                step(dve.tensor_tensor(oh[:, :, :], iota[:, 0:E_GROUPS].unsqueeze(1).broadcast_to([P, TT, E_GROUPS]),
                                       idxf[:, :, 0:1].broadcast_to([P, TT, E_GROUPS]), ALU.is_equal))
                dve.wait_ge(exp_ready, 1)
                step(dve.tensor_reduce(sums[:, :, 0], eg[:, :, :], AX.X, ALU.add))
                step(dve.reciprocal(sums[:, :, 1], sums[:, :, 0]))
                for t in range(TT):
                    step(dve.tensor_tensor(pick[:, t, :, :], L[:, t, E_GROUPS:NR].rearrange("p (g e) -> p g e", g=E_GROUPS),
                                           oh[:, t, :].unsqueeze(2).broadcast_to([P, E_GROUPS, E_EACH]), ALU.mult))
                    step(dve.tensor_reduce(own[:, t, :], pick[:, t, :, :].rearrange("p g e -> p e g"), AX.X, ALU.add))
                    step(dve.max(top[:, t, :], own[:, t, :]))
                    step(dve.max_index(idx[:, t, :], top[:, t, :], own[:, t, :]))
                step(dve.tensor_copy(idxf[:, :, :], idx[:, :, :]))
                dve.tensor_tensor(sums[:, :, 2], top[:, :, 1], top[:, :, 0], ALU.subtract).then_inc(gap_ready, 1)
                dve.wait_ge(odds_ready, 1)
                step(dve.tensor_scalar(sums[:, :, 4], sums[:, :, 3], 1.0, None, ALU.add))
                step(dve.reciprocal(sums[:, :, 5], sums[:, :, 4]))
                step(dve.tensor_tensor(sums[:, :, 6], sums[:, :, 5], sums[:, :, 1], ALU.mult))
                step(dve.tensor_tensor(sums[:, :, 7], sums[:, :, 6], sums[:, :, 3], ALU.mult))
                for n in range(2):
                    step(dve.tensor_tensor(both[:, n, :, :], iota[:, 0:E_EACH].unsqueeze(1).broadcast_to([P, TT, E_EACH]),
                                           idxf[:, :, n:n + 1].broadcast_to([P, TT, E_EACH]), ALU.is_equal))
                    step(dve.tensor_tensor(both[:, n, :, :], both[:, n, :, :], sums[:, :, 6 + n:7 + n].broadcast_to([P, TT, E_EACH]), ALU.mult))
                step(dve.tensor_tensor(own[:, :, :], both[:, 0, :, :], both[:, 1, :, :], ALU.add))
                for t in range(TT):
                    step(dve.tensor_tensor(wt[:, t, :].rearrange("p (g e) -> p g e", g=E_GROUPS),
                                           own[:, t, :].unsqueeze(1).broadcast_to([P, E_GROUPS, E_EACH]),
                                           oh[:, t, :].unsqueeze(2).broadcast_to([P, E_GROUPS, E_EACH]), ALU.mult))

            @block.scalar
            def _(act):
                act.wait_ge(shifted, 1)
                act.activation(eg[:, :, :], eg[:, :, :], ACT.Exp).then_inc(exp_ready, 1)
                act.wait_ge(gap_ready, 1)
                act.activation(sums[:, :, 3], sums[:, :, 2], ACT.Exp).then_inc(odds_ready, 1)


def experts_stage(nc, c, w, h, wt, y):
    with ExitStack() as ctx:
        def sb(n, shape):
            return ctx.enter_context(nc.sbuf_tensor(f"ex_{n}", shape, F32))
        wrow, wb = sb("wrow", [EXPERTS, T]), sb("wb", [P, 2, T])
        silu, hid = sb("silu", [P, 2, T]), sb("hid", [P, 2, EC, T])
        turned, wrow_ready, spread, wb_ready, gate_done, silu_ready, up_read, hid_ready, down_done, added = c.semaphores("ex", (
            "turned", "wrow_ready", "spread", "wb_ready", "gate_done", "silu_ready", "up_read", "hid_ready", "down_done", "added"))
        GU = [c.bank[0:2], c.bank[2:4]]
        DN = c.bank[4:6]
        with nc.Block() as block:
            @block.sync
            def _(sp):
                w.feed(sp, U_EXPERT * EXPERTS)

            @block.tensor
            def _(pe):
                for t in range(TT):
                    mm = pe.matmul(c.bank[6][0:EXPERTS, t * P:(t + 1) * P], wt[:, t, :], c.ident[:, :], start=True, stop=True)
                mm.then_inc(turned, 1)
                pe.wait_ge(wrow_ready, 1)
                for e in range(EXPERTS):
                    if e >= 1:
                        pe.wait_ge(wb_ready, e)
                    pe.matmul(c.bank[7][:, :], c.ident[0:EXPERTS, e:e + 1].broadcast_to([EXPERTS, P]), wrow[:, :], start=True, stop=True).then_inc(spread, 1)
                    for q in range(EC):
                        n = e * EC + q
                        unit = w.arrived(pe, 0, e * U_EXPERT + q)
                        if n >= 2:
                            pe.wait_ge(up_read, n - 1)
                        for half in range(2):
                            for k in range(DC):
                                b = (half * DC + k) * P
                                mm = pe.matmul(GU[n % 2][half][:, :], unit[:, b:b + P], h[:, k, :], start=(k == 0), stop=(k == DC - 1))
                            mm.then_inc((gate_done, w.used)[half], 1)
                    pe.wait_ge(hid_ready, EC * (e + 1))
                    for m in range(DC):
                        n = e * DC + m
                        if m % 4 == 0:
                            unit = w.arrived(pe, 0, e * U_EXPERT + EC + m // 4)
                        if n >= 2:
                            pe.wait_ge(added, n - 1)
                        for k in range(EC):
                            b = (m % 4 * EC + k) * P
                            mm = pe.matmul(DN[n % 2][:, :], unit[:, b:b + P], hid[:, e % 2, k, :], start=(k == 0), stop=(k == EC - 1))
                        mm.then_inc(w.used if m % 4 == 3 else down_done, 1)

            @block.scalar
            def _(act):
                for e in range(EXPERTS):
                    act.wait_ge(spread, e + 1)
                    if e >= 2:
                        act.wait_ge(hid_ready, EC * (e - 1))
                    act.copy(wb[:, e % 2, :], c.bank[7][:, :]).then_inc(wb_ready, 1)
                    for q in range(EC):
                        n = e * EC + q
                        act.wait_ge(gate_done, n + 1)
                        if n >= 2:
                            act.wait_ge(up_read, n - 1)
                        act.activation(silu[:, n % 2, :], GU[n % 2][0][:, :], ACT.Silu).then_inc(silu_ready, 1)

            @block.vector
            def _(dve):
                dve.wait_ge(turned, 1)
                dve.tensor_copy(wrow[:, :], c.bank[6][0:EXPERTS, :]).then_inc(wrow_ready, 1)
                for e in range(EXPERTS):
                    for q in range(EC):
                        n = e * EC + q
                        dve.wait_ge(silu_ready, n + 1)
                        dve.wait_ge(w.used, w.at + e * U_EXPERT + q + 1)
                        dve.tensor_tensor(hid[:, e % 2, q, :], silu[:, n % 2, :], GU[n % 2][1][:, :], ALU.mult).then_inc(up_read, 1)
                        dve.wait_ge(up_read, n + 1)
                        dve.wait_ge(wb_ready, e + 1)
                        dve.tensor_tensor(hid[:, e % 2, q, :], hid[:, e % 2, q, :], wb[:, e % 2, :], ALU.mult).then_inc(hid_ready, 1)
                    for m in range(DC):
                        n = e * DC + m
                        if m % 4 == 3:
                            dve.wait_ge(w.used, w.at + e * U_EXPERT + EC + m // 4 + 1)
                        else:
                            dve.wait_ge(down_done, e * 6 + m - m // 4 + 1)
                        if e == 0:
                            dve.tensor_copy(y[:, m, :], DN[n % 2][:, :]).then_inc(added, 1)
                        else:
                            dve.wait_ge(added, n - DC + 1)
                            dve.tensor_tensor(y[:, m, :], y[:, m, :], DN[n % 2][:, :], ALU.add).then_inc(added, 1)
    w.at += U_EXPERT * EXPERTS


def last_residual_stage(nc, c, x, y, gate):
    grown, added = c.semaphores("lres", ("grown", "added"))
    with nc.Block() as block:
        @block.scalar
        def _(act):
            for m in range(DC):
                act.mul(x[:, m, :], x[:, m, :], ALPHA).then_inc(grown, 1)

        @block.vector
        def _(dve):
            for m in range(DC):
                dve.wait_ge(grown, m + 1)
                dve.scalar_tensor_tensor(out=x[:, m, :], in0=y[:, m, :], scalar=gate(m), in1=x[:, m, :],
                                         op0=ALU.mult, op1=ALU.add).then_inc(added, 1)


def load_stage(nc, pairs, name):
    done = nc.alloc_semaphore(name)
    with nc.Block() as block:
        @block.sync
        def _(sp):
            for dst, src in pairs:
                sp.dma_start(dst, src).then_inc(done, 16)
            sp.wait_ge(done, 16 * len(pairs))


class Bag:
    pass


def second_block(nc, c, w, a, x, out, upto, dump):
    with ExitStack() as block_ctx:
        def sb(n, shape, dt=F32):
            return block_ctx.enter_context(nc.sbuf_tensor(n, shape, dt))
        mod, mod1 = sb("mod", [P, 6 * DC, 2]), sb("mod1", [P, 6 * DC, 2])
        c.same = sb("same", [P, P])

        def at(part, which=0, plus=False):
            return lambda k: (mod1 if plus else mod)[:, part * DC + k, which:which + 1]

        with ExitStack() as mixer_ctx:
            def sm(n, shape, dt=F32):
                return mixer_ctx.enter_context(nc.sbuf_tensor(n, shape, dt))
            late = sm("late", [P, 4 * TT * DM + TAT * DM])

            def view(first, count, wide):
                return late[:, first:first + count * wide].rearrange("p (k t) -> p k t", t=wide)
            hsum, ysum = view(0, TT, DM), view(2048, TT, DM)
            u, r, f, g = Bag(), Bag(), Bag(), Bag()
            u.mo, r.g, r.bonus, r.vtm = sm("mo", [P, MC, T]), view(4096, MC, T), view(6144, MC, T), view(8192, TAT, DM)
            f.gain = sm("state_gain", [P, 2, MC, TAT])
            f.scratch = nc.dram_tensor("factors", [2, TAT, P, MC, 4, P], F32, kind="Internal").ap()
            with ExitStack() as in_ctx:
                def si(n, shape, dt=F32):
                    return in_ctx.enter_context(nc.sbuf_tensor(n, shape, dt))
                u.conv = si("conv", [P, CONV_CHUNKS, TA])
                u.lw, u.la, u.lg = si("lw", [P, TA]), si("la", [64, TA]), si("lg", [P, T])
                u.bias = si("gate_bias", [64, 2])
                with ExitStack() as m_ctx:
                    def smm(n, shape, dt=F32):
                        return m_ctx.enter_context(nc.sbuf_tensor(n, shape, dt))
                    u.v1 = smm("v1", [P, TAT, NH, DH + 1])
                    raw = smm("gate_raw", [P, 2 * TA])
                    u.li, u.lf = raw[0:64, 0:TA], raw[0:64, TA:2 * TA]
                    with ExitStack() as p_ctx:
                        def sp_(n, shape, dt=F32):
                            return p_ctx.enter_context(nc.sbuf_tensor(n, shape, dt))
                        cond, ada_b = sp_("cond", [P, DC, 2]), sp_("ada_b", [P, 6 * DC])
                        load_stage(nc, [(cond[:, :, :], a["cond"]), (ada_b[:, :], a["ada_b"]), (u.bias[:, :], a["gate_bias"]),
                                        (c.same[:, :], a["same"])], "consts_ada")
                        ada_stage(nc, c, w, cond, mod, mod1, ada_b[:, :])
                        h = view(0, DC, TA)
                        room = u.conv[:, :, :].rearrange("p m t -> p (m t)")
                        ctx_in = room[:, 12288:12288 + DC * CTX].rearrange("p (k t) -> p k t", t=CTX)
                        load_stage(nc, [(ctx_in[:, :, :], a["ctx"]), (h[:, :, CTX:TA], x[:, :, :])], "load_ctx")
                        layer_norm_stage(nc, c, ctx_in, h[:, :, 0:CTX], CTX, at(1, 1, True), at(0, 1), "lnc", room)
                        layer_norm_stage(nc, c, h[:, :, CTX:TA], h[:, :, CTX:TA], T, at(1, 0, True), at(0, 0), "lnx", room)
                        if upto == 5:
                            return dump(h)
                        pads = [(sp_(f"grid{i}", [P, ROWS + 2, GRID_W + 2]), sp_(f"seq{i}", [P, CTX + 2])) for i in range(2)]
                        with nc.Block() as block:
                            @block.gpsimd
                            def _(pool):
                                for grid, seq in pads:
                                    pool.memset(grid[:, :, :], 0.0)
                                    pool.memset(seq[:, :], 0.0)
                                pool.memset(u.v1[:, :, :, :], 1.0)
                        project_in_stage(nc, c, w, h, u, pads)
                    if upto == 6:
                        return dump(u.conv)
                    g.bm, g.cols = smm("bm", [GR, TA]), smm("gate_cols", [P, 3 * TAT, GR])
                    g.rows, g.inter = view(0, 3, TA)[0:GR], view(3 * TA, 1, TA)[0:GR, 0, :]
                    g.reset, g.temps = view(4 * TA, 1, TA)[0:GR, 0, :], view(8192, 4, TA)[0:GR]
                    g.sc = raw[:, 0:2 * DM].rearrange("p (i e t) -> p i e t", i=2, t=P)
                    g.hout = raw[:, 2 * DM:3 * DM].rearrange("p (i e t) -> p i e t", i=2, t=DH)
                    g.qi, g.decay = view(4096, 2 * MC, T).rearrange("p (d m) t -> p d m t", d=2), smm("decay", [P, 2, MC, TAT])
                    g.ktm = view(8192, TAT, DM)
                    g.kw, g.expo = view(2048, 2, DM), view(3072, 8, P).rearrange("p (i e) t -> p i e t", i=2)
                    u.pair, u.never = smm("pair_rows", [GR, 8, P]), smm("never", [P, 2, P])
                    load_stage(nc, [(u.pair[:, :, :], a["pair_rows"]), (u.never[:, :, :], a["never"])], "consts_ml")
                    gates_stage(nc, c, u, g)
                    mlstm_stage(nc, c, u, g, hsum)
                    if upto == 7:
                        return dump(hsum)
                lowrank = si("lowrank", [P, 3, DM])
                load_stage(nc, [(lowrank[:, :, :], a["lowrank"])], "load_lowrank")
                r.a, r.kh, r.kmod = u.conv[:, 0:MC, :], u.conv[:, MC:2 * MC, :], u.conv[:, 3 * MC:4 * MC, :]
                r.room = view(2048, 2, TA)
                rwkv_common_stage(nc, c, u, r, lowrank)
                for d in range(2):
                    rwkv_factors_stage(nc, c, u, r, f, lowrank, d)
            with ExitStack() as r_ctx:
                masks = Bag()
                masks.pair = r_ctx.enter_context(nc.sbuf_tensor("pair_mask", [P, 2, 2 * P], F32))
                masks.first = r_ctx.enter_context(nc.sbuf_tensor("first_mask", [P, 2, P], F32))
                masks.level = r_ctx.enter_context(nc.sbuf_tensor("level_mask", [P, 2, LEVELS, P], U32))
                load_stage(nc, [(masks.pair[:, :, :], a["pair_mask"]), (masks.first[:, :, :], a["first_mask"]),
                                (masks.level[:, :, :, :], a["level_mask"])], "load_masks")
                for d in range(2):
                    rwkv_stage(nc, c, r, f, masks, ysum, d)
            if upto == 8:
                return dump(ysum)
            mixed = sm("mixed", [P, DC, T])
            head_norm_stage(nc, c, hsum, ysum, u.mo, r.g, r.bonus, mixed)
            residual_stage(nc, c, w, mixed, x, at(2))
        col = lambda name: (lambda k: c.cols[:, COLS[name] + k:COLS[name] + k + 1])
        layer_norm_stage(nc, c, x, x, T, col("ln1_g"), col("ln1_b"), "ln1")
        if upto == 9:
            return dump(x)
        h, dev, wt = sb("h2", [P, DC, T]), sb("y2", [P, DC, T]), sb("wt", [P, TT, EXPERTS])
        rt, rt_bias, iota = sb("rt", [P, DC, E_GROUPS + EXPERTS]), sb("rt_bias", [1, E_GROUPS + EXPERTS]), sb("iota", [P, 8])
        load_stage(nc, [(dev[:, :, :], x[:, :, :]), (rt[:, :, :], a["rt"]), (rt_bias[:, :], a["rt_bias"]), (iota[:, :], a["iota"])], "load_rt")
        layer_norm_stage(nc, c, dev, h, T, at(4, 0, True), at(3), "lnm")
        router_stage(nc, c, h, rt, rt_bias, iota, wt)
        experts_stage(nc, c, w, h, wt, dev)
        last_residual_stage(nc, c, x, dev, at(5))
        layer_norm_stage(nc, c, x, x, T, col("ln2_g"), col("ln2_b"), "ln2")
        if upto == 10:
            return dump(x)
        stored = nc.alloc_semaphore("output_stored")
        with nc.Block() as block:
            @block.sync
            def _(sp):
                sp.dma_start(out, x[:, :, :]).then_inc(stored, 16)
                sp.wait_ge(stored, 16)



COLS = {}


def columns(names):
    at = 0
    for n, wide in names:
        COLS[n] = at
        at += wide
    return at


N_COLS = columns([("norm_mix0", DC), ("norm_mix1", DC), ("norm_ffn0", DC), ("norm_ffn1", DC), ("norm_final", DC),
                  ("conv", 9 * CONV_CHUNKS), ("r_w0", 2 * MC), ("r_a0", MC), ("r_kk", MC), ("r_ka", MC), ("r_bonus", MC),
                  ("m_norm_w", MC), ("r_norm_w", MC), ("r_norm_b", MC), ("ln1_g", DC), ("ln1_b", DC), ("ln2_g", DC), ("ln2_b", DC)])


def first_block(nc, c, w, a, x, upto, dump):
    first = ExitStack()
    h = first.enter_context(nc.sbuf_tensor("h", [P, DC, T], F32))
    rms_stage(nc, c, x, h, COLS["norm_mix0"], "rms0")
    with ExitStack() as layer:
        def sl(n, shape):
            return layer.enter_context(nc.sbuf_tensor(n, shape, F32))
        q, k_, v, o = sl("q_a", [P, DC, T]), sl("k_a", [P, 2, T]), sl("v_a", [P, TT, 2 * P]), sl("o_a", [P, DC, T])
        dist, sink = sl("dist_a", [P, 3 * P]), sl("sink", [P, HEADS])
        consts = nc.alloc_semaphore("consts_a")
        with nc.Block() as block:
            @block.sync
            def _(sp):
                sp.dma_start(dist[:, :], a["dist_a"]).then_inc(consts, 16)
                sp.dma_start(sink[:, :], a["sink"].partition_broadcast(P)).then_inc(consts, 16)
                sp.wait_ge(consts, 32)
        project_a_stage(nc, c, w, h, q, k_, v)
        attention_stage(nc, c, w, attention_a_items(q, k_, v, dist, o), "att_a", sink)
        out_stage(nc, c, w, o, x, "out_a")
    if upto == 1:
        return dump(x)
    rms_stage(nc, c, x, h, COLS["norm_ffn0"], "rms1")
    ffn_stage(nc, c, w, h, x, "ffn0")
    if upto == 2:
        return dump(x)
    rms_stage(nc, c, x, h, COLS["norm_mix1"], "rms2")
    with ExitStack() as layer:
        def sl(n, shape):
            return layer.enter_context(nc.sbuf_tensor(n, shape, F32))
        v, o = sl("v_b", [P, 3, TT, D]), sl("o_b", [P, DC, T])
        qk = [sl(f"qk{i}", [P, 6, T]) for i in range(2)]
        dist = sl("dist_b", [P, TT, T + 2 * P])
        consts = nc.alloc_semaphore("consts_b")
        with nc.Block() as block:
            @block.sync
            def _(sp):
                sp.dma_start(dist[:, :, :], a["dist_b"]).then_inc(consts, 16)
                sp.wait_ge(consts, 16)
        values_b_stage(nc, c, w, h, v)
        attention_stage(nc, c, w, attention_b_items(qk, v, dist, o), "att_b", None, ProjectB(c, h, qk))
        out_stage(nc, c, w, o, x, "out_b")
    if upto == 3:
        return dump(x)
    rms_stage(nc, c, x, h, COLS["norm_ffn1"], "rms3")
    ffn_stage(nc, c, w, h, x, "ffn1")
    first.close()
    rms_stage(nc, c, x, x, COLS["norm_final"], "rms4")
    if upto == 4:
        return dump(x)
    return True


def program(nc, a, out, upto=99, dump=None):
    with ExitStack() as ctx:
        def sb(n, shape, dt=F32):
            return ctx.enter_context(nc.sbuf_tensor(n, shape, dt))

        c = Core(nc)
        ring = [sb(f"ring{i}", [P, UNIT]) for i in range(RING)]
        c.wide = [ctx.enter_context(nc.psum_tensor(f"wide{i}", [P, 1024], F32)) for i in range(4)]
        c.bank = [c.wide[i // 2][:, i % 2 * 512:(i % 2 + 1) * 512] for i in range(8)]
        c.ident = sb("ident", [P, P])
        c.ones = sb("ones", [P, P])
        c.cols = sb("cols", [P, N_COLS])
        x = sb("x", [P, DC, T])
        units = a["weights"].shape[0]
        w = Weights(ring, a["weights"], [nc.alloc_semaphore(f"loaded{i}") for i in range(RING)],
                    nc.alloc_semaphore("used"), units)
        inputs = nc.alloc_semaphore("inputs_loaded")
        with nc.Block() as block:
            @block.sync
            def _(sp):
                sp.dma_start(x[:, :, :], a["x"]).then_inc(inputs, 16)
                sp.dma_start(c.cols[:, :], a["cols"]).then_inc(inputs, 16)
                sp.dma_start(c.ident[:, :], a["ident"]).then_inc(inputs, 16)
                for n in range(RING):
                    w.load(sp, n)
                sp.wait_ge(inputs, 48)

            @block.vector
            def _(dve):
                dve.memset(c.ones[:, :], 1.0)

        if not first_block(nc, c, w, a, x, upto, dump):
            return
        second_block(nc, c, w, a, x, out, upto, dump)



def blocks(wt):
    k, n = wt.shape
    return wt.reshape(k // P, P, n // P, P).transpose(2, 0, 1, 3)


def unitize(b):
    return b.reshape(-1, BLOCKS, P, P).transpose(0, 2, 1, 3).reshape(-1, P, UNIT)


def by_column_chunk(wt):
    return unitize(blocks(wt).reshape(-1, P, P))


def by_row_chunk(wt):
    return unitize(blocks(wt).transpose(1, 0, 2, 3).reshape(-1, P, P))


def gate_and_up(g, u):
    return unitize(np.stack([blocks(g), blocks(u)], 1).reshape(-1, P, P))


def feature_columns(v):
    return v.reshape(-1, P).T


def first_block_units(i):
    order = [m // 4 * 8 + m % 4 + 4 * half for m in range(DC) for half in range(2)]
    heads = np.concatenate([np.arange(h * DH, (h + 1) * DH) for h in order])
    qkv, out_a = i["w_qkv_a"][0], i["w_out_a"][0]
    yield by_column_chunk(np.concatenate([qkv[:, :D][:, heads], qkv[:, D:D + 2 * P]], 1))
    yield by_row_chunk(qkv[:, D + 2 * P:])
    yield by_column_chunk(out_a[heads, :])
    yield gate_and_up(i["w_gate"][0], i["w_up"][0])
    yield by_column_chunk(i["w_down"][0])
    b = i["w_qkv_b"][0].reshape(D, 3, 3, D)
    for g in range(3):
        for half in range(2):
            yield by_row_chunk(b[:, g, 2, half * T:(half + 1) * T])
    for m in range(DC):
        cols = slice(m * P, (m + 1) * P)
        yield by_column_chunk(np.concatenate([b[:, g, s, cols] for g in range(3) for s in range(2)], 1))
    yield by_column_chunk(i["w_out_b"][0])
    yield gate_and_up(i["w_gate"][1], i["w_up"][1])
    yield by_column_chunk(i["w_down"][1])


def second_block_units(i):
    yield by_column_chunk(i["w_ada_2"][0])
    w_in = i["w_in_2"][0]
    at = np.cumsum([0, DM, DM, DM, DM, DM, DM, DM, 4 * NH, 64, 64, 64, P])
    mv, mo, gates, lw_f, lw_b, la, lg = [w_in[:, at[n]:at[n + 1]] for n in range(5, 12)]
    zeros = np.zeros((D, P), w_in.dtype)
    pad = lambda n: zeros[:, :n]
    gate = lambda n: [gates[:, n * NH:(n + 1) * NH], pad(24), gates[:, (n + 2) * NH:(n + 3) * NH], pad(24)]
    yield by_column_chunk(np.concatenate([w_in[:, :5 * DM], lw_f, lw_b, la, pad(64), lg, *gate(0), *gate(1), mo], 1))
    yield by_row_chunk(mv)
    yield by_column_chunk(i["w_out_2"][0])
    for e in range(EXPERTS):
        yield gate_and_up(i["ex_gate_2"][0, e], i["ex_up_2"][0, e])
        yield by_column_chunk(i["ex_down_2"][0, e])


def distances():
    i, j = np.arange(P)[:, None], np.arange(3 * P)[None, :]
    rel = np.abs(j - P - i)
    dist_a = np.where(rel <= P, rel, FAR).astype(np.float32)
    dist_b = np.empty((P, TT, T + 2 * P), np.float32)
    own = np.abs(i - np.arange(P)[None, :])
    for r in range(TT):
        rel = np.abs(4 * i + r - np.arange(T)[None, :])
        dist_b[:, r, :T] = np.where(rel <= 64, rel, FAR)
        dist_b[:, r, T:T + P] = np.where(own <= 64, 4 * own, FAR)
        dist_b[:, r, T + P:] = np.where(own % 4 == 0, 4 * own, FAR)
    return dist_a, dist_b


def mixer_constants():
    pair = np.zeros((GR, 8, P), np.float32)
    for d in range(2):
        for h in range(NH):
            pair[SIDE[d] + h, d * MC + h // 2, h % 2 * DH:h % 2 * DH + DH] = 1
    i = np.arange(P)
    same = (i[:, None] // DH == i[None, :] // DH).astype(np.float32)
    before = [i[:, None] < i[None, :], i[:, None] > i[None, :]]
    upto = [b | np.eye(P, dtype=bool) for b in before]
    never = np.stack([np.where(u_, 0, -1e30) for u_ in upto], 1).astype(np.float32)
    pair_mask = np.stack([np.concatenate([b, u_], 1) for b, u_ in zip(before, upto)], 1).astype(np.float32)
    level = np.zeros((P, 2, LEVELS, P), np.uint32)
    for k in range(LEVELS):
        in_block = i[:, None] >> (k + 1) == i[None, :] >> (k + 1)
        high, low = i[:, None] >> k & 1, i[None, :] >> k & 1
        level[:, 0, k, :] = in_block & (high == 1) & (low == 0)
        level[:, 1, k, :] = in_block & (high == 0) & (low == 1)
    return {"pair_rows": pair, "same": same, "never": never, "pair_mask": pair_mask,
            "level_mask": level, "first_mask": np.ascontiguousarray(level[:, :, 0, :]).astype(np.float32),
            "iota": np.tile(np.arange(8, dtype=np.float32), (P, 1))}


def feature_major(v):
    return np.ascontiguousarray(v.T.reshape(-1, P, v.shape[0]).transpose(1, 0, 2))


def arrays_of(i):
    i = {k: np.asarray(v) for k, v in i.items()}
    dist_a, dist_b = distances()
    of = lambda name: i[name + "_2"][0].reshape(-1)
    cols = [i["norm_mix"][0], i["norm_mix"][1], i["norm_ffn"][0], i["norm_ffn"][1], i["norm_final"], of("conv_w"), of("r_w0"),
            of("r_a0"), of("r_kk"), of("r_ka"), of("r_bonus"), of("m_norm_w"), of("r_norm_w"), of("r_norm_b"),
            of("ln1_g"), of("ln1_b"), of("ln2_g"), of("ln2_b")]
    gate_bias = np.zeros((64, 2), np.float32)
    for n, name in enumerate(("m_bias_i_2", "m_bias_f_2")):
        gate_bias[0:NH, n], gate_bias[32:32 + NH, n] = i[name][0]
    lowrank = np.zeros((P, 3, DM), np.float32)
    lowrank[:, 0, :] = i["r_wB_2"][0].reshape(P, DM)
    lowrank[:64, 1, :], lowrank[:, 2, :] = i["r_aB_2"][0], i["r_gB_2"][0]
    rt = np.concatenate([i["rt_g_2"][0], i["rt_e_2"][0]], 1)
    return {
        "weights": np.concatenate([*first_block_units(i), *second_block_units(i)]),
        "x": feature_major(i["x"][0]),
        "ctx": feature_major(i["ctx_2"][0]),
        "cond": np.ascontiguousarray(np.stack([feature_columns(i["c_2"][0]), feature_columns(i["c_ctx_2"])], 2)),
        "ada_b": np.ascontiguousarray(feature_columns(i["b_ada_2"][0])),
        "cols": np.ascontiguousarray(np.concatenate([feature_columns(v) for v in cols], 1)),
        "gate_bias": gate_bias,
        "lowrank": lowrank,
        "rt": np.ascontiguousarray(rt.reshape(DC, P, -1).transpose(1, 0, 2)),
        "rt_bias": np.concatenate([i["rt_g_b_2"][0], i["rt_e_b_2"][0]])[None, :],
        "ident": np.eye(P, dtype=np.float32),
        "dist_a": dist_a,
        "dist_b": dist_b,
        "sink": np.ascontiguousarray(i["sink_a"][0]),
        **mixer_constants(),
    }



def kernel(**inputs):
    import concourse.bacc as bacc
    from concourse.bass_utils import run_bass_kernel_spmd

    nc = bacc.Bacc("TRN2", target_bir_lowering=False, num_devices=1)
    arrays = {"in_" + k: v for k, v in arrays_of(inputs).items()}
    aps = {k[3:]: nc.dram_tensor(k, v.shape, mybir.dt.from_np(v.dtype), kind="ExternalInput").ap() for k, v in arrays.items()}
    out = nc.dram_tensor("out", (P, DC, T), F32, kind="ExternalOutput").ap()
    program(nc, aps, out)
    result = run_bass_kernel_spmd(nc, [arrays], core_ids=[0]).results[0]["out"]
    return np.ascontiguousarray(result.transpose(1, 0, 2).reshape(D, T).T)[None]
```

```python
from contextlib import ExitStack

import numpy as np

import concourse.bass as bass
from concourse import mybir

F32 = mybir.dt.float32
F32R = mybir.dt.float32r
U32 = mybir.dt.uint32
ALU = mybir.AluOpType
ACT = mybir.ActivationFunctionType
AX = mybir.AxisListType

P = 128
D = 1024
DC = D // P
T = 512
TT = T // P
DH = 64
HEADS = 16
D_FF = -(-8 * D // (3 * 256)) * 256
FC = D_FF // P
BLOCKS = 16
UNIT = BLOCKS * P
RING = 4
EPS = 1e-6
FAR = 1e33

U_QKV_A = 12 * DC // BLOCKS
U_OUT = DC * DC // BLOCKS
U_GATE_UP = FC
U_DOWN = FC * DC // BLOCKS
U_V_B = 3 * DC * DC // BLOCKS
U_QK_B = 3


class Weights:

    def __init__(self, ring, stream, loaded, used, units):
        self.ring, self.stream, self.loaded, self.used, self.units = ring, stream, loaded, used, units
        self.at = 0

    def arrived(self, pe, j, i):
        n = self.at + i
        pe.wait_ge(self.loaded[n % RING], 16 * (j + (n // RING + 1)))
        return self.ring[n % RING]


    def write_hi(self, act, hi_ready, j, i):
        n = self.at + i
        act.wait_ge(self.loaded[n % RING], 16 * (j + (n // RING + 1)))
        if n >= 2:
            act.wait_ge(self.used, j * RING + (n - 1))
        act.copy(self.hi[n % 2][:, :], self.ring[n % RING][:, :]).then_inc(hi_ready, 1)

    def write_lo(self, pool, hi_ready, lo_ready, j, i):
        n = self.at + i
        pool.wait_ge(hi_ready, j * RING + (i + 1))
        pool.tensor_tensor(self.lo[n % RING][:, :], self.ring[n % RING][:, :],
                           self.hi[n % 2][:, :].bitcast(F32), ALU.subtract).then_inc(lo_ready, 1)

    def parts(self, pe, lo_ready, j, i):
        n = self.at + i
        pe.wait_ge(lo_ready, j * RING + (i + 1))
        return self.hi[n % 2], self.lo[n % RING]

    def load(self, sp, n):
        sp.dma_start(self.ring[n % RING][:, :], self.stream[n]).then_inc(self.loaded[n % RING], 16)

    def feed(self, sp, units):
        def one(j, i):
            n = self.at + i
            sp.wait_ge(self.used, j * RING + (n + 1))
            sp.dma_start(self.ring[n % RING][:, :], self.stream[j * RING + (n + RING)]).then_inc(
                self.loaded[n % RING], 16)
        last = max(0, min(units, self.units - RING - self.at))
        whole = last // RING
        if whole > 1:
            with sp.Fori(0, whole) as j:
                for i in range(RING):
                    one(j, i)
        else:
            whole = 0
        for i in range(whole * RING, last):
            one(0, i)


def over(eng, count, step, body, least=2):
    whole = count // step if count // step >= least else 0
    if whole:
        with eng.Fori(0, whole) as j:
            for i in range(step):
                body(j, i)
    for i in range(whole * step, count):
        body(0, i)


def product(pe, dst, a, b, start, stop):
    pe.matmul(dst, a[0], b[0], start=start, stop=False)
    pe.matmul(dst, a[0], b[1], start=False, stop=False)
    return pe.matmul(dst, a[1], b[0], start=False, stop=stop)


class Core:

    def __init__(self, nc):
        self.nc, self.retired = nc, []

    def semaphores(self, name, names):
        fresh = [self.nc.alloc_semaphore(f"{name}_{n}") for n in names]
        if self.retired:
            self.nc.clear_and_free_semaphores(self.retired)
        self.retired = fresh
        return fresh



def rms_stage(nc, c, src, dst, gain, name):
    split = isinstance(dst, tuple)
    with ExitStack() as ctx:
        sq = ctx.enter_context(nc.sbuf_tensor(f"{name}_sq", [P, DC, T], F32))
        rstd = ctx.enter_context(nc.sbuf_tensor(f"{name}_rstd", [P, 2, T], F32))
        squared, summed, mean_ready, root_ready, rstd_ready, scaled, hi_ready, even_lo_ready, odd_lo_ready, odd_squared = c.semaphores(
            name, ("squared", "summed", "mean_ready", "root_ready", "rstd_ready", "scaled", "hi_ready", "even_lo_ready",
                   "odd_lo_ready", "odd_squared"))
        whole = sq if split else dst

        def lo(eng, k, ready):
            eng.wait_ge(hi_ready, k + 1)
            eng.tensor_tensor(dst[1][:, k, :], whole[:, k, :], dst[0][:, k, :].bitcast(F32), ALU.subtract).then_inc(ready, 1)

        with nc.Block() as block:
            if split:
                @block.gpsimd
                def _(pool):
                    for k in range(1, DC, 2):
                        lo(pool, k, odd_lo_ready)

            @block.scalar
            def _(act):
                for k in range(0, DC, 2):
                    act.activation(sq[:, k, :], src[:, k, :], ACT.Square).then_inc(squared, 1)
                act.wait_ge(mean_ready, 1)
                act.activation(rstd[:, 1, :], rstd[:, 0, :], ACT.Sqrt).then_inc(root_ready, 1)
                if split:
                    for k in range(DC):
                        act.wait_ge(scaled, k + 1)
                        act.copy(dst[0][:, k, :], whole[:, k, :]).then_inc(hi_ready, 1)

            @block.tensor
            def _(pe):
                for k in range(DC):
                    pe.wait_ge((squared, odd_squared)[k % 2], k // 2 + 1)
                    m = pe.matmul(c.bank[0][:, :], c.ones[:, :], sq[:, k, :], start=(k == 0), stop=(k == DC - 1))
                m.then_inc(summed, 1)

            @block.vector
            def _(dve):
                for k in range(1, DC, 2):
                    dve.tensor_tensor(sq[:, k, :], src[:, k, :], src[:, k, :], ALU.mult).then_inc(odd_squared, 1)
                dve.wait_ge(summed, 1)
                dve.tensor_scalar(rstd[:, 0, :], c.bank[0][:, :], 1.0 / D, EPS, ALU.mult, ALU.add).then_inc(mean_ready, 1)
                dve.wait_ge(root_ready, 1)
                dve.reciprocal(rstd[:, 0, :], rstd[:, 1, :]).then_inc(rstd_ready, 1)
                dve.wait_ge(rstd_ready, 1)
                for k in range(DC):
                    dve.scalar_tensor_tensor(out=whole[:, k, :], in0=src[:, k, :], scalar=c.cols[:, gain + k:gain + k + 1],
                                             in1=rstd[:, 0, :], op0=ALU.mult, op1=ALU.mult).then_inc(scaled, 1)
                    if split and k % 2 == 1:
                        lo(dve, k - 1, even_lo_ready)



def ffn_stage(nc, c, w, h, x, name):
    with ExitStack() as ctx:
        def sb(n, shape, dt=F32):
            return ctx.enter_context(nc.sbuf_tensor(f"{name}_{n}", shape, dt))
        hidden = sb("hidden_hi", [P, FC, T], F32R), sb("hidden_lo", [P, FC, T], F32R)
        silu, whole = sb("silu", [P, 2, T]), sb("whole", [P, 2, T])
        gate_done, silu_ready, whole_ready, hidden_hi_ready, hidden_ready, down_done, added, hi_ready, lo_ready = c.semaphores(
            name, ("gate_done", "silu_ready", "whole_ready", "hidden_hi_ready", "hidden_ready", "down_done", "added",
                   "hi_ready", "lo_ready"))
        bank = c.bank
        units = U_GATE_UP + U_DOWN
        with nc.Block() as block:
            @block.sync
            def _(sp):
                w.feed(sp, units)

            @block.gpsimd
            def _(pool):
                over(pool, units, RING, lambda j, i: w.write_lo(pool, hi_ready, lo_ready, j, i))

            @block.tensor
            def _(pe):
                def gate_up(first, j, i):
                    unit = w.parts(pe, lo_ready, j, first + i)
                    if first + i >= 2:
                        pe.wait_ge(whole_ready, j * RING + (first + i - 1))
                    for half in range(2):
                        for k in range(DC):
                            b = (half * DC + k) * P
                            m = product(pe, bank[2 * (i % 2) + half][:, :], [part[:, b:b + P] for part in unit],
                                        [part[:, k, :] for part in h], k == 0, k == DC - 1)
                        m.then_inc((gate_done, w.used)[half], 1)

                for i in range(RING):
                    gate_up(0, 0, i)
                over(pe, FC - RING, RING, lambda j, i: gate_up(RING, j, i))
                pe.wait_ge(hidden_ready, FC)
                for m_ in range(DC):
                    if m_ >= 2:
                        pe.wait_ge(added, m_ - 1)
                    for k in range(FC):
                        b = m_ * FC + k
                        if b % BLOCKS == 0:
                            unit = w.parts(pe, lo_ready, 0, FC + b // BLOCKS)
                        q = b % BLOCKS * P
                        m = product(pe, bank[4 + m_ % 2][:, :], [part[:, q:q + P] for part in unit],
                                    [part[:, k, :] for part in hidden], k == 0, k == FC - 1)
                        if b % BLOCKS == BLOCKS - 1:
                            m.then_inc(w.used, 1)
                        elif k == FC - 1:
                            m.then_inc(down_done, 1)

            @block.scalar
            def _(act):
                w.write_hi(act, hi_ready, 0, 0)
                w.write_hi(act, hi_ready, 0, 1)

                def one(j, i):
                    act.wait_ge(gate_done, j * RING + (i + 1))
                    act.activation(silu[:, i % 2, :], bank[2 * (i % 2)][:, :], ACT.Silu).then_inc(silu_ready, 1)
                    w.write_hi(act, hi_ready, j, i + 2)
                    act.wait_ge(whole_ready, j * RING + (i + 1))
                    act.copy(hidden[0][:, j * RING + i, :], whole[:, i % 2, :]).then_inc(hidden_hi_ready, 1)
                over(act, FC, RING, one)
                for n in range(FC + 2, units):
                    w.write_hi(act, hi_ready, 0, n)

            @block.vector
            def _(dve):
                def one(j, i):
                    dve.wait_ge(w.used, j * RING + (w.at + i + 1))
                    dve.wait_ge(silu_ready, j * RING + (i + 1))
                    dve.tensor_tensor(whole[:, i % 2, :], silu[:, i % 2, :], bank[2 * (i % 2) + 1][:, :],
                                      ALU.mult).then_inc(whole_ready, 1)
                    dve.wait_ge(hidden_hi_ready, j * RING + (i + 1))
                    dve.tensor_tensor(hidden[1][:, j * RING + i, :], whole[:, i % 2, :], hidden[0][:, j * RING + i, :].bitcast(F32),
                                      ALU.subtract).then_inc(hidden_ready, 1)
                over(dve, FC, RING, one)
                for m_ in range(DC):
                    if m_ < DC - 1:
                        dve.wait_ge(down_done, m_ + 1)
                    else:
                        dve.wait_ge(w.used, w.at + units)
                    dve.tensor_tensor(x[:, m_, :], x[:, m_, :], bank[4 + m_ % 2][:, :], ALU.add).then_inc(added, 1)
    w.at += units



def out_stage(nc, c, w, o, parts, x, name, kept=None):
    with ExitStack() as ctx:
        chunk_done, added, hi_ready, lo_ready, o_hi_ready, o_ready, x_back = c.semaphores(
            name, ("chunk_done", "added", "hi_ready", "lo_ready", "o_hi_ready", "o_ready", "x_back"))
        bank = c.bank
        with nc.Block() as block:
            @block.sync
            def _(sp):
                if kept is not None:
                    sp.wait_ge(o_ready, DC)
                    sp.dma_start(x[:, :, :], kept).then_inc(x_back, 16)
                w.feed(sp, U_OUT)

            @block.gpsimd
            def _(pool):
                for n in range(U_OUT):
                    w.write_lo(pool, hi_ready, lo_ready, 0, n)

            @block.scalar
            def _(act):
                w.write_hi(act, hi_ready, 0, 0)
                for k in range(DC):
                    act.copy(parts[0][:, k, :], o[:, k, :]).then_inc(o_hi_ready, 1)
                for n in range(1, U_OUT):
                    w.write_hi(act, hi_ready, 0, n)

            @block.tensor
            def _(pe):
                for m_ in range(DC):
                    if m_ % 2 == 0:
                        unit = w.parts(pe, lo_ready, 0, m_ // 2)
                    for k in range(DC):
                        b = (m_ % 2 * DC + k) * P
                        if m_ == 0:
                            pe.wait_ge(o_ready, k + 1)
                        m = product(pe, bank[m_][:, :], [part[:, b:b + P] for part in unit], [part[:, k, :] for part in parts],
                                    k == 0, k == DC - 1)
                    m.then_inc((chunk_done, w.used)[m_ % 2], 1)

            @block.vector
            def _(dve):
                for k in range(DC):
                    dve.wait_ge(o_hi_ready, k + 1)
                    dve.tensor_tensor(parts[1][:, k, :], o[:, k, :], parts[0][:, k, :].bitcast(F32), ALU.subtract).then_inc(o_ready, 1)
                if kept is not None:
                    dve.wait_ge(x_back, 16)
                for m_ in range(DC):
                    if m_ % 2 == 0:
                        dve.wait_ge(chunk_done, m_ // 2 + 1)
                    else:
                        dve.wait_ge(w.used, w.at + m_ // 2 + 1)
                    dve.tensor_tensor(x[:, m_, :], x[:, m_, :], bank[m_][:, :], ALU.add).then_inc(added, 1)
    w.at += U_OUT


def project_a_stage(nc, c, w, h, q, k_, v):
    KVC = 2
    chunk_done, copied, v_done, v_copied, hi_ready, lo_ready = c.semaphores("proj_a", (
        "chunk_done", "copied", "v_done", "v_copied", "hi_ready", "lo_ready"))
    bank = c.bank
    with nc.Block() as block:
        @block.sync
        def _(sp):
            w.feed(sp, U_QKV_A)

        @block.gpsimd
        def _(pool):
            for n in range(U_QKV_A):
                w.write_lo(pool, hi_ready, lo_ready, 0, n)

        @block.tensor
        def _(pe):
            for m_ in range(DC + KVC):
                if m_ % 2 == 0:
                    unit = w.parts(pe, lo_ready, 0, m_ // 2)
                if m_ >= 4:
                    pe.wait_ge(copied, m_ - 3)
                for k in range(DC):
                    b = (m_ % 2 * DC + k) * P
                    m = product(pe, bank[m_ % 4][:, :], [part[:, b:b + P] for part in unit], [part[:, k, :] for part in h],
                                k == 0, k == DC - 1)
                m.then_inc((chunk_done, w.used)[m_ % 2], 1)
            unit = w.parts(pe, lo_ready, 0, U_QKV_A - 1)
            for t in range(TT):
                for k in range(DC):
                    m = product(pe, bank[4 + t][:, 0:2 * P], [part[:, k, t * P:(t + 1) * P] for part in h],
                                [part[:, 2 * k * P:2 * (k + 1) * P] for part in unit], k == 0, k == DC - 1)
                m.then_inc(v_done if t < TT - 1 else w.used, 1)

        @block.scalar
        def _(act):
            w.write_hi(act, hi_ready, 0, 0)
            w.write_hi(act, hi_ready, 0, 1)
            for m_ in range(DC + KVC):
                if m_ % 2 == 0:
                    act.wait_ge(chunk_done, m_ // 2 + 1)
                else:
                    act.wait_ge(w.used, w.at + m_ // 2 + 1)
                if m_ < DC:
                    act.mul(q[:, m_, :], bank[m_ % 4][:, :], DH ** -0.5).then_inc(copied, 1)
                else:
                    act.copy(k_[:, m_ - DC, :], bank[m_ % 4][:, :]).then_inc(copied, 1)
                if m_ % 2 and m_ // 2 + 2 < U_QKV_A:
                    w.write_hi(act, hi_ready, 0, m_ // 2 + 2)

        @block.vector
        def _(dve):
            for t in range(TT):
                if t < TT - 1:
                    dve.wait_ge(v_done, t + 1)
                else:
                    dve.wait_ge(w.used, w.at + U_QKV_A)
                dve.tensor_copy(v[:, t, :], bank[4 + t][:, 0:2 * P]).then_inc(v_copied, 1)
    w.at += U_QKV_A


class Item:

    def __init__(self, head, half, slope, dist, scores, values, out, pair=0):
        self.head, self.half, self.slope, self.dist, self.scores, self.values, self.out, self.pair = (
            head, half, slope, dist, scores, values, out, pair)
        self.keys = dist.shape[-1]


def attention_stage(nc, c, w, items, name, sink, project=None):
    N = len(items)
    WIDE = max(i.keys for i in items)
    LAG = 2
    SB = LAG + 1
    with ExitStack() as ctx:
        def sb(n, shape):
            return ctx.enter_context(nc.sbuf_tensor(f"{name}_{n}", shape, F32))
        bias = sb("bias", [P, 2, WIDE])
        prob = sb("prob", [P, SB, WIDE])
        probT = sb("probT", [P, 2, WIDE])
        top = sb("top", [P, N])
        negtop = sb("negtop", [P, N])
        den = sb("den", [P, N])
        sunk = sb("sunk", [P, N])
        total = sb("total", [P, N])
        rden = sb("rden", [P, N])
        (bias_ready, scores_done, biased, negtop_ready, prob_ready, sunk_ready, total_ready, rden_ready, prob_scaled,
         turned, probT_ready, out_done, out_copied, pair_chunk_done, pair_chunk_copied, hi_ready, lo_ready) = c.semaphores(name, (
             "bias_ready", "scores_done", "biased", "negtop_ready", "prob_ready", "sunk_ready", "total_ready",
             "rden_ready", "prob_scaled", "turned", "probT_ready", "out_done", "out_copied", "pair_chunk_done",
             "pair_chunk_copied", "hi_ready", "lo_ready"))
        S = [c.wide[0], c.wide[1]]
        PT = c.wide[2]
        O = c.bank[6]
        per = project.chunks if project else 0
        pairs = project.pairs if project else 0
        in_pair = N // pairs if pairs else N + 1

        def chunk_after(i):
            if not project:
                return None
            pair, j = i // in_pair + 1, i % in_pair
            return (pair, j) if pair < pairs and j < per else None

        with nc.Block() as block:
            if project:
                @block.sync
                def _(sp):
                    w.feed(sp, project.units)

            def unit_after(i):
                chunk = chunk_after(i)
                if chunk and chunk[1] % 2 == 0:
                    n = (chunk[0] * per + chunk[1]) // 2 + 1
                    return n if n < project.units else None

            @block.gpsimd
            def _(pool):
                if project:
                    for n in range(per // 2 + 1):
                        w.write_lo(pool, hi_ready, lo_ready, 0, n)
                for i, it in enumerate(items):
                    if i >= 2:
                        pool.wait_ge(biased, i - 1)
                    pool.tensor_scalar(bias[:, i % 2, 0:it.keys], it.dist, -it.slope, None, ALU.mult).then_inc(bias_ready, 1)
                    if unit_after(i):
                        w.write_lo(pool, hi_ready, lo_ready, 0, unit_after(i))

            @block.tensor
            def _(pe):
                def pair_chunk(pair, j):
                    n = pair * per + j
                    if n >= 1:
                        pe.wait_ge(pair_chunk_copied, n)
                    unit = w.parts(pe, lo_ready, 0, n // 2)
                    for k in range(DC):
                        b = (n % 2 * DC + k) * P
                        m = product(pe, c.bank[7][:, :], [part[:, b:b + P] for part in unit],
                                    [part[:, k, :] for part in project.h], k == 0, k == DC - 1)
                    m.then_inc((pair_chunk_done, w.used)[n % 2], 1)

                def transposes(i):
                    it = items[i]
                    pe.wait_ge(prob_scaled, i + 1)
                    if i >= 1:
                        pe.wait_ge(probT_ready, i)
                    for t in range(it.keys // P):
                        m = pe.transpose(PT[:, t * P:(t + 1) * P], prob[:, i % SB, t * P:(t + 1) * P], c.ident[:, :])
                    m.then_inc(turned, 1)

                def values(i):
                    it = items[i]
                    pe.wait_ge(probT_ready, i + 1)
                    if i >= 1:
                        pe.wait_ge(out_copied, i)
                    n = it.keys // P
                    for t in range(n):
                        m = pe.matmul(O[it.half * DH:(it.half + 1) * DH, 0:P], it.values[t], probT[:, i % 2, t * P:(t + 1) * P],
                                      start=(t == 0), stop=(t == n - 1))
                    m.then_inc(out_done, 1)

                for j in range(per):
                    pair_chunk(0, j)
                for i in range(N + LAG + 1):
                    if i < N:
                        it = items[i]
                        if project and i % in_pair == 0:
                            pe.wait_ge(pair_chunk_copied, (i // in_pair + 1) * per)
                        if i >= 2:
                            pe.wait_ge(biased, i - 1)
                        for lhs, rhs, at in it.scores:
                            m = pe.matmul(S[i % 2][:, at:at + rhs.shape[-1]], lhs, rhs, start=True, stop=True)
                        m.then_inc(scores_done, 1)
                    if LAG + 1 <= i:
                        values(i - LAG - 1)
                    if i < N and chunk_after(i):
                        pair_chunk(*chunk_after(i))
                    if LAG <= i < N + LAG:
                        transposes(i - LAG)

            @block.vector
            def _(dve):
                def scale_of(i):
                    dve.wait_ge(prob_ready, i + 1)
                    if sink is not None:
                        dve.wait_ge(sunk_ready, i + 1)
                        dve.tensor_tensor(total[:, i:i + 1], den[:, i:i + 1], sunk[:, i:i + 1], ALU.add).then_inc(total_ready, 1)
                        dve.wait_ge(total_ready, i + 1)
                    src = den if sink is None else total
                    dve.reciprocal(rden[:, i:i + 1], src[:, i:i + 1]).then_inc(rden_ready, 1)
                    dve.wait_ge(rden_ready, i + 1)
                    keys = items[i].keys
                    dve.tensor_scalar(prob[:, i % SB, 0:keys], prob[:, i % SB, 0:keys], rden[:, i:i + 1], None, ALU.mult).then_inc(prob_scaled, 1)

                def copy_out(i):
                    it = items[i]
                    dve.wait_ge(out_done, i + 1)
                    dve.tensor_copy(it.out, O[it.half * DH:(it.half + 1) * DH, 0:P]).then_inc(out_copied, 1)

                for j in range(per):
                    if j % 2:
                        project.copy(dve, w, 0, j, pair_chunk_done, pair_chunk_copied)
                for i in range(N + LAG + 1):
                    if i < N:
                        it = items[i]
                        dve.wait_ge(scores_done, i + 1)
                        dve.wait_ge(bias_ready, i + 1)
                        if i >= SB:
                            dve.wait_ge(turned, i - SB + 1)
                        dve.tensor_tensor_reduce(prob[:, i % SB, 0:it.keys], S[i % 2][:, 0:it.keys], bias[:, i % 2, 0:it.keys],
                                                 1.0, -3e38, ALU.add, ALU.max, top[:, i:i + 1]).then_inc(biased, 1)
                        dve.wait_ge(biased, i + 1)
                        dve.tensor_scalar(negtop[:, i:i + 1], top[:, i:i + 1], -1.0, None, ALU.mult).then_inc(negtop_ready, 1)
                    if 0 <= i - LAG + 1 < N:
                        scale_of(i - LAG + 1)
                    if i >= LAG + 1:
                        copy_out(i - LAG - 1)
                    if i < N and chunk_after(i) and chunk_after(i)[1] % 2:
                        project.copy(dve, w, *chunk_after(i), pair_chunk_done, pair_chunk_copied)

            @block.scalar
            def _(act):
                if project:
                    w.write_hi(act, hi_ready, 0, 0)
                for j in range(per):
                    if j % 2 == 0:
                        project.copy(act, w, 0, j, pair_chunk_done, pair_chunk_copied)
                        w.write_hi(act, hi_ready, 0, j // 2 + 1)
                for i in range(N + LAG):
                    if i < N:
                        it = items[i]
                        act.wait_ge(negtop_ready, i + 1)
                        if sink is not None:
                            act.activation(sunk[:, i:i + 1], sink[:, it.head:it.head + 1], ACT.Exp,
                                           bias=negtop[:, i:i + 1]).then_inc(sunk_ready, 1)
                        act.activation(prob[:, i % SB, 0:it.keys], prob[:, i % SB, 0:it.keys], ACT.Exp,
                                       bias=negtop[:, i:i + 1], accum_out=den[:, i:i + 1]).then_inc(prob_ready, 1)
                    if i < N and chunk_after(i) and chunk_after(i)[1] % 2 == 0:
                        project.copy(act, w, *chunk_after(i), pair_chunk_done, pair_chunk_copied)
                        if unit_after(i):
                            w.write_hi(act, hi_ready, 0, unit_after(i))
                    if i >= LAG:
                        n = i - LAG
                        act.wait_ge(turned, n + 1)
                        if n >= 2:
                            act.wait_ge(out_done, n - 1)
                        act.copy(probT[:, n % 2, 0:items[n].keys], PT[:, 0:items[n].keys]).then_inc(probT_ready, 1)
    if project:
        w.at += project.units


def slopes():
    return [2.0 ** (-8.0 * (h + 1) / HEADS) for h in range(HEADS)]


def attention_a_items(q, k_, v, dist, o):
    items = []
    for m in range(DC):
        for half in range(2):
            head = m // 4 * 8 + m % 4 + 4 * half
            kv = m // 4 * 2 + half
            rows = slice(half * DH, (half + 1) * DH)
            for b in range(TT):
                first, last = max(0, b - 1), min(TT, b + 2)
                off = (first - b + 1) * P
                keys = (last - first) * P
                items.append(Item(head, half, slopes()[head], dist[:, off:off + keys],
                                  [(q[rows, m, b * P:(b + 1) * P], k_[rows, m // 4, first * P:last * P], 0)],
                                  [v[:, t, kv * DH:(kv + 1) * DH] for t in range(first, last)],
                                  o[rows, m, b * P:(b + 1) * P]))
    return items


def attention_b_items(qk, v, dist, o):
    items = []
    for m in range(DC):
        for half in range(2):
            rows = slice(half * DH, (half + 1) * DH)
            buf = qk[m % 2]
            cols = slice((2 * m + half) * DH, (2 * m + half + 1) * DH)
            for r in range(TT):
                tile = slice(r * P, (r + 1) * P)
                items.append(Item(2 * m + half, half, slopes()[2 * m + half], dist[:, r, :],
                                  [(buf[rows, 0, tile], buf[rows, 1, :], 0), (buf[rows, 2, tile], buf[rows, 3, tile], T),
                                   (buf[rows, 4, tile], buf[rows, 5, tile], T + P)],
                                  [v[:, 0, t, cols] for t in range(TT)] + [v[:, 1, r, cols], v[:, 2, r, cols]],
                                  o[rows, m, :].rearrange("p (i r) -> p r i", r=4)[:, r, :]))
    return items


class ProjectB:
    chunks, pairs, units = 6, DC, U_QK_B * DC

    def __init__(self, c, h, qk):
        self.c, self.h, self.qk = c, h, qk

    def copy(self, eng, w, pair, j, done, copied):
        n = pair * self.chunks + j
        if n % 2 == 0:
            eng.wait_ge(done, n // 2 + 1)
        else:
            eng.wait_ge(w.used, w.at + n // 2 + 1)
        src, dst = self.c.bank[7][:, :], self.qk[pair % 2][:, j, :]
        if j != 1:
            src = src.rearrange("p (i r) -> p r i", r=4)
            dst = dst.rearrange("p (r i) -> p r i", r=4)
        if j % 2 == 0:
            eng.mul(dst, src, DH ** -0.5).then_inc(copied, 1)
        else:
            eng.tensor_copy(dst, src).then_inc(copied, 1)


def values_b_stage(nc, c, w, h, v):
    copied_act, copied_dve, hi_ready, lo_ready = c.semaphores("v_b", ("copied_act", "copied_dve", "hi_ready", "lo_ready"))
    with nc.Block() as block:
        @block.sync
        def _(sp):
            w.feed(sp, U_V_B)

        @block.gpsimd
        def _(pool):
            for n in range(U_V_B):
                w.write_lo(pool, hi_ready, lo_ready, 0, n)

        @block.tensor
        def _(pe):
            for n in range(6):
                g = n // 2
                if n >= 2:
                    pe.wait_ge(copied_act, 2 * (n - 1))
                    pe.wait_ge(copied_dve, 2 * (n - 1))
                for k in range(DC):
                    if k % 4 == 0:
                        unit = w.parts(pe, lo_ready, 0, 2 * n + k // 4)
                    for t in range(TT):
                        rows = [part[:, k, t * P:(t + 1) * P] if g == 0 else part[:, k, :].rearrange("p (i r) -> p r i", r=4)[:, t, :]
                                for part in h]
                        m = product(pe, c.bank[n % 2 * 4 + t][:, :], rows, [part[:, k % 4 * T:(k % 4 + 1) * T] for part in unit],
                                    k == 0, k == DC - 1)
                    if k % 4 == 3:
                        m.then_inc(w.used, 1)

        @block.scalar
        def _(act):
            w.write_hi(act, hi_ready, 0, 0)
            w.write_hi(act, hi_ready, 0, 1)
            for n in range(6):
                if n < 5:
                    w.write_hi(act, hi_ready, 0, 2 * n + 2)
                    w.write_hi(act, hi_ready, 0, 2 * n + 3)
                act.wait_ge(w.used, w.at + 2 * n + 2)
                for t in range(2):
                    act.copy(v[:, n // 2, t, n % 2 * T:(n % 2 + 1) * T], c.bank[n % 2 * 4 + t][:, :]).then_inc(copied_act, 1)

        @block.vector
        def _(dve):
            for n in range(6):
                dve.wait_ge(w.used, w.at + 2 * n + 2)
                for t in range(2, 4):
                    dve.tensor_copy(v[:, n // 2, t, n % 2 * T:(n % 2 + 1) * T], c.bank[n % 2 * 4 + t][:, :]).then_inc(copied_dve, 1)
    w.at += U_V_B



DM = 512
MC = DM // P
NH = 8
CTX = 256
TA = CTX + T
TAT = TA // P
GRID_W = 64
ROWS = T // GRID_W
CONV_CHUNKS = 5 * MC
DECAY = float(np.exp(-0.5))
LN_EPS = 1e-6
GN_EPS = 64e-5
ALPHA = 2.0 ** 0.25
U_ADA = 6 * DC * DC // BLOCKS
U_IN = 16
U_IN_COLUMNS = 14
U_OUT2 = DC * DC // BLOCKS
E_GROUPS, E_EACH = 4, 8
EXPERTS = E_GROUPS * E_EACH
D_EXPERT = 512
EC = D_EXPERT // P
U_EXPERT = 6


def ada_stage(nc, c, w, cond, mod, mod1, bias, room):
    act_ready, row_ready, summed, mod_ready, mod1_ready = c.semaphores("ada", (
        "act_ready", "row_ready", "summed", "mod_ready", "mod1_ready"))
    n_out = 6 * DC
    groups = U_ADA // 2
    rows = room[0:2, 0:n_out * P]
    out = c.bank[0][:, 0:2 * n_out].rearrange("p (m s) -> p m s", s=2)
    with nc.Block() as block:
        @block.sync
        def _(sp):
            w.feed(sp, U_ADA)

        @block.scalar
        def _(act):
            act.activation(cond[:, :, :], cond[:, :, :], ACT.Silu).then_inc(act_ready, 1)
            for g in range(groups):
                act.wait_ge(w.used, w.at + 2 * g + 2)
                act.copy(rows[:, g * T:(g + 1) * T], c.bank[1 + g % 2][0:2, :]).then_inc(row_ready, 1)

        @block.tensor
        def _(pe):
            pe.wait_ge(act_ready, 1)

            def one(first, j, i):
                if first and i % 2 == 0:
                    pe.wait_ge(row_ready, j * 2 + ((first + i) // 2 - 1))
                unit = w.arrived(pe, j, first + i)
                for n in range(4):
                    k = i % 2 * 4 + n
                    m = pe.matmul(c.bank[1 + i // 2][0:2, :], cond[:, k, :], unit[:, n * T:(n + 1) * T], start=(k == 0), stop=(k == DC - 1))
                m.then_inc(w.used, 1)

            for i in range(RING):
                one(0, 0, i)
            over(pe, U_ADA - RING, RING, lambda j, i: one(RING, j, i))
            pe.wait_ge(row_ready, groups)
            for m_ in range(n_out):
                m = pe.matmul(out[:, m_, :], rows[:, m_ * P:(m_ + 1) * P], c.ident[0:2, 0:2], start=True, stop=True)
            m.then_inc(summed, 1)

        @block.vector
        def _(dve):
            dve.wait_ge(summed, 1)
            dve.tensor_tensor(mod[:, :, :], out, bias.unsqueeze(2).broadcast_to([P, n_out, 2]), ALU.add).then_inc(mod_ready, 1)
            dve.wait_ge(mod_ready, 1)
            dve.tensor_scalar(mod1[:, :, :], mod[:, :, :], 1.0, None, ALU.add).then_inc(mod1_ready, 1)
    w.at += U_ADA


def layer_norm_stage(nc, c, src, dst, n, scale, shift, name, room=None):
    with ExitStack() as ctx:
        if room is None:
            room = ctx.enter_context(nc.sbuf_tensor(f"{name}_room", [P, (DC + 3) * n], F32))
        sq = room[:, 0:DC * n].rearrange("p (k t) -> p k t", t=n)
        st = room[:, DC * n:(DC + 3) * n].rearrange("p (k t) -> p k t", t=n)
        summed, mean_ready, centered, squared, square_summed, var_ready, root_ready, rstd_ready, scaled, done = c.semaphores(
            name, ("summed", "mean_ready", "centered", "squared", "square_summed", "var_ready", "root_ready",
                   "rstd_ready", "scaled", "done"))
        with nc.Block() as block:
            @block.tensor
            def _(pe):
                for k in range(DC):
                    m = pe.matmul(c.bank[0][:, 0:n], c.ones[:, :], src[:, k, :], start=(k == 0), stop=(k == DC - 1))
                m.then_inc(summed, 1)
                for k in range(DC):
                    pe.wait_ge(squared, k + 1)
                    m = pe.matmul(c.bank[1][:, 0:n], c.ones[:, :], sq[:, k, :], start=(k == 0), stop=(k == DC - 1))
                m.then_inc(square_summed, 1)

            @block.vector
            def _(dve):
                dve.wait_ge(summed, 1)
                dve.tensor_scalar(st[:, 0, :], c.bank[0][:, 0:n], 1.0 / D, None, ALU.mult).then_inc(mean_ready, 1)
                dve.wait_ge(mean_ready, 1)
                for k in range(DC):
                    dve.tensor_tensor(src[:, k, :], src[:, k, :], st[:, 0, :], ALU.subtract).then_inc(centered, 1)
                dve.wait_ge(square_summed, 1)
                dve.tensor_scalar(st[:, 1, :], c.bank[1][:, 0:n], 1.0 / D, LN_EPS, ALU.mult, ALU.add).then_inc(var_ready, 1)
                dve.wait_ge(root_ready, 1)
                dve.reciprocal(st[:, 1, :], st[:, 2, :]).then_inc(rstd_ready, 1)
                dve.wait_ge(rstd_ready, 1)
                dve.wait_ge(centered, DC)
                for k in range(DC):
                    dve.tensor_tensor(src[:, k, :], src[:, k, :], st[:, 1, :], ALU.mult).then_inc(scaled, 1)

            @block.scalar
            def _(act):
                for k in range(DC):
                    act.wait_ge(centered, k + 1)
                    act.activation(sq[:, k, :], src[:, k, :], ACT.Square).then_inc(squared, 1)
                act.wait_ge(var_ready, 1)
                act.activation(st[:, 2, :], st[:, 1, :], ACT.Sqrt).then_inc(root_ready, 1)
                for k in range(DC):
                    act.wait_ge(scaled, k + 1)
                    act.activation(dst[:, k, :], src[:, k, :], ACT.Identity, bias=shift(k), scale=scale(k)).then_inc(done, 1)


def split_stage(nc, c, src, hi, lo, name):
    chunks = src.shape[1]
    hi_done, lo_done = c.semaphores(name, ("hi_done", "lo_done"))
    with nc.Block() as block:
        @block.scalar
        def _(act):
            for k in range(chunks):
                act.copy(hi[k], src[:, k, :]).then_inc(hi_done, 1)

        @block.vector
        def _(dve):
            for k in range(chunks):
                dve.wait_ge(hi_done, k + 1)
                dve.tensor_tensor(lo[k], src[:, k, :], hi[k].bitcast(F32), ALU.subtract).then_inc(lo_done, 1)



def project_in_stage(nc, c, w, h, u, pads):
    items = [("conv", m) for m in range(CONV_CHUNKS)] + [("lw", 0), ("la", 0), ("lg", 0), ("li", 0), ("lf", 0)]
    items += [("mo", m) for m in range(MC)]
    chunk_of = []
    for kind, m in items:
        chunk_of.append(chunk_of[-1] + (kind != "lf") if chunk_of else 0)
    chunk_done, copied, convolved, v_copied_act, v_copied_dve, silu_done, hi_ready, lo_ready, ones_written = c.semaphores(
        "proj_in", ("chunk_done", "copied", "convolved", "v_copied_act", "v_copied_dve", "silu_done", "hi_ready", "lo_ready", "ones_written"))
    ends = [i + 1 == len(items) or chunk_of[i + 1] != chunk_of[i] for i in range(len(items))]
    ends = [e and chunk_of[i] % 2 == 1 for i, e in enumerate(ends)]
    CONV = 12

    def complete(eng, n):
        if ends[n]:
            eng.wait_ge(w.used, w.at + chunk_of[n] // 2 + 1)
        else:
            eng.wait_ge(chunk_done, sum(not e for e in ends[:n + 1]))

    def lat(n):
        return c.wide[n % 4][:, 0:T]

    def con(n):
        return c.wide[n % 4][:, T:TA]

    with nc.Block() as block:
        @block.sync
        def _(sp):
            w.feed(sp, U_IN)

        @block.gpsimd
        def _(pool):
            over(pool, U_IN, RING, lambda j, i: w.write_lo(pool, hi_ready, lo_ready, j, i))
            pool.wait_ge(w.used, w.at + U_IN)
            pool.memset(u.v1[:, :, :, DH:DH + 1], 1.0).then_inc(ones_written, 1)

        @block.tensor
        def _(pe):
            for n, (kind, m) in enumerate(items):
                q = chunk_of[n]
                if kind != "lf" and q % 2 == 0:
                    unit = w.parts(pe, lo_ready, 0, q // 2)
                if n >= 4:
                    pe.wait_ge(copied, n - 3)
                first = P // 2 if kind == "lf" else 0
                wide = P // 2 if kind in ("la", "li", "lf") else P
                parts = [(lat(n), slice(CTX, TA))] + ([(con(n), slice(0, CTX))] if kind not in ("mo", "lg") else [])
                for dst, toks in parts:
                    for k in range(DC):
                        b = (q % 2 * DC + k) * P + first
                        mm = product(pe, dst[0:wide, :], [part[:, b:b + wide] for part in unit], [part[k][:, toks] for part in h],
                                     k == 0, k == DC - 1)
                mm.then_inc(w.used if ends[n] else chunk_done, 1)
            pe.wait_ge(copied, len(items))
            for k in range(DC):
                if k % 4 == 0:
                    unit = w.parts(pe, lo_ready, 0, U_IN_COLUMNS + k // 4)
                for t in range(TAT):
                    mm = product(pe, c.bank[t][:, :], [part[k][:, t * P:(t + 1) * P] for part in h],
                                 [part[:, k % 4 * DM:(k % 4 + 1) * DM] for part in unit], k == 0, k == DC - 1)
                if k % 4 == 3:
                    mm.then_inc(w.used, 1)

        @block.scalar
        def _(act):
            def silu(m):
                act.wait_ge(convolved, CONV * (m + 1))
                act.activation(u.conv[:, m, :], u.conv[:, m, :], ACT.Silu).then_inc(silu_done, 1)

            w.write_hi(act, hi_ready, 0, 0)
            w.write_hi(act, hi_ready, 0, 1)
            for n, (kind, m) in enumerate(items):
                complete(act, n)
                if n >= 1 and ends[n - 1] and chunk_of[n] // 2 + 1 < U_IN:
                    w.write_hi(act, hi_ready, 0, chunk_of[n] // 2 + 1)
                if kind == "conv":
                    grid, seq = pads[m % 2]
                    if m >= 2:
                        act.wait_ge(convolved, CONV * (m - 1))
                    act.copy(seq[:, 1:CTX + 1], con(n))
                    act.copy(grid[:, 1:ROWS + 1, 1:GRID_W + 1], lat(n).rearrange("p (r x) -> p r x", x=GRID_W)).then_inc(copied, 1)
                    if 3 <= m < 3 + 2 * MC:
                        silu(m - 3)
                elif kind == "lw":
                    act.activation(u.lw[:, CTX:TA], lat(n), ACT.Tanh)
                    act.activation(u.lw[:, 0:CTX], con(n), ACT.Tanh).then_inc(copied, 1)
                elif kind == "la":
                    act.copy(u.la[:, CTX:TA], lat(n)[0:64, :])
                    act.copy(u.la[:, 0:CTX], con(n)[0:64, :]).then_inc(copied, 1)
                elif kind == "lg":
                    act.activation(u.lg[:, :], lat(n), ACT.Sigmoid).then_inc(copied, 1)
                elif kind in ("li", "lf"):
                    dst, b = (u.li, u.bias[0:64, 0:1]) if kind == "li" else (u.lf, u.bias[0:64, 1:2])
                    act.activation(dst[:, CTX:TA], lat(n)[0:64, :], ACT.Identity, bias=b)
                    act.activation(dst[:, 0:CTX], con(n)[0:64, :], ACT.Identity, bias=b).then_inc(copied, 1)
                else:
                    act.activation(u.mo[:, m, :], lat(n), ACT.Sigmoid).then_inc(copied, 1)
            w.write_hi(act, hi_ready, 0, U_IN - 1)
            act.wait_ge(w.used, w.at + U_IN)
            for t in range(3):
                act.copy(u.v1[:, t, :, 0:DH], c.bank[t].rearrange("p (h e) -> p h e", e=DH)).then_inc(v_copied_act, 1)

        @block.vector
        def _(dve):
            for m in range(CONV_CHUNKS):
                grid, seq = pads[m % 2]
                dve.wait_ge(copied, m + 1)
                at = CONV * m
                go = u.conv[:, m, CTX:TA].rearrange("p (r x) -> p r x", x=GRID_W)
                so = u.conv[:, m, 0:CTX]

                def weight(dy, dx):
                    col = COLS["conv"] + (3 * dy + dx) * CONV_CHUNKS + m
                    return c.cols[:, col:col + 1]

                def shifted(dy, dx):
                    return grid[:, dy:dy + ROWS, dx:dx + GRID_W]

                dve.tensor_scalar(go, shifted(0, 0), weight(0, 0), None, ALU.mult).then_inc(convolved, 1)
                dve.tensor_scalar(so, seq[:, 0:CTX], weight(1, 0), None, ALU.mult).then_inc(convolved, 1)
                step = 2
                for tap in range(1, 9):
                    dy, dx = tap // 3, tap % 3
                    dve.wait_ge(convolved, at + step - (1 if tap <= 3 else 0))
                    dve.scalar_tensor_tensor(out=go, in0=shifted(dy, dx), scalar=weight(dy, dx), in1=go,
                                             op0=ALU.mult, op1=ALU.add).then_inc(convolved, 1)
                    step += 1
                    if tap <= 2:
                        dve.wait_ge(convolved, at + step - 1)
                        dve.scalar_tensor_tensor(out=so, in0=seq[:, tap:tap + CTX], scalar=weight(1, tap), in1=so,
                                                 op0=ALU.mult, op1=ALU.add).then_inc(convolved, 1)
                        step += 1
                assert step == CONV
            dve.wait_ge(w.used, w.at + U_IN)
            for t in range(3, TAT):
                dve.tensor_copy(u.v1[:, t, :, 0:DH], c.bank[t].rearrange("p (h e) -> p h e", e=DH)).then_inc(v_copied_dve, 1)
    w.at += U_IN



ORDER = ([0, 1, 2, 3, 4, 5], [1, 0, 5, 4, 3, 2])
SIDE = (0, 32)
GR = 40


def chain_of(eng, sem):
    count = [0]

    def step(ins, wait=True):
        ins.then_inc(sem, 1)
        count[0] += 1
        if wait:
            eng.wait_ge(sem, count[0])
        return count[0]
    return step


def gates_stage(nc, c, u, g):
    dve_step, neg_ready, exp_ready, ln_ready, pre_ready, post_ready, turned, cols_copied, spread, spread_copied = c.semaphores(
        "gates", ("dve_step", "neg_ready", "exp_ready", "ln_ready", "pre_ready", "post_ready", "turned", "cols_copied",
                  "spread", "spread_copied"))
    R = slice(0, GR)

    def tiles(x):
        return x[R, :].rearrange("p (j t) -> p j t", t=P)

    with ExitStack() as ctx:
        def sb(n, shape):
            return ctx.enter_context(nc.sbuf_tensor(f"gates_{n}", shape, F32))
        low, arg, m, b = (g.temps[:, n, :] for n in range(4))
        small, reset = sb("small", [GR, 2, TAT]), g.reset
        with nc.Block() as block:
            @block.vector
            def _(dve):
                step = chain_of(dve, dve_step)
                step(dve.memset(reset[:, :], 1.0))
                step(dve.memset(reset[0:32, 0:TA:P], 0.0))
                step(dve.memset(reset[32:GR, P - 1:TA:P], 0.0))
                step(dve.tensor_scalar(low[:, :], u.lf[R, :], 0.0, None, ALU.min))
                dve.scalar_tensor_tensor(out=arg[:, :], in0=low[:, :], scalar=2.0, in1=u.lf[R, :], op0=ALU.mult,
                                         op1=ALU.subtract).then_inc(neg_ready, 1)
                dve.wait_ge(ln_ready, 1)
                step(dve.tensor_tensor(low[:, :], low[:, :], arg[:, :], ALU.subtract))
                for side, rev in ((slice(0, 32), False), (slice(32, GR), True)):
                    if not rev:
                        step(dve.tensor_tensor_scan(m[side, :], low[side, :], u.li[side, :], 0.0, ALU.add, ALU.max))
                        step(dve.tensor_tensor_scan(b[side, :], reset[side, :], low[side, :], 0.0, ALU.mult, ALU.add))
                    else:
                        for lo, hi, init in ((0, CTX, 0.0), (CTX, TA, m[side, 0:1])):
                            def back(x):
                                return x[side, lo:hi][:, ::-1]
                            step(dve.tensor_tensor_scan(back(m), back(low), back(u.li), init, ALU.add, ALU.max))
                            step(dve.tensor_tensor_scan(back(b), back(reset), back(low), 0.0, ALU.mult, ALU.add))
                step(dve.tensor_tensor(g.bm[:, :], b[:, :], m[:, :], ALU.subtract))
                step(dve.tensor_tensor(g.rows[:, 0, :], u.li[R, :], b[:, :], ALU.subtract))
                step(dve.memset(small[:, :, :], 0.0))
                for d in range(2):
                    side = slice(SIDE[d], SIDE[d] + 8)
                    end = 0 if d else P - 1
                    step(dve.tensor_copy(small[side, 1, :], g.bm[side, end:TA:P]))
                    for before, tile in zip(ORDER[d], ORDER[d][1:]):
                        at = before * P + end
                        step(dve.tensor_copy(small[side, 0, tile:tile + 1], m[side, at:at + 1]))
                step(dve.tensor_tensor(tiles(g.inter), tiles(g.bm), small[:, 0, :].unsqueeze(2).broadcast_to([GR, TAT, P]), ALU.add))
                step(dve.tensor_tensor(g.rows[:, 1, :].rearrange("p (j t) -> p j t", t=P),
                                       g.rows[:, 0, :].rearrange("p (j t) -> p j t", t=P),
                                       small[:, 1, :].unsqueeze(2).broadcast_to([GR, TAT, P]), ALU.add))
                dve.tensor_scalar(g.rows[:, 2, :], m[:, :], -1.0, None, ALU.mult).then_inc(pre_ready, 1)
                dve.wait_ge(turned, 3 * TAT)
                dve.tensor_copy(g.cols[:, 0:9, :], c.bank[0][:, 0:9 * GR].rearrange("p (n r) -> p n r", r=GR)).then_inc(cols_copied, 1)
                dve.tensor_copy(g.cols[:, 9:18, :], c.bank[1][:, 0:9 * GR].rearrange("p (n r) -> p n r", r=GR)).then_inc(cols_copied, 1)
                for d in range(2):
                    for mm in range(MC):
                        n = d * MC + mm
                        dve.wait_ge(spread, n + 1)
                        dve.scalar_tensor_tensor(out=g.qi[:, d, mm, :], in0=u.conv[:, mm, CTX:TA], scalar=DH ** -0.5,
                                                 in1=c.wide[2 + n % 2][:, 0:T], op0=ALU.mult, op1=ALU.mult)
                        dve.tensor_copy(g.decay[:, d, mm, :], c.wide[2 + n % 2][:, T:T + TAT]).then_inc(spread_copied, 1)

            @block.scalar
            def _(act):
                act.wait_ge(neg_ready, 1)
                act.activation(arg[:, :], arg[:, :], ACT.Exp).then_inc(exp_ready, 1)
                act.wait_ge(exp_ready, 1)
                act.activation(arg[:, :], arg[:, :], ACT.Ln, bias=1.0).then_inc(ln_ready, 1)
                act.wait_ge(pre_ready, 1)
                act.activation(g.inter[:, :], g.inter[:, :], ACT.Exp).then_inc(post_ready, 1)
                act.activation(g.rows[:, 1:3, :], g.rows[:, 1:3, :], ACT.Exp).then_inc(post_ready, 1)

            @block.tensor
            def _(pe):
                pe.wait_ge(post_ready, 2)
                pe.wait_ge(pre_ready, 1)
                for n in range(3 * TAT):
                    a, t = n // TAT, n % TAT
                    pe.matmul(c.bank[n // 9][:, n % 9 * GR:(n % 9 + 1) * GR], g.rows[:, a, t * P:(t + 1) * P],
                              c.ident[0:GR, 0:GR], start=True, stop=True).then_inc(turned, 1)
                for d in range(2):
                    for mm in range(MC):
                        n = d * MC + mm
                        if n >= 2:
                            pe.wait_ge(spread_copied, n - 1)
                        pe.matmul(c.wide[2 + n % 2][:, 0:T], u.pair[:, n, :], g.inter[:, CTX:TA], start=True, stop=True)
                        end = 0 if d else P - 1
                        pe.matmul(c.wide[2 + n % 2][:, T:T + TAT], u.pair[:, n, :], g.inter[:, end:TA:P],
                                  start=True, stop=True).then_inc(spread, 1)


def mlstm_stage(nc, c, u, g, hsum):
    with ExitStack() as ctx:
        def sb(n, shape):
            return ctx.enter_context(nc.sbuf_tensor(f"ml_{n}", shape, F32))
        ktm, kw, expo = g.ktm, g.kw, g.expo
        sc, hout = g.sc, g.hout
        state = sb("state", [P, 2, MC, DH + 1])
        small = sb("small", [P, 3, 2, 4])
        (k_turned, k_copied, kw_ready, gain_done, state_step, bm_spread, masked, exp_ready, qk_done, sc_ready, out_done,
         den_step, h_ready, h_added) = c.semaphores("ml", (
             "k_turned", "k_copied", "kw_ready", "gain_done", "state_step", "bm_spread", "masked", "exp_ready", "qk_done",
             "sc_ready", "out_done", "den_step", "h_ready", "h_added"))
        steps = [(d, p, ORDER[d][p]) for p in range(TAT) for d in range(2)]
        groups = [(n, d, t, q) for n, (d, p, t) in enumerate(steps) if t >= 2 for q in range(2)]
        first_of = {}
        for i, (n, *_ ) in enumerate(groups):
            first_of.setdefault(n, i)
        BM, QK, OUT, GAIN = c.bank[0:2], c.bank[2:4], c.bank[4:6], c.bank[6:8]
        with nc.Block() as block:
            @block.tensor
            def _(pe):
                for t in range(TAT):
                    if t >= 2:
                        pe.wait_ge(k_copied, t - 1)
                    for m in range(MC):
                        mm = pe.matmul(c.bank[t % 2][:, m * P:(m + 1) * P], u.conv[:, MC + m, t * P:(t + 1) * P], c.ident[:, :],
                                       start=True, stop=True)
                    mm.then_inc(k_turned, 1)
                pe.wait_ge(k_copied, TAT)
                for n, (d, p, t) in enumerate(steps):
                    if t >= 2:
                        for q in range(2):
                            i = first_of[n] + q
                            if i >= 2:
                                pe.wait_ge(masked, 4 * (i - 1))
                                pe.wait_ge(sc_ready, i - 1)
                            for e in range(4):
                                mm = pe.matmul(BM[i % 2][:, e * P:(e + 1) * P], c.ident[0:GR, SIDE[d] + 2 * e + q:SIDE[d] + 2 * e + q + 1].broadcast_to([GR, P]),
                                               g.bm[:, t * P:(t + 1) * P], start=True, stop=True)
                            mm.then_inc(bm_spread, 1)
                            for e in range(4):
                                head = 2 * e + q
                                rows = slice(head % 2 * DH, head % 2 * DH + DH)
                                mm = pe.matmul(QK[i % 2][:, e * P:(e + 1) * P], u.conv[rows, MC + head // 2, t * P:(t + 1) * P],
                                               u.conv[rows, head // 2, t * P:(t + 1) * P], start=True, stop=True)
                            mm.then_inc(qk_done, 1)
                        for q in range(2):
                            i = first_of[n] + q
                            pe.wait_ge(sc_ready, i + 1)
                            pe.wait_ge(state_step, 2 * n)
                            if i >= 2:
                                pe.wait_ge(h_ready, i - 1)
                            for e in range(4):
                                head = 2 * e + q
                                rows = slice(head % 2 * DH, head % 2 * DH + DH)
                                dst = OUT[i % 2][:, e * (DH + 1):(e + 1) * (DH + 1)]
                                pe.matmul(dst, sc[:, i % 2, e, :], u.v1[:, t, head, :], start=True, stop=False)
                                lt = (t - 2) * P
                                mm = pe.matmul(dst, g.qi[rows, d, head // 2, lt:lt + P], state[rows, d, head // 2, :],
                                               start=False, stop=True)
                            mm.then_inc(out_done, 1)
                    if p < TAT - 1:
                        pe.wait_ge(kw_ready, n + 1)
                        if n >= 2:
                            pe.wait_ge(state_step, 2 * n)
                        for head in range(NH):
                            rows = slice(head % 2 * DH, head % 2 * DH + DH)
                            m = head // 2
                            mm = pe.matmul(GAIN[n % 2][rows, m * (DH + 1):(m + 1) * (DH + 1)], kw[:, n % 2, head * DH:(head + 1) * DH],
                                           u.v1[:, t, head, :], start=True, stop=True)
                        mm.then_inc(gain_done, 1)

            @block.scalar
            def _(act):
                for t in range(TAT):
                    act.wait_ge(k_turned, t + 1)
                    act.copy(ktm[:, t, :], c.bank[t % 2][:, :]).then_inc(k_copied, 1)
                for i, (n, d, t, q) in enumerate(groups):
                    act.wait_ge(masked, 4 * (i + 1))
                    act.activation(expo[:, i % 2, :, :], expo[:, i % 2, :, :], ACT.Exp).then_inc(exp_ready, 1)

            @block.vector
            def _(dve):
                dve.memset(state[:, :, :, :], 0.0).then_inc(state_step, 1)
                dve.memset(hsum[:, :, :], 0.0).then_inc(state_step, 1)
                dve.wait_ge(state_step, 2)

                for n, (d, p, t) in enumerate(steps):
                    if p < TAT - 1:
                        dve.wait_ge(k_copied, TAT)
                        if n >= 2:
                            dve.wait_ge(gain_done, n - 1)
                        wts = g.cols[:, TAT + t, SIDE[d]:SIDE[d] + 8]
                        dve.tensor_tensor(kw[:, n % 2, :].rearrange("p (h e) -> p h e", e=DH),
                                          ktm[:, t, :].rearrange("p (h e) -> p h e", e=DH),
                                          wts.unsqueeze(2).broadcast_to([P, NH, DH]), ALU.mult).then_inc(kw_ready, 1)
                    if t >= 2:
                        for q in range(2):
                            i = first_of[n] + q
                            if i >= 2:
                                dve.wait_ge(sc_ready, i - 1)
                            dve.wait_ge(bm_spread, i + 1)
                            for e in range(4):
                                row = SIDE[d] + 2 * e + q
                                dve.scalar_tensor_tensor(out=expo[:, i % 2, e, :], in0=BM[i % 2][:, e * P:(e + 1) * P],
                                                         scalar=g.cols[:, t, row:row + 1], in1=u.never[:, d, :], op0=ALU.add,
                                                         op1=ALU.add).then_inc(masked, 1)
                        for q in range(2):
                            i = first_of[n] + q
                            dve.wait_ge(exp_ready, i + 1)
                            dve.wait_ge(qk_done, i + 1)
                            if i >= 2:
                                dve.wait_ge(out_done, i - 1)
                            dve.scalar_tensor_tensor(out=sc[:, i % 2, :, :].rearrange("p e t -> p (e t)"),
                                                     in0=QK[i % 2], scalar=DH ** -0.5,
                                                     in1=expo[:, i % 2, :, :].rearrange("p e t -> p (e t)"),
                                                     op0=ALU.mult, op1=ALU.mult).then_inc(sc_ready, 1)
                        for q in range(2):
                            i = first_of[n] + q
                            o = OUT[i % 2][:, 0:4 * (DH + 1)].rearrange("p (h e) -> p h e", e=DH + 1)
                            rows = slice(SIDE[d] + q, SIDE[d] + NH, 2)
                            dve.wait_ge(out_done, i + 1)
                            dve.tensor_tensor(small[:, 0, i % 2, :], o[:, :, DH], g.cols[:, 2 * TAT + t, rows], ALU.max).then_inc(den_step, 1)
                            dve.wait_ge(den_step, 3 * i + 1)
                            dve.scalar_tensor_tensor(out=small[:, 1, i % 2, :], in0=o[:, :, DH], scalar=-1.0,
                                                     in1=small[:, 0, i % 2, :], op0=ALU.mult, op1=ALU.max).then_inc(den_step, 1)
                            dve.wait_ge(den_step, 3 * i + 2)
                            dve.reciprocal(small[:, 2, i % 2, :], small[:, 1, i % 2, :]).then_inc(den_step, 1)
                            dve.wait_ge(den_step, 3 * i + 3)
                            dve.tensor_tensor(hout[:, i % 2, :, :], o[:, :, 0:DH],
                                              small[:, 2, i % 2, :].unsqueeze(2).broadcast_to([P, 4, DH]),
                                              ALU.mult).then_inc(h_ready, 1)
                            dve.wait_ge(h_ready, i + 1)
                            hs = hsum[:, t - 2, :].rearrange("p (m a e) -> p a m e", a=2, e=DH)[:, q, :, :]
                            dve.tensor_tensor(hs, hs, hout[:, i % 2, :, :], ALU.add).then_inc(h_added, 1)
                            dve.wait_ge(h_added, i + 1)
                    if p < TAT - 1:
                        dve.wait_ge(gain_done, n + 1)
                        dve.tensor_tensor(state[:, d, :, :], state[:, d, :, :],
                                          g.decay[:, d, :, t:t + 1].broadcast_to([P, MC, DH + 1]), ALU.mult).then_inc(state_step, 1)
                        dve.wait_ge(state_step, 2 * n + 3)
                        dve.tensor_tensor(state[:, d, :, :], state[:, d, :, :],
                                          GAIN[n % 2][:, 0:MC * (DH + 1)].rearrange("p (m e) -> p m e", e=DH + 1),
                                          ALU.add).then_inc(state_step, 1)



LEVELS = 7


def rwkv_common_stage(nc, c, u, r, lowrank):
    with ExitStack() as ctx:
        def sb(n, shape):
            return ctx.enter_context(nc.sbuf_tensor(f"rc_{n}", shape, F32))
        grown, kap, sq, t1, rk = sb("grown", [P, TA]), sb("kap", [P, TA]), sb("sq", [P, TA]), sb("t1", [P, TA]), sb("rk", [P, 3, T])
        one_ka = sb("one_ka", [P, MC])
        (dve_step, a_done, a_ready, kap_ready, sq_ready, sum_done, safe_ready, root_ready, g_done, g_ready, bonus_ready,
         bonus_done, turned, v_copied, m_done) = c.semaphores("rc", (
             "dve_step", "a_done", "a_ready", "kap_ready", "sq_ready", "sum_done", "safe_ready", "root_ready", "g_done",
             "g_ready", "bonus_ready", "bonus_done", "turned", "v_copied", "m_done"))
        col = lambda name, m: c.cols[:, COLS[name] + m:COLS[name] + m + 1]
        with nc.Block() as block:
            @block.tensor
            def _(pe):
                for m in range(MC):
                    ms = slice(m * P, (m + 1) * P)
                    if m >= 1:
                        pe.wait_ge(m_done, m)
                        pe.wait_ge(a_ready, m)
                        pe.wait_ge(g_ready, m)
                    pe.matmul(c.wide[0][:, 0:T], lowrank[0:64, 1, ms], u.la[:, CTX:TA], start=True, stop=True)
                    pe.matmul(c.wide[0][:, T:TA], lowrank[0:64, 1, ms], u.la[:, 0:CTX], start=True, stop=True).then_inc(a_done, 1)
                    pe.matmul(c.bank[4][:, :], lowrank[:, 2, ms], u.lg[:, :], start=True, stop=True).then_inc(g_done, 1)
                    pe.wait_ge(sq_ready, m + 1)
                    pe.matmul(c.wide[1][:, 0:T], c.same[:, :], sq[:, CTX:TA], start=True, stop=True)
                    pe.matmul(c.wide[1][:, T:TA], c.same[:, :], sq[:, 0:CTX], start=True, stop=True).then_inc(sum_done, 1)
                    pe.wait_ge(bonus_ready, m + 1)
                    pe.matmul(c.bank[5][:, :], c.same[:, :], rk[:, 2, :], start=True, stop=True).then_inc(bonus_done, 1)
                for t in range(TAT):
                    if t >= 2:
                        pe.wait_ge(v_copied, t - 1)
                    for m in range(MC):
                        mm = pe.matmul(c.bank[6 + t % 2][:, m * P:(m + 1) * P], u.conv[:, 4 * MC + m, t * P:(t + 1) * P],
                                       c.ident[:, :], start=True, stop=True)
                    mm.then_inc(turned, 1)

            @block.scalar
            def _(act):
                for m in range(MC):
                    act.wait_ge(a_done, m + 1)
                    if m >= 1:
                        act.wait_ge(m_done, m)
                    act.activation(r.a[:, m, CTX:TA], c.wide[0][:, 0:T], ACT.Sigmoid, bias=col("r_a0", m))
                    act.activation(r.a[:, m, 0:CTX], c.wide[0][:, T:TA], ACT.Sigmoid, bias=col("r_a0", m)).then_inc(a_ready, 1)
                    act.wait_ge(g_done, m + 1)
                    act.copy(r.g[:, m, :], c.bank[4][:, :]).then_inc(g_ready, 1)
                    act.wait_ge(kap_ready, m + 1)
                    act.activation(sq[:, :], kap[:, :], ACT.Square).then_inc(sq_ready, 1)
                    act.wait_ge(safe_ready, m + 1)
                    act.activation(t1[:, :], t1[:, :], ACT.Sqrt).then_inc(root_ready, 1)
                for t in range(TAT):
                    act.wait_ge(turned, t + 1)
                    act.copy(r.vtm[:, t, :], c.bank[6 + t % 2][:, :]).then_inc(v_copied, 1)

            @block.vector
            def _(dve):
                step = chain_of(dve, dve_step)
                step(dve.tensor_scalar(one_ka[:, :], c.cols[:, COLS["r_ka"]:COLS["r_ka"] + MC], -1.0, 1.0, ALU.mult, ALU.add))
                for m in range(MC):
                    rr, rkk, rv = u.conv[:, 2 * MC + m, :], u.conv[:, 3 * MC + m, :], u.conv[:, 4 * MC + m, :]
                    dve.tensor_scalar(kap[:, :], rkk, col("r_kk", m), None, ALU.mult).then_inc(kap_ready, 1)
                    dve.wait_ge(a_ready, m + 1)
                    step(dve.tensor_scalar(grown[:, :], r.a[:, m, :], col("r_ka", m), one_ka[:, m:m + 1], ALU.mult, ALU.add))
                    step(dve.tensor_tensor(r.kmod[:, m, :], grown[:, :], rkk, ALU.mult))
                    step(dve.tensor_tensor(rk[:, 0, :], rr[:, CTX:TA], r.kmod[:, m, CTX:TA], ALU.mult))
                    dve.tensor_scalar(rk[:, 2, :], rk[:, 0, :], col("r_bonus", m), None, ALU.mult).then_inc(bonus_ready, 1)
                    dve.wait_ge(sum_done, m + 1)
                    step(dve.tensor_scalar(t1[:, CTX:TA], c.wide[1][:, 0:T], 1e-24, None, ALU.max))
                    dve.tensor_scalar(t1[:, 0:CTX], c.wide[1][:, T:TA], 1e-24, None, ALU.max).then_inc(safe_ready, 1)
                    dve.wait_ge(root_ready, m + 1)
                    step(dve.reciprocal(t1[:, :], t1[:, :]))
                    step(dve.tensor_tensor(r.kh[:, m, :], kap[:, :], t1[:, :], ALU.mult))
                    step(dve.scalar_tensor_tensor(out=r.a[:, m, :], in0=r.a[:, m, :], scalar=-1.0, in1=r.kh[:, m, :],
                                                  op0=ALU.mult, op1=ALU.mult))
                    dve.wait_ge(bonus_done, m + 1)
                    dve.tensor_tensor(r.bonus[:, m, :], c.bank[5][:, :], rv[:, CTX:TA], ALU.mult).then_inc(m_done, 1)


def rwkv_factors_stage(nc, c, u, r, f, lowrank, d):
    mid = 64 if d else 63
    end = 0 if d else P - 1
    with ExitStack() as ctx:
        def sb(n, shape):
            return ctx.enter_context(nc.sbuf_tensor(f"rf{d}_{n}", shape, F32))
        sg, cum = r.room, sb("cum", [P, 2, TA])
        e = u.conv[:, 4 * MC:4 * MC + 3, :]
        out = sb("out", [P, 2, TAT, 4, P])
        reset = u.conv[:, 4 * MC + 3, :]
        mids, last = sb("mids", [P, MC, TAT]), sb("last", [P, MC, TAT])
        dve_step, z_done, sg_ready, s_ready, exp_ready, m_done, edge_ready, gain_ready, stored = c.semaphores(f"rf{d}", (
            "dve_step", "z_done", "sg_ready", "s_ready", "exp_ready", "m_done", "edge_ready", "gain_ready", "stored"))
        rows = slice(64 * d, 64 * d + 64)

        def tiles(x):
            return x.rearrange("p (j t) -> p j t", t=P)
        with nc.Block() as block:
            @block.sync
            def _(sp):
                for m in range(MC):
                    sp.wait_ge(m_done, m + 1)
                    sp.dma_start(f.scratch[d, :, :, m].rearrange("t p a x -> p t a x"), out[:, m % 2, :, :, :]).then_inc(stored, 16)
                    sp.wait_ge(stored, 16 * (m + 1))

            @block.tensor
            def _(pe):
                for m in range(MC):
                    if m >= 2:
                        pe.wait_ge(sg_ready, m - 1)
                    z = c.wide[m % 2]
                    pe.matmul(z[:, 0:T], lowrank[rows, 0, m * P:(m + 1) * P], u.lw[rows, CTX:TA], start=True, stop=True)
                    pe.matmul(z[:, T:TA], lowrank[rows, 0, m * P:(m + 1) * P], u.lw[rows, 0:CTX], start=True, stop=True).then_inc(z_done, 1)

            @block.scalar
            def _(act):
                def sigmoid(m):
                    b = c.cols[:, COLS["r_w0"] + d * MC + m:COLS["r_w0"] + d * MC + m + 1]
                    act.wait_ge(z_done, m + 1)
                    if m >= 2:
                        act.wait_ge(m_done, m - 1)
                    act.activation(sg[:, m % 2, CTX:TA], c.wide[m % 2][:, 0:T], ACT.Sigmoid, bias=b)
                    act.activation(sg[:, m % 2, 0:CTX], c.wide[m % 2][:, T:TA], ACT.Sigmoid, bias=b).then_inc(sg_ready, 1)

                sigmoid(0)
                sigmoid(1)
                for m in range(MC):
                    act.wait_ge(s_ready, m + 1)
                    if m >= 1:
                        act.wait_ge(m_done, m)
                    act.activation(e[:, 0, :], sg[:, m % 2, :], ACT.Exp, scale=DECAY)
                    act.activation(e[:, 1, :], cum[:, m % 2, :], ACT.Exp, scale=-DECAY)
                    act.activation(e[:, 2, :], cum[:, m % 2, :], ACT.Exp, scale=DECAY).then_inc(exp_ready, 1)
                    if m + 2 < MC:
                        act.wait_ge(m_done, m + 1)
                        sigmoid(m + 2)
                act.wait_ge(edge_ready, 1)
                act.activation(f.gain[:, d, :, :], f.gain[:, d, :, :], ACT.Exp, scale=-DECAY).then_inc(gain_ready, 1)

            @block.vector
            def _(dve):
                step = chain_of(dve, dve_step)
                step(dve.memset(reset[:, :], 1.0))
                first = P - 1 if d else 0
                step(dve.memset(reset[:, first:TA:P], 0.0))
                for m in range(MC):
                    s_, q = sg[:, m % 2, :], cum[:, m % 2, :]
                    dve.wait_ge(sg_ready, m + 1)
                    if d == 0:
                        step(dve.tensor_tensor_scan(q, reset[:, :], s_, 0.0, ALU.mult, ALU.add))
                    else:
                        step(dve.tensor_tensor_scan(q[:, ::-1], reset[:, ::-1], s_[:, ::-1], 0.0, ALU.mult, ALU.add))
                    step(dve.tensor_copy(mids[:, m, :], q[:, mid:TA:P]))
                    step(dve.tensor_copy(last[:, m, :], q[:, end:TA:P]))
                    dve.tensor_tensor(tiles(q), tiles(q), mids[:, m, :].unsqueeze(2).broadcast_to([P, TAT, P]), ALU.subtract).then_inc(s_ready, 1)
                    dve.wait_ge(exp_ready, m + 1)
                    step(dve.tensor_tensor(e[:, 0, :], e[:, 0, :], e[:, 1, :], ALU.mult))
                    if m >= 2:
                        dve.wait_ge(stored, 16 * (m - 1))
                    dve.tensor_tensor(out[:, m % 2, :, 0, :], tiles(r.kh[:, m, :]), tiles(e[:, 0, :]), ALU.mult)
                    dve.tensor_tensor(out[:, m % 2, :, 1, :], tiles(u.conv[:, 2 * MC + m, :]), tiles(e[:, 1, :]), ALU.mult)
                    dve.tensor_tensor(out[:, m % 2, :, 2, :], tiles(r.a[:, m, :]), tiles(e[:, 2, :]), ALU.mult)
                    dve.tensor_tensor(out[:, m % 2, :, 3, :], tiles(r.kmod[:, m, :]), tiles(e[:, 2, :]), ALU.mult).then_inc(m_done, 1)
                step(dve.tensor_tensor(f.gain[:, d, :, :], last[:, :, :], mids[:, :, :], ALU.subtract))
                for now, then in zip(ORDER[d], ORDER[d][1:]):
                    step(dve.tensor_tensor(f.gain[:, d, :, now:now + 1], f.gain[:, d, :, now:now + 1], mids[:, :, then:then + 1], ALU.add))
                dve.tensor_copy(last[:, 0, 0:1], mids[:, 0, 0:1]).then_inc(edge_ready, 1)


def rwkv_stage(nc, c, r, f, masks, ysum, d):
    with ExitStack() as ctx:
        def sb(n, shape, dt=F32):
            return ctx.enter_context(nc.sbuf_tensor(f"rw{d}_{n}", shape, dt))
        G = sb("G", [P, 2, NH, 4 * P])
        X = sb("X", [P, NH, P])
        XT = sb("XT", [P, 2, NH, P])
        Q = sb("Q", [P, NH, P])
        tm = sb("tm", [P, 2, 2, DM])
        F = sb("F", [P, 2, MC, 4, P])
        base = sb("base", [P, NH, DH])
        U = sb("U", [P, NH, DH])
        S = sb("S", [P, MC, DH])
        S2 = sb("S2", [P, MC, DH])
        (pair_done, pair_masked, au_done, x0_ready, tm_done, tm_copied, q_done, q_ready, x_done, xt_done, x_ready, base_done, base_ready,
         u_done, u_ready, y_done, y_added, gain_done, state_step, x_step, loaded0, loaded1) = c.semaphores(f"rw{d}", (
             "pair_done", "pair_masked", "au_done", "x0_ready", "tm_done", "tm_copied", "q_done", "q_ready", "x_done", "xt_done",
             "x_ready", "base_done", "base_ready", "u_done", "u_ready", "y_done", "y_added", "gain_done", "state_step", "x_step", "loaded0", "loaded1"))
        order = ORDER[d]
        loaded = (loaded0, loaded1)
        QB, XB, XTB = [c.bank[0], c.bank[3]], [c.bank[1], c.bank[4]], [c.bank[2], c.bank[5]]
        side = [c.bank[6], c.bank[7]]
        pair_mask, first_u, first_t = masks.pair[:, d, :], masks.first[:, d, :], masks.first[:, 1 - d, :]
        level, level_t = masks.level[:, d, :, :], masks.level[:, 1 - d, :, :]

        def heads(g):
            return range(g, NH, 2)

        def place(h):
            return h % 2 * 4 + h // 2

        def rows_of(head):
            return slice(head % 2 * DH, head % 2 * DH + DH)

        with nc.Block() as block:
            @block.sync
            def _(sp):
                for p, t in enumerate(order):
                    if p >= 2:
                        sp.wait_ge(state_step, 3 * (p - 2) + 4)
                    sp.dma_start(F[:, p % 2, :, :, :], f.scratch[d, t]).then_inc(loaded[p % 2], 16)

            @block.tensor
            def _(pe):
                def pairs(p):
                    t = order[p]
                    pe.wait_ge(loaded[p % 2], 16 * (p // 2 + 1))
                    for h in range(NH):
                        rows, m = rows_of(h), h // 2
                        if p * NH + h >= 2:
                            pe.wait_ge(pair_masked, p * NH + h - 1)
                        if p >= 2 and h < 2:
                            pe.wait_ge(state_step, 3 * (p - 2) + 4)
                            if p > 3:
                                pe.wait_ge(y_added, 2 * (p - 3))
                        dst = side[h % 2]
                        ar, b, k = F[rows, p % 2, m, 0:2, :].rearrange("p a t -> p (a t)"), F[rows, p % 2, m, 2, :], F[rows, p % 2, m, 3, :]
                        pe.matmul(dst[:, 0:2 * P], b, ar, start=True, stop=True)
                        pe.matmul(dst[:, 2 * P:4 * P], k, ar, start=True, stop=True).then_inc(pair_done, 1)
                    for g in range(2):
                        if p >= 1:
                            pe.wait_ge(x_ready, 2 * (LEVELS - 1) * p)
                        for e, h in enumerate(heads(g)):
                            rows, m = rows_of(h), h // 2
                            mm = pe.matmul(QB[g][:, e * P:(e + 1) * P], F[rows, p % 2, m, 0, :], F[rows, p % 2, m, 2, :], start=True, stop=True)
                        mm.then_inc(au_done, 1)
                    for a in range(2):
                        pe.wait_ge(pair_masked, (p + 1) * NH - 1 + a)
                        for m in range(MC):
                            mm = pe.transpose(side[a][:, m * P:(m + 1) * P], F[:, p % 2, m, 2 + a, :], c.ident[:, :])
                        mm.then_inc(tm_done, 1)

                def level_step(p, k):
                    for g in range(2):
                        n = 2 * (LEVELS - 1) * p + 2 * (k - 1) + g
                        if k == 1:
                            pe.wait_ge(x0_ready, 2 * p + g + 1)
                        else:
                            pe.wait_ge(x_ready, n - 1)
                        for e, h in enumerate(heads(g)):
                            mm = pe.matmul(QB[g][:, e * P:(e + 1) * P], G[:, p % 2, place(h), 0:P], X[:, place(h), :], start=True, stop=True)
                        mm.then_inc(q_done, 1)
                    for g in range(2):
                        n = 2 * (LEVELS - 1) * p + 2 * (k - 1) + g
                        pe.wait_ge(q_ready, n + 1)
                        for e, h in enumerate(heads(g)):
                            mm = pe.matmul(XTB[g][:, e * P:(e + 1) * P], Q[:, place(h), :], XT[:, p % 2, place(h), :], start=True, stop=True)
                        mm.then_inc(xt_done, 1)
                        if k < LEVELS - 1:
                            for e, h in enumerate(heads(g)):
                                mm = pe.matmul(XB[g][:, e * P:(e + 1) * P], XT[:, p % 2, place(h), :], Q[:, place(h), :], start=True, stop=True)
                            mm.then_inc(x_done, 1)

                def chain(p, part):
                    t = order[p]
                    if part == 0:
                        pe.wait_ge(tm_copied, 2 * min(p + 2, TAT))
                        pe.wait_ge(state_step, 3 * p + 1)
                        for h in range(NH):
                            rows, m = rows_of(h), h // 2
                            dst = side[h % 2][:, m * DH:(m + 1) * DH]
                            pe.matmul(dst, F[rows, p % 2, m, 0, :], S[rows, m, :], start=True, stop=False)
                            mm = pe.matmul(dst, G[:, p % 2, place(h), 2 * P:3 * P], r.vtm[:, t, h * DH:(h + 1) * DH], start=False, stop=True)
                        mm.then_inc(base_done, 1)
                    elif part == 1:
                        pe.wait_ge(base_ready, 2 * p + 2)
                        pe.wait_ge(x_ready, 2 * (LEVELS - 1) * (p + 1))
                        for h in range(NH):
                            mm = pe.matmul(side[h % 2][:, h // 2 * DH:(h // 2 + 1) * DH], XT[:, p % 2, place(h), :], base[:, place(h), :], start=True, stop=True)
                        mm.then_inc(u_done, 1)
                    else:
                        pe.wait_ge(u_ready, 2 * p + 2)
                        if t >= 2:
                            for h in range(NH):
                                rows, m, hs = rows_of(h), h // 2, slice(h * DH, (h + 1) * DH)
                                dst = side[h % 2][:, m * DH:(m + 1) * DH]
                                pe.matmul(dst, F[rows, p % 2, m, 1, :], S[rows, m, :], start=True, stop=False)
                                pe.matmul(dst, G[:, p % 2, place(h), P:2 * P], U[:, place(h), :], start=False, stop=False)
                                mm = pe.matmul(dst, G[:, p % 2, place(h), 3 * P:4 * P], r.vtm[:, t, hs], start=False, stop=True)
                            mm.then_inc(y_done, 1)
                        if p < TAT - 1:
                            for h in range(NH):
                                rows, m, hs = rows_of(h), h // 2, slice(h * DH, (h + 1) * DH)
                                dst = side[h % 2][rows, (MC + m) * DH:(MC + m + 1) * DH]
                                pe.matmul(dst, tm[:, p % 2, 0, hs], U[:, place(h), :], start=True, stop=False)
                                mm = pe.matmul(dst, tm[:, p % 2, 1, hs], r.vtm[:, t, hs], start=False, stop=True)
                            mm.then_inc(gain_done, 1)

                for p in range(TAT + 1):
                    if p < TAT:
                        pairs(p)
                        for k in range(1, LEVELS):
                            level_step(p, k)
                            if p >= 1 and k <= 3:
                                chain(p - 1, k - 1)
                    else:
                        for part in range(3):
                            chain(p - 1, part)

            @block.vector
            def _(dve):
                dve.memset(S[:, :, :], 0.0).then_inc(state_step, 1)
                def start(p):
                    for h in range(NH):
                        dve.wait_ge(pair_done, p * NH + h + 1)
                        if p >= 2:
                            dve.wait_ge(state_step, 3 * (p - 2) + 4)
                        dve.tensor_tensor(G[:, p % 2, place(h), :].rearrange("p (a t) -> p a t", a=2), side[h % 2].rearrange("p (a t) -> p a t", a=2),
                                          pair_mask.unsqueeze(1).broadcast_to([P, 2, 2 * P]), ALU.mult).then_inc(pair_masked, 1)
                    for g in range(2):
                        hs = slice(4 * g, 4 * g + 4)
                        dve.wait_ge(au_done, 2 * p + g + 1)
                        dve.wait_ge(pair_masked, p * NH + NH)
                        dve.tensor_tensor(X[:, hs, :], QB[g].rearrange("p (h t) -> p h t", h=4),
                                          first_u.unsqueeze(1).broadcast_to([P, 4, P]), ALU.mult).then_inc(x_step, 1)
                        dve.tensor_tensor(XT[:, p % 2, hs, :], G[:, p % 2, hs, 0:P],
                                          first_t.unsqueeze(1).broadcast_to([P, 4, P]), ALU.mult).then_inc(x_step, 1)
                        dve.wait_ge(x_step, 4 * p + 2 * g + 2)
                        dve.tensor_tensor(X[:, hs, :], X[:, hs, :], c.ident[:, :].unsqueeze(1).broadcast_to([P, 4, P]), ALU.add)
                        dve.tensor_tensor(XT[:, p % 2, hs, :], XT[:, p % 2, hs, :], c.ident[:, :].unsqueeze(1).broadcast_to([P, 4, P]),
                                          ALU.add).then_inc(x0_ready, 1)

                def grow(p, k):
                    for g in range(2):
                        hs = slice(4 * g, 4 * g + 4)
                        n = 2 * (LEVELS - 1) * p + 2 * (k - 1) + g
                        dve.wait_ge(xt_done, n + 1)
                        if k < LEVELS - 1:
                            dve.wait_ge(x_done, 2 * (LEVELS - 2) * p + 2 * (k - 1) + g + 1)
                            dve.copy_predicated(X[:, hs, :], level[:, k, :].unsqueeze(1).broadcast_to([P, 4, P]),
                                                XB[g].rearrange("p (h t) -> p h t", h=4))
                        dve.copy_predicated(XT[:, p % 2, hs, :], level_t[:, k, :].unsqueeze(1).broadcast_to([P, 4, P]),
                                            XTB[g].rearrange("p (h t) -> p h t", h=4)).then_inc(x_ready, 1)

                def finish(p):
                    t = order[p]
                    if t >= 2:
                        dve.wait_ge(y_done, sum(q >= 2 for q in order[:p + 1]))
                        if p < TAT - 1:
                            dve.wait_ge(gain_done, p + 1)
                        for g in range(2):
                            y = ysum[:, t - 2, :].rearrange("p (m a e) -> p a m e", a=2, e=DH)[:, g, :, :]
                            part = side[g][:, 0:MC * DH].rearrange("p (m e) -> p m e", e=DH)
                            if d == 0:
                                dve.tensor_copy(y, part).then_inc(y_added, 1)
                            else:
                                dve.tensor_tensor(y, y, part, ALU.add).then_inc(y_added, 1)
                    if p < TAT - 1:
                        dve.wait_ge(gain_done, p + 1)
                        for g in range(2):
                            half = slice(g * DH, (g + 1) * DH)
                            dve.tensor_tensor(S2[half, :, :], S[half, :, :], side[g][half, MC * DH:2 * MC * DH].rearrange("p (m e) -> p m e", e=DH),
                                              ALU.add).then_inc(state_step, 1)
                        dve.wait_ge(state_step, 3 * p + 3)
                        dve.tensor_tensor(S[:, :, :], S2[:, :, :], f.gain[:, d, :, t:t + 1].broadcast_to([P, MC, DH]), ALU.mult).then_inc(state_step, 1)

                for p in range(TAT + 1):
                    if p < TAT:
                        start(p)
                        for k in range(1, LEVELS):
                            grow(p, k)
                            if p >= 1 and k == 3:
                                finish(p - 1)
                    else:
                        finish(p - 1)

            @block.scalar
            def _(act):
                def mover(p, k):
                    for g in range(2):
                        hs = slice(4 * g, 4 * g + 4)
                        n = 2 * (LEVELS - 1) * p + 2 * (k - 1) + g
                        act.wait_ge(q_done, n + 1)
                        if n >= 2:
                            act.wait_ge(x_ready, n - 1)
                        act.copy(Q[:, hs, :], QB[g].rearrange("p (h t) -> p h t", h=4)).then_inc(q_ready, 1)

                def carry(p, part):
                    if part == 0:
                        act.wait_ge(base_done, p + 1)
                        for g in range(2):
                            act.copy(base[:, 4 * g:4 * g + 4, :], side[g][:, 0:MC * DH].rearrange("p (m e) -> p m e", e=DH)).then_inc(base_ready, 1)
                    elif part == 1:
                        act.wait_ge(u_done, p + 1)
                        for g in range(2):
                            act.copy(U[:, 4 * g:4 * g + 4, :], side[g][:, 0:MC * DH].rearrange("p (m e) -> p m e", e=DH)).then_inc(u_ready, 1)

                for p in range(TAT + 1):
                    if p < TAT:
                        for a in range(2):
                            act.wait_ge(tm_done, 2 * p + a + 1)
                            if p >= 2:
                                act.wait_ge(state_step, 3 * (p - 2) + 4)
                            act.copy(tm[:, p % 2, a, :], side[a]).then_inc(tm_copied, 1)
                        for k in range(1, LEVELS):
                            mover(p, k)
                            if p >= 1 and k <= 3:
                                carry(p - 1, k - 1)
                    else:
                        for part in range(3):
                            carry(p - 1, part)



def head_norm_stage(nc, c, hsum, ysum, mo, g, bonus, mixed):
    with ExitStack() as ctx:
        def sb(n, shape):
            return ctx.enter_context(nc.sbuf_tensor(f"hn_{n}", shape, F32))
        sq = sb("sq", [P, DM])
        st = sb("st", [P, 8, 4, NH])
        tmp = sb("tmp", [P, 2, T])
        dve_step, var_ready, root_ready, normed, turned, scaled, mixed_ready = c.semaphores("hn", (
            "dve_step", "var_ready", "root_ready", "normed", "turned", "scaled", "mixed_ready"))
        pieces = [(hsum, t, LN_EPS) for t in range(TT)] + [(ysum, t, GN_EPS) for t in range(TT)]

        def by_head(x):
            return x.rearrange("p (h e) -> p h e", e=DH)
        with nc.Block() as block:
            @block.vector
            def _(dve):
                step = chain_of(dve, dve_step)
                for n, (src, t, eps) in enumerate(pieces):
                    x = by_head(src[:, t, :])
                    step(dve.tensor_reduce(st[:, n, 0, :], x, AX.X, ALU.add))
                    step(dve.tensor_scalar(st[:, n, 0, :], st[:, n, 0, :], 1.0 / DH, None, ALU.mult))
                    step(dve.tensor_tensor(x, x, st[:, n, 0, :].unsqueeze(2).broadcast_to([P, NH, DH]), ALU.subtract))
                    step(dve.tensor_tensor(sq[:, :], src[:, t, :], src[:, t, :], ALU.mult))
                    step(dve.tensor_reduce(st[:, n, 1, :], by_head(sq[:, :]), AX.X, ALU.add))
                    dve.tensor_scalar(st[:, n, 1, :], st[:, n, 1, :], 1.0 / DH, eps, ALU.mult, ALU.add).then_inc(var_ready, 1)
                for n, (src, t, eps) in enumerate(pieces):
                    x = by_head(src[:, t, :])
                    dve.wait_ge(root_ready, n + 1)
                    step(dve.reciprocal(st[:, n, 3, :], st[:, n, 2, :]))
                    dve.tensor_tensor(x, x, st[:, n, 3, :].unsqueeze(2).broadcast_to([P, NH, DH]), ALU.mult).then_inc(normed, 1)
                for k in range(2 * MC):
                    m = k % MC
                    dve.wait_ge(turned, k + 1)
                    if k < MC:
                        dve.scalar_tensor_tensor(out=mixed[:, k, :], in0=c.bank[k][:, :], scalar=c.cols[:, COLS["m_norm_w"] + m:COLS["m_norm_w"] + m + 1],
                                                 in1=mo[:, m, :], op0=ALU.mult, op1=ALU.mult).then_inc(mixed_ready, 1)
                    else:
                        step(dve.tensor_scalar(tmp[:, k % 2, :], c.bank[k][:, :], c.cols[:, COLS["r_norm_w"] + m:COLS["r_norm_w"] + m + 1],
                                               c.cols[:, COLS["r_norm_b"] + m:COLS["r_norm_b"] + m + 1], ALU.mult, ALU.add))
                        step(dve.tensor_tensor(tmp[:, k % 2, :], tmp[:, k % 2, :], bonus[:, m, :], ALU.add))
                        dve.tensor_tensor(mixed[:, k, :], tmp[:, k % 2, :], g[:, m, :], ALU.mult).then_inc(mixed_ready, 1)

            @block.scalar
            def _(act):
                for n in range(2 * TT):
                    act.wait_ge(var_ready, n + 1)
                    act.activation(st[:, n, 2, :], st[:, n, 1, :], ACT.Sqrt).then_inc(root_ready, 1)

            @block.tensor
            def _(pe):
                for k in range(2 * MC):
                    src, m = (hsum, k) if k < MC else (ysum, k - MC)
                    pe.wait_ge(normed, TT if k < MC else 2 * TT)
                    for t in range(TT):
                        mm = pe.transpose(c.bank[k][:, t * P:(t + 1) * P], src[:, t, m * P:(m + 1) * P], c.ident[:, :])
                    mm.then_inc(turned, 1)


def residual_stage(nc, c, w, o, x, gate):
    chunk_done, grown, added = c.semaphores("res", ("chunk_done", "grown", "added"))
    with nc.Block() as block:
        @block.sync
        def _(sp):
            w.feed(sp, U_OUT2)

        @block.scalar
        def _(act):
            for m in range(DC):
                act.mul(x[:, m, :], x[:, m, :], ALPHA).then_inc(grown, 1)

        @block.tensor
        def _(pe):
            for m in range(DC):
                unit = w.arrived(pe, 0, m // 2) if m % 2 == 0 else unit
                for k in range(DC):
                    b = (m % 2 * DC + k) * P
                    mm = pe.matmul(c.bank[m][:, :], unit[:, b:b + P], o[:, k, :], start=(k == 0), stop=(k == DC - 1))
                mm.then_inc((chunk_done, w.used)[m % 2], 1)

        @block.vector
        def _(dve):
            for m in range(DC):
                if m % 2 == 0:
                    dve.wait_ge(chunk_done, m // 2 + 1)
                else:
                    dve.wait_ge(w.used, w.at + m // 2 + 1)
                dve.wait_ge(grown, m + 1)
                dve.scalar_tensor_tensor(out=x[:, m, :], in0=c.bank[m][:, :], scalar=gate(m), in1=x[:, m, :],
                                         op0=ALU.mult, op1=ALU.add).then_inc(added, 1)
    w.at += U_OUT2



NOBODY = 1 << 20


def router_stage(nc, c, h, rt, rt_bias, iota, earlier, route, tokens):
    NR = E_GROUPS + EXPERTS
    with ExitStack() as ctx:
        def sb(n, shape, dt=F32):
            return ctx.enter_context(nc.sbuf_tensor(f"rt_{n}", shape, dt))
        L = sb("L", [P, TT, NR])
        lg8, top, idx, idxf = sb("lg8", [P, TT, 8]), sb("top", [P, TT, 8]), sb("idx", [P, TT, 8], U32), sb("idxf", [P, TT, 8])
        eg, sums, group = sb("eg", [P, TT, E_GROUPS]), sb("sums", [P, TT, 8]), sb("group", [P, TT])
        oh, pick, own = sb("oh", [P, TT, E_GROUPS]), sb("pick", [P, TT, E_GROUPS, E_EACH]), sb("own", [P, TT, E_EACH])
        expert, chosen, member = sb("expert", [P, 2, TT]), sb("chosen", [P, 2, TT, EXPERTS]), sb("member", [P, TT, EXPERTS])
        rank, most = sb("rank", [P, 2, TT]), sb("most", [P, 4])
        dve_step, logits_done, shifted, exp_ready, gap_ready, odds_ready, members_ready, ranks_done, turned, copied, tokens_stored = c.semaphores("rt", (
            "dve_step", "logits_done", "shifted", "exp_ready", "gap_ready", "odds_ready", "members_ready", "ranks_done",
            "turned", "copied", "tokens_stored"))
        logits, before, total = c.bank[0], c.bank[1][:, 0:TT * EXPERTS], c.bank[1][:, 256:256 + EXPERTS]
        with nc.Block() as block:
            @block.tensor
            def _(pe):
                for t in range(TT):
                    dst = logits[:, t * NR:(t + 1) * NR]
                    for k in range(DC):
                        pe.matmul(dst, h[:, k, t * P:(t + 1) * P], rt[:, k, :], start=(k == 0), stop=False)
                    mm = pe.matmul(dst, c.ones[0:1, :], rt_bias[0:1, :], start=False, stop=True)
                mm.then_inc(logits_done, 1)
                for t in range(TT):
                    if t == TT - 1:
                        pe.wait_ge(copied, 1)
                    for k in range(DC):
                        mm = pe.transpose(c.wide[t % 3 + 1][:, k * P:(k + 1) * P], h[:, k, t * P:(t + 1) * P], c.ident[:, :])
                    mm.then_inc(turned, 1)
                pe.wait_ge(members_ready, 1)
                for t in range(TT):
                    for s in range(t + 1):
                        pe.matmul(before[:, t * EXPERTS:(t + 1) * EXPERTS], (earlier if s == t else c.ones)[:, :], member[:, s, :],
                                  start=(s == 0), stop=(s == t))
                for t in range(TT):
                    mm = pe.matmul(total, c.ones[:, :], member[:, t, :], start=(t == 0), stop=(t == TT - 1))
                mm.then_inc(ranks_done, 1)

            @block.vector
            def _(dve):
                step = chain_of(dve, dve_step)
                dve.wait_ge(logits_done, 1)
                step(dve.tensor_copy(L[:, :, :].rearrange("p t n -> p (t n)"), logits[:, 0:TT * NR]))
                step(dve.memset(lg8[:, :, :], -3e38))
                step(dve.tensor_copy(lg8[:, :, 0:E_GROUPS], L[:, :, 0:E_GROUPS]))
                for t in range(TT):
                    step(dve.max(top[:, t, :], lg8[:, t, :]))
                    step(dve.max_index(idx[:, t, :], top[:, t, :], lg8[:, t, :]))
                step(dve.tensor_copy(group[:, :], idx[:, :, 0]))
                dve.tensor_tensor(eg[:, :, :], L[:, :, 0:E_GROUPS], top[:, :, 0:1].broadcast_to([P, TT, E_GROUPS]), ALU.subtract).then_inc(shifted, 1)
                step(dve.tensor_tensor(oh[:, :, :], iota[:, 0:E_GROUPS].unsqueeze(1).broadcast_to([P, TT, E_GROUPS]),
                                       group[:, :].unsqueeze(2).broadcast_to([P, TT, E_GROUPS]), ALU.is_equal))
                dve.wait_ge(exp_ready, 1)
                step(dve.tensor_reduce(sums[:, :, 0], eg[:, :, :], AX.X, ALU.add))
                step(dve.reciprocal(sums[:, :, 1], sums[:, :, 0]))
                for t in range(TT):
                    step(dve.tensor_tensor(pick[:, t, :, :], L[:, t, E_GROUPS:NR].rearrange("p (g e) -> p g e", g=E_GROUPS),
                                           oh[:, t, :].unsqueeze(2).broadcast_to([P, E_GROUPS, E_EACH]), ALU.mult))
                    step(dve.tensor_reduce(own[:, t, :], pick[:, t, :, :].rearrange("p g e -> p e g"), AX.X, ALU.add))
                    step(dve.max(top[:, t, :], own[:, t, :]))
                    step(dve.max_index(idx[:, t, :], top[:, t, :], own[:, t, :]))
                step(dve.tensor_copy(idxf[:, :, :], idx[:, :, :]))
                dve.tensor_tensor(sums[:, :, 2], top[:, :, 1], top[:, :, 0], ALU.subtract).then_inc(gap_ready, 1)
                dve.wait_ge(odds_ready, 1)
                step(dve.tensor_scalar(sums[:, :, 4], sums[:, :, 3], 1.0, None, ALU.add))
                step(dve.reciprocal(sums[:, :, 5], sums[:, :, 4]))
                step(dve.tensor_tensor(route.share[:, :, 0], sums[:, :, 5], sums[:, :, 1], ALU.mult))
                step(dve.tensor_tensor(route.share[:, :, 1], route.share[:, :, 0], sums[:, :, 3], ALU.mult))
                for n in range(2):
                    step(dve.scalar_tensor_tensor(out=expert[:, n, :], in0=group[:, :], scalar=float(E_EACH), in1=idxf[:, :, n],
                                                  op0=ALU.mult, op1=ALU.add))
                    step(dve.tensor_tensor(chosen[:, n, :, :], iota[:, :].unsqueeze(1).broadcast_to([P, TT, EXPERTS]),
                                           expert[:, n, :].unsqueeze(2).broadcast_to([P, TT, EXPERTS]), ALU.is_equal))
                dve.tensor_tensor(member[:, :, :], chosen[:, 0, :, :], chosen[:, 1, :, :], ALU.add).then_inc(members_ready, 1)
                dve.wait_ge(ranks_done, 1)
                for n in range(2):
                    step(dve.tensor_tensor(chosen[:, n, :, :], chosen[:, n, :, :], before.rearrange("p (t e) -> p t e", t=TT), ALU.mult))
                    step(dve.tensor_reduce(rank[:, n, :], chosen[:, n, :, :], AX.X, ALU.add))
                    step(dve.scalar_tensor_tensor(out=rank[:, n, :], in0=expert[:, n, :], scalar=float(T), in1=rank[:, n, :],
                                                  op0=ALU.mult, op1=ALU.add))
                step(dve.tensor_copy(route.row[:, :, :], rank[:, :, :]))
                step(dve.tensor_reduce(most[:, 0:1], total, AX.X, ALU.max))
                step(dve.tensor_scalar(most[:, 1:2], most[:, 0:1], float(P), 1.0, ALU.is_gt, ALU.add))
                for n in range(2, TT):
                    step(dve.scalar_tensor_tensor(out=most[:, n:n + 1], in0=most[:, 0:1], scalar=float(n * P), in1=most[:, n - 1:n],
                                                  op0=ALU.is_gt, op1=ALU.add))
                step(dve.tensor_copy(route.rounds[:, :], most[:, TT - 1:TT]))

            @block.scalar
            def _(act):
                act.wait_ge(shifted, 1)
                act.activation(eg[:, :, :], eg[:, :, :], ACT.Exp).then_inc(exp_ready, 1)
                act.wait_ge(gap_ready, 1)
                act.activation(sums[:, :, 3], sums[:, :, 2], ACT.Exp).then_inc(odds_ready, 1)
                for t in range(TT):
                    act.wait_ge(turned, t + 1)
                    act.copy(route.tokens[:, t, :], c.wide[t % 3 + 1][:, :]).then_inc(copied, 1)

            @block.sync
            def _(sp):
                sp.wait_ge(copied, TT)
                sp.dma_start(tokens.rearrange("(t p) d -> p t d", p=P), route.tokens[:, :, :]).then_inc(tokens_stored, 16)
                sp.wait_ge(tokens_stored, 16)


def slots_stage(nc, c, route, pairs, table):
    with ExitStack() as ctx:
        free = ctx.enter_context(nc.sbuf_tensor("sl_free", [P, 2 * P], U32))
        rows = ctx.enter_context(nc.sbuf_tensor("sl_rows", [P, 2 * P], U32))
        rowsf = ctx.enter_context(nc.sbuf_tensor("sl_rowsf", [P, 2, P], F32))
        filled, emptied, placed, fetched, converted, turned, done = c.semaphores("sl", (
            "filled", "emptied", "placed", "fetched", "converted", "turned", "done"))
        by_row = table.rearrange("(c s) v -> c (s v)", c=P)
        with nc.Block() as block:
            @block.gpsimd
            def _(pool):
                pool.memset(free[:, :], NOBODY).then_inc(filled, 1)
                last_slot = pool.to_reg(EXPERTS * T - 1)
                pool.wait_ge(emptied, 16)
                for t in range(TT):
                    for n in range(2):
                        pool.indirect_dma_start(table, bass.IndirectOffsetOnAxis(route.row[:, n, t:t + 1], 0), pairs[:, t, n, :], None,
                                                bounds_check=last_slot, oob_is_err=False).then_inc(placed, 16)

            @block.sync
            def _(sp):
                sp.wait_ge(filled, 1)
                sp.dma_start(by_row, free[:, :]).then_inc(emptied, 16)
                sp.wait_ge(placed, 16 * 2 * TT)
                sp.dma_start(rows[:, :], by_row).then_inc(fetched, 16)

            @block.vector
            def _(dve):
                dve.wait_ge(fetched, 16)
                dve.tensor_copy(rowsf[:, :, :], rows[:, :].rearrange("p (s v) -> p v s", v=2)).then_inc(converted, 1)
                dve.wait_ge(turned, 1)
                dve.tensor_copy(route.slots[:, :, :], c.bank[0][:, 0:2 * P].rearrange("p (v c) -> p v c", v=2)).then_inc(done, 1)

            @block.tensor
            def _(pe):
                pe.wait_ge(converted, 1)
                for v in range(2):
                    mm = pe.transpose(c.bank[0][:, v * P:(v + 1) * P], rowsf[:, v, :], c.ident[:, :])
                mm.then_inc(turned, 1)


def gate_up_at(s, n):
    return n if s == 0 else U_EXPERT * s - 2 + n


def down_at(e, n):
    return U_EXPERT * e + (4 if e == EXPERTS - 1 else 8) + n


def experts_stage(nc, c, w, route, tokens, pair_rows):
    ALL = U_EXPERT * EXPERTS
    base = w.at
    with ExitStack() as ctx:
        def sb(n, shape, dt=F32):
            return ctx.enter_context(nc.sbuf_tensor(f"ex_{n}", shape, dt))
        w_hi, w_lo = [sb(f"w_hi{i}", [P, UNIT], F32R) for i in range(RING)], [sb(f"w_lo{i}", [P, UNIT], F32R) for i in range(RING)]
        rows, results = sb("rows", [P, 2, D]), sb("results", [P, 2, D])
        x_hi, x_lo = [sb(f"x_hi{i}", [P, D], F32R) for i in range(2)], [sb(f"x_lo{i}", [P, D], F32R) for i in range(2)]
        silu, hidden = sb("silu", [P, T]), sb("hidden", [P, T])
        h_hi, h_lo = sb("h_hi", [P, T], F32R), sb("h_lo", [P, T], F32R)
        take, give = [sb(f"take{i}", [P, 1], U32) for i in range(2)], [sb(f"give{i}", [P, 1], U32) for i in range(2)]
        (gathered0, gathered1, scattered0, scattered1, index_ready, hi_ready, unit_used, x_turned, x_hi_ready, x_ready, silu_ready,
         hidden_ready, h_turned, h_hi_ready, h_ready, low_read, high_read, blank_ready) = c.semaphores("ex", (
             "gathered0", "gathered1", "scattered0", "scattered1", "index_ready", "hi_ready", "unit_used", "x_turned", "x_hi_ready",
             "x_ready", "silu_ready", "hidden_ready", "h_turned", "h_hi_ready", "h_ready", "low_read", "high_read", "blank_ready"))
        blank, held = sb("blank", [P, 1]), sb("held", [P, 2])
        gathered, scattered = [gathered0, gathered1], [scattered0, scattered1]
        GATE, UP, DOWN, XT, HT = c.bank[0], c.bank[1], c.bank[2:4], c.wide[2], c.bank[6]

        def rounds_of(eng):
            return eng.value_load(route.rounds[0:1, 0:1], min_val=1, max_val=TT)

        def steps(eng, r, step):
            step(EXPERTS * r, 0, 0)
            with eng.Fori(0, EXPERTS // 2 - 1) as j:
                for s in range(1, 3):
                    step(EXPERTS * r + 2 * j, 2 * j, s)
            step(EXPERTS * r, 0, EXPERTS - 1)
            step(EXPERTS * r, 0, EXPERTS)

        with nc.Block() as block:
            @block.sync
            def _(sp):
                with sp.Fori(0, rounds_of(sp)) as r:
                    with sp.Fori(0, ALL // RING - 1) as j:
                        for i in range(RING):
                            n = base + i
                            sp.wait_ge(w.used, ALL * r + RING * j + (n + 1))
                            sp.dma_start(w.ring[n % RING][:, :], w.stream[RING * j + (n + RING)]).then_inc(w.loaded[n % RING], 16)
                    for i in range(RING):
                        n = base + i
                        sp.wait_ge(w.used, ALL * r + (n + ALL - RING + 1))
                        sp.dma_start(w.ring[n % RING][:, :], w.stream[n]).then_inc(w.loaded[n % RING], 16)

            @block.gpsimd
            def _(pool):
                for p in range(2):
                    pool.dma_start(results[:, p, :], tokens[0:P, :]).then_inc(scattered[p], 16)
                pool.memset(blank[:, :], 0.0).then_inc(blank_ready, 1)
                pool.wait_ge(blank_ready, 1)
                last_token, last_pair = pool.to_reg(T - 1), pool.to_reg(2 * T - 1)
                with pool.Fori(0, rounds_of(pool)) as r:
                    def indices(dst, column, before):
                        pool.tensor_tensor(held[:, 0:1], blank[:, :], blank[:, :], ALU.add).then_inc(index_ready, 1)
                        pool.tensor_copy(dst, column).then_inc(index_ready, 1)
                        pool.wait_ge(index_ready, 3 * before + 2)
                        pool.tensor_tensor(held[:, 1:2], blank[:, :], blank[:, :], ALU.add).then_inc(index_ready, 1)

                    def take_rows(e, j2, s, before):
                        indices(take[s % 2][:, :], route.slots[:, 0, bass.ds(TT * j2 + r + TT * s, 1)], before)
                        pool.indirect_dma_start(rows[:, s % 2, :], None, tokens, bass.IndirectOffsetOnAxis(take[s % 2][:, 0:1], 0),
                                                bounds_check=last_token, oob_is_err=False).then_inc(gathered[s % 2], 16)

                    pool.wait_ge(low_read, EXPERTS * r + 1)
                    pool.wait_ge(high_read, EXPERTS * r + 1)
                    for s in range(2):
                        take_rows(EXPERTS * r, 0, s, 2 * EXPERTS * r + s)

                    def step(e, j2, s):
                        if 1 <= s < EXPERTS - 1:
                            pool.wait_ge(x_turned, e + s)
                            take_rows(e, j2, s + 1, 2 * e + 2 * s)
                        if s >= 1:
                            g = s - 1
                            pool.wait_ge(low_read, e + (g + 2))
                            pool.wait_ge(high_read, e + (g + 2))
                            indices(give[g % 2][:, :], route.slots[:, 1, bass.ds(TT * j2 + r + TT * g, 1)],
                                    2 * e + min(2 * s + 1, EXPERTS + s - 1))
                            pool.indirect_dma_start(pair_rows, bass.IndirectOffsetOnAxis(give[g % 2][:, 0:1], 0), results[:, g % 2, :], None,
                                                    bounds_check=last_pair, oob_is_err=False).then_inc(scattered[g % 2], 16)
                    steps(pool, r, step)

            @block.tensor
            def _(pe):
                def turn_rows(e, j2, s):
                    pe.wait_ge(gathered[s % 2], 8 * e + (s // 2 + 1) * 16)
                    for k in range(DC):
                        mm = pe.transpose(XT[:, k * P:(k + 1) * P], rows[:, s % 2, k * P:(k + 1) * P], c.ident[:, :])
                    mm.then_inc(x_turned, 1)

                def products(dst, a_hi, a_lo, b_hi, b_lo, first, last):
                    pe.matmul(dst, a_hi, b_hi, start=first, stop=False)
                    pe.matmul(dst, a_hi, b_lo, start=False, stop=False)
                    return pe.matmul(dst, a_lo, b_hi, start=False, stop=last)

                def step(e, j2, s):
                    if s < EXPERTS:
                        pe.wait_ge(x_ready, e + (s + 1))
                        for n in range(4):
                            at = gate_up_at(s, n)
                            pe.wait_ge(w.used, U_EXPERT * e + (base + at + 1))
                            for i in range(4):
                                k = n % 2 * 4 + i
                                mm = products((GATE, UP)[n // 2][:, :], x_hi[s % 2][:, k * P:(k + 1) * P], x_lo[s % 2][:, k * P:(k + 1) * P],
                                              w_hi[at % RING][:, i * T:(i + 1) * T], w_lo[at % RING][:, i * T:(i + 1) * T], k == 0, k == DC - 1)
                            mm.then_inc(unit_used, 1)
                    if s < EXPERTS - 1:
                        turn_rows(e, j2, s + 1)
                    if s >= 1:
                        pe.wait_ge(h_ready, e + s)
                        pe.wait_ge(low_read, e + s)
                        pe.wait_ge(high_read, e + s)
                        for n in range(2):
                            at = down_at(s - 1, n)
                            pe.wait_ge(w.used, U_EXPERT * e + (base + at + 1))
                            for i in range(2):
                                k = n * 2 + i
                                for half in range(2):
                                    b = i * D + half * T
                                    mm = products(DOWN[half][:, :], h_hi[:, k * P:(k + 1) * P], h_lo[:, k * P:(k + 1) * P],
                                                  w_hi[at % RING][:, b:b + T], w_lo[at % RING][:, b:b + T], k == 0, k == EC - 1)
                            mm.then_inc(unit_used, 1)
                    if s < EXPERTS:
                        pe.wait_ge(hidden_ready, e + (s + 1))
                        for q in range(EC):
                            mm = pe.transpose(HT[:, q * P:(q + 1) * P], hidden[:, q * P:(q + 1) * P], c.ident[:, :])
                        mm.then_inc(h_turned, 1)

                with pe.Fori(0, rounds_of(pe)) as r:
                    turn_rows(EXPERTS * r, 0, 0)
                    steps(pe, r, step)

            @block.scalar
            def _(act):
                act.copy(rows[:, 0, :], route.tokens[:, 0, :]).then_inc(low_read, 1)

                def hi(e, at):
                    n = base + at
                    act.wait_ge(w.loaded[n % RING], 24 * e + 16 * (n // RING + 1))
                    if at >= RING:
                        act.wait_ge(unit_used, U_EXPERT * e + (at - RING + 1))
                    act.copy(w_hi[at % RING][:, :], w.ring[n % RING][:, :]).then_inc(hi_ready, 1)

                def x_part(e, s):
                    act.wait_ge(x_turned, e + (s + 1))
                    act.copy(x_hi[s % 2][:, :], XT[:, :]).then_inc(x_hi_ready, 1)

                def step(e, j2, s):
                    if s >= 1:
                        for n in range(2):
                            hi(e, down_at(s - 1, n))
                    if s < EXPERTS:
                        act.wait_ge(unit_used, U_EXPERT * e + (gate_up_at(s, 1) + 1))
                        act.activation(silu[:, :], GATE[:, :], ACT.Silu).then_inc(silu_ready, 1)
                    if s < EXPERTS - 1:
                        hi(e, gate_up_at(s + 1, 0))
                        x_part(e, s + 1)
                        hi(e, gate_up_at(s + 1, 1))
                        hi(e, gate_up_at(s + 1, 2))
                    if s >= 1:
                        g = s - 1
                        act.wait_ge(unit_used, U_EXPERT * e + (down_at(g, 1) + 1))
                        act.wait_ge(scattered[g % 2], 8 * e + 16 * (g // 2 + 1))
                        act.copy(results[:, g % 2, 0:T], DOWN[0][:, :]).then_inc(low_read, 1)
                    if s < EXPERTS - 1:
                        hi(e, gate_up_at(s + 1, 3))
                    if s < EXPERTS:
                        act.wait_ge(h_turned, e + (s + 1))
                        act.copy(h_hi[:, :], HT[:, :]).then_inc(h_hi_ready, 1)

                with act.Fori(0, rounds_of(act)) as r:
                    for n in range(4):
                        hi(EXPERTS * r, n)
                    x_part(EXPERTS * r, 0)
                    steps(act, r, step)

            @block.vector
            def _(dve):
                dve.tensor_copy(rows[:, 1, :], route.tokens[:, 1, :]).then_inc(high_read, 1)

                def lo(e, at):
                    n = base + at
                    dve.wait_ge(hi_ready, U_EXPERT * e + (at + 1))
                    dve.tensor_tensor(w_lo[at % RING][:, :], w.ring[n % RING][:, :], w_hi[at % RING][:, :].bitcast(F32),
                                      ALU.subtract).then_inc(w.used, 1)

                def x_part(e, s):
                    dve.wait_ge(x_hi_ready, e + (s + 1))
                    dve.tensor_tensor(x_lo[s % 2][:, :], XT[:, :], x_hi[s % 2][:, :].bitcast(F32), ALU.subtract).then_inc(x_ready, 1)

                def step(e, j2, s):
                    if s >= 1:
                        for n in range(2):
                            lo(e, down_at(s - 1, n))
                    if s < EXPERTS:
                        dve.wait_ge(silu_ready, e + (s + 1))
                        dve.wait_ge(unit_used, U_EXPERT * e + (gate_up_at(s, 3) + 1))
                        dve.tensor_tensor(hidden[:, :], silu[:, :], UP[:, :], ALU.mult).then_inc(hidden_ready, 1)
                    if s < EXPERTS - 1:
                        lo(e, gate_up_at(s + 1, 0))
                        x_part(e, s + 1)
                        lo(e, gate_up_at(s + 1, 1))
                        lo(e, gate_up_at(s + 1, 2))
                    if s >= 1:
                        g = s - 1
                        dve.wait_ge(unit_used, U_EXPERT * e + (down_at(g, 1) + 1))
                        dve.wait_ge(scattered[g % 2], 8 * e + 16 * (g // 2 + 1))
                        dve.tensor_copy(results[:, g % 2, T:D], DOWN[1][:, :]).then_inc(high_read, 1)
                    if s < EXPERTS - 1:
                        lo(e, gate_up_at(s + 1, 3))
                    if s < EXPERTS:
                        dve.wait_ge(h_hi_ready, e + (s + 1))
                        dve.tensor_tensor(h_lo[:, :], HT[:, :], h_hi[:, :].bitcast(F32), ALU.subtract).then_inc(h_ready, 1)

                with dve.Fori(0, rounds_of(dve)) as r:
                    for n in range(4):
                        lo(EXPERTS * r, n)
                    x_part(EXPERTS * r, 0)
                    steps(dve, r, step)
    w.at += ALL


def combine_stage(nc, c, route, pair_rows, y):
    with ExitStack() as ctx:
        both = ctx.enter_context(nc.sbuf_tensor("cb_both", [P, TT, 2, D], F32))
        loaded, scaled, summed, turned, low_done, high_done = c.semaphores("cb", ("loaded", "scaled", "summed", "turned", "low_done", "high_done"))
        with nc.Block() as block:
            @block.sync
            def _(sp):
                for t in range(TT):
                    sp.dma_start(both[:, t, :, :].rearrange("p n d -> p (n d)"),
                                 pair_rows[2 * P * t:2 * P * (t + 1), :].rearrange("(p n) d -> p (n d)", n=2)).then_inc(loaded, 16)
                    sp.wait_ge(loaded, 16 * (t + 1))

            @block.vector
            def _(dve):
                for t in range(TT):
                    dve.wait_ge(loaded, 16 * (t + 1))
                    dve.tensor_scalar(both[:, t, 0, :], both[:, t, 0, :], route.share[:, t, 0:1], None, ALU.mult).then_inc(scaled, 1)
                    dve.wait_ge(scaled, t + 1)
                    dve.scalar_tensor_tensor(out=both[:, t, 0, :], in0=both[:, t, 1, :], scalar=route.share[:, t, 1:2], in1=both[:, t, 0, :],
                                             op0=ALU.mult, op1=ALU.add).then_inc(summed, 1)
                for t in range(TT):
                    dve.wait_ge(turned, 2 * t + 2)
                    dve.tensor_copy(y[:, 4:8, t * P:(t + 1) * P], c.wide[t][:, T:D].rearrange("p (k t) -> p k t", k=4)).then_inc(high_done, 1)

            @block.tensor
            def _(pe):
                for t in range(TT):
                    pe.wait_ge(summed, t + 1)
                    for k in range(DC):
                        mm = pe.transpose(c.wide[t][:, k * P:(k + 1) * P], both[:, t, 0, k * P:(k + 1) * P], c.ident[:, :])
                        if k % 4 == 3:
                            mm.then_inc(turned, 1)

            @block.scalar
            def _(act):
                for t in range(TT):
                    act.wait_ge(turned, 2 * t + 1)
                    act.copy(y[:, 0:4, t * P:(t + 1) * P], c.wide[t][:, 0:T].rearrange("p (k t) -> p k t", k=4)).then_inc(low_done, 1)


def last_residual_stage(nc, c, x, y, gate):
    grown, added = c.semaphores("lres", ("grown", "added"))
    with nc.Block() as block:
        @block.scalar
        def _(act):
            for m in range(DC):
                act.mul(x[:, m, :], x[:, m, :], ALPHA).then_inc(grown, 1)

        @block.vector
        def _(dve):
            for m in range(DC):
                dve.wait_ge(grown, m + 1)
                dve.scalar_tensor_tensor(out=x[:, m, :], in0=y[:, m, :], scalar=gate(m), in1=x[:, m, :],
                                         op0=ALU.mult, op1=ALU.add).then_inc(added, 1)


def load_stage(nc, pairs, name):
    done = nc.alloc_semaphore(name)
    with nc.Block() as block:
        @block.sync
        def _(sp):
            for dst, src in pairs:
                sp.dma_start(dst, src).then_inc(done, 16)
            sp.wait_ge(done, 16 * len(pairs))


class Bag:
    pass


def second_block(nc, c, w, a, x, out, upto, dump):
    with ExitStack() as block_ctx:
        def sb(n, shape, dt=F32):
            return block_ctx.enter_context(nc.sbuf_tensor(n, shape, dt))
        mod, mod1 = sb("mod", [P, 6 * DC, 2]), sb("mod1", [P, 6 * DC, 2])
        c.same = sb("same", [P, P])

        def at(part, which=0, plus=False):
            return lambda k: (mod1 if plus else mod)[:, part * DC + k, which:which + 1]

        with ExitStack() as mixer_ctx:
            def sm(n, shape, dt=F32):
                return mixer_ctx.enter_context(nc.sbuf_tensor(n, shape, dt))
            at_late = -(-nc.sbuf_base // 32) * 32
            room_late = 4 * TT * DM + TAT * DM
            lo_in_late = (room_late - DC * TA) // TA
            in_hi = nc.alloc_sbuf_tensor_at("in_hi", [P, DC, TA], F32R, offset=at_late)
            in_lo = nc.alloc_sbuf_tensor_at("in_lo", [P, lo_in_late, TA], F32R, offset=at_late + 4 * DC * TA)
            late = sm("late", [P, room_late])

            def view(first, count, wide):
                return late[:, first:first + count * wide].rearrange("p (k t) -> p k t", t=wide)
            hsum, ysum = view(0, TT, DM), view(2048, TT, DM)
            u, r, f, g = Bag(), Bag(), Bag(), Bag()
            u.mo, r.g, r.bonus, r.vtm = sm("mo", [P, MC, T]), view(4096, MC, T), view(6144, MC, T), view(8192, TAT, DM)
            f.gain = sm("state_gain", [P, 2, MC, TAT])
            f.scratch = nc.dram_tensor("factors", [2, TAT, P, MC, 4, P], F32, kind="Internal").ap()
            with ExitStack() as in_ctx:
                def si(n, shape, dt=F32):
                    return in_ctx.enter_context(nc.sbuf_tensor(n, shape, dt))
                u.conv = si("conv", [P, CONV_CHUNKS, TA])
                u.lw, u.la, u.lg = si("lw", [P, TA]), si("la", [64, TA]), si("lg", [P, T])
                u.bias = si("gate_bias", [64, 2])
                with ExitStack() as m_ctx:
                    def smm(n, shape, dt=F32):
                        return m_ctx.enter_context(nc.sbuf_tensor(n, shape, dt))
                    raw = smm("gate_raw", [P, 2 * TA])
                    at_v1 = -(-nc.sbuf_base // 32) * 32
                    unit_hi = [nc.alloc_sbuf_tensor_at(f"in_unit_hi{i}", [P, UNIT], F32R, offset=at_v1 + i * 4 * UNIT) for i in range(2)]
                    u.v1 = smm("v1", [P, TAT, NH, DH + 1])
                    u.li, u.lf = raw[0:64, 0:TA], raw[0:64, TA:2 * TA]
                    with ExitStack() as p_ctx:
                        def sp_(n, shape, dt=F32):
                            return p_ctx.enter_context(nc.sbuf_tensor(n, shape, dt))
                        cond, ada_b = sp_("cond", [P, DC, 2]), sp_("ada_b", [P, 6 * DC])
                        sp_("after_v1", [P, 2 * UNIT - TAT * NH * (DH + 1)])
                        load_stage(nc, [(cond[:, :, :], a["cond"]), (ada_b[:, :], a["ada_b"]), (u.bias[:, :], a["gate_bias"]),
                                        (c.same[:, :], a["same"])], "consts_ada")
                        room = u.conv[:, :, :].rearrange("p m t -> p (m t)")
                        ada_stage(nc, c, w, cond, mod, mod1, ada_b[:, :], room)
                        h = room[:, 5632:5632 + DC * TA].rearrange("p (k t) -> p k t", t=TA)
                        ctx_in = room[:, 12288:12288 + DC * CTX].rearrange("p (k t) -> p k t", t=CTX)
                        load_stage(nc, [(ctx_in[:, :, :], a["ctx"]), (h[:, :, CTX:TA], x[:, :, :])], "load_ctx")
                        layer_norm_stage(nc, c, ctx_in, h[:, :, 0:CTX], CTX, at(1, 1, True), at(0, 1), "lnc", room)
                        layer_norm_stage(nc, c, h[:, :, CTX:TA], h[:, :, CTX:TA], T, at(1, 0, True), at(0, 0), "lnx", room)
                        if upto == 5:
                            return dump(h)
                        pads = [(sp_(f"grid{i}", [P, ROWS + 2, GRID_W + 2]), sp_(f"seq{i}", [P, CTX + 2])) for i in range(2)]
                        with nc.Block() as block:
                            @block.gpsimd
                            def _(pool):
                                for grid, seq in pads:
                                    pool.memset(grid[:, :, :], 0.0)
                                    pool.memset(seq[:, :], 0.0)
                        w.hi = unit_hi
                        lo_rest = sp_("in_lo_rest", [P, DC - lo_in_late, TA], F32R)
                        h_parts = ([in_hi[:, k, :] for k in range(DC)],
                                   [in_lo[:, k, :] for k in range(lo_in_late)] + [lo_rest[:, k, :] for k in range(DC - lo_in_late)])
                        split_stage(nc, c, h, h_parts[0], h_parts[1], "split_in")
                        project_in_stage(nc, c, w, h_parts, u, pads)
                    if upto == 6:
                        return dump(u.conv)
                    g.bm, g.cols = smm("bm", [GR, TA]), smm("gate_cols", [P, 3 * TAT, GR])
                    g.rows, g.inter = view(0, 3, TA)[0:GR], view(3 * TA, 1, TA)[0:GR, 0, :]
                    g.reset, g.temps = view(4 * TA, 1, TA)[0:GR, 0, :], view(8192, 4, TA)[0:GR]
                    g.sc = raw[:, 0:2 * DM].rearrange("p (i e t) -> p i e t", i=2, t=P)
                    g.hout = raw[:, 2 * DM:3 * DM].rearrange("p (i e t) -> p i e t", i=2, t=DH)
                    g.qi, g.decay = view(4096, 2 * MC, T).rearrange("p (d m) t -> p d m t", d=2), smm("decay", [P, 2, MC, TAT])
                    g.ktm = view(8192, TAT, DM)
                    g.kw, g.expo = view(2048, 2, DM), view(3072, 8, P).rearrange("p (i e) t -> p i e t", i=2)
                    u.pair, u.never = smm("pair_rows", [GR, 8, P]), smm("never", [P, 2, P])
                    load_stage(nc, [(u.pair[:, :, :], a["pair_rows"]), (u.never[:, :, :], a["never"])], "consts_ml")
                    gates_stage(nc, c, u, g)
                    mlstm_stage(nc, c, u, g, hsum)
                    if upto == 7:
                        return dump(hsum)
                lowrank = si("lowrank", [P, 3, DM])
                load_stage(nc, [(lowrank[:, :, :], a["lowrank"])], "load_lowrank")
                r.a, r.kh, r.kmod = u.conv[:, 0:MC, :], u.conv[:, MC:2 * MC, :], u.conv[:, 3 * MC:4 * MC, :]
                r.room = view(2048, 2, TA)
                rwkv_common_stage(nc, c, u, r, lowrank)
                for d in range(2):
                    rwkv_factors_stage(nc, c, u, r, f, lowrank, d)
            with ExitStack() as r_ctx:
                masks = Bag()
                masks.pair = r_ctx.enter_context(nc.sbuf_tensor("pair_mask", [P, 2, 2 * P], F32))
                masks.first = r_ctx.enter_context(nc.sbuf_tensor("first_mask", [P, 2, P], F32))
                masks.level = r_ctx.enter_context(nc.sbuf_tensor("level_mask", [P, 2, LEVELS, P], U32))
                load_stage(nc, [(masks.pair[:, :, :], a["pair_mask"]), (masks.first[:, :, :], a["first_mask"]),
                                (masks.level[:, :, :, :], a["level_mask"])], "load_masks")
                for d in range(2):
                    rwkv_stage(nc, c, r, f, masks, ysum, d)
            if upto == 8:
                return dump(ysum)
            mixed = sm("mixed", [P, DC, T])
            head_norm_stage(nc, c, hsum, ysum, u.mo, r.g, r.bonus, mixed)
            residual_stage(nc, c, w, mixed, x, at(2))
        col = lambda name: (lambda k: c.cols[:, COLS[name] + k:COLS[name] + k + 1])
        layer_norm_stage(nc, c, x, x, T, col("ln1_g"), col("ln1_b"), "ln1")
        if upto == 9:
            return dump(x)
        route = Bag()
        route.share, route.row, route.rounds = sb("share", [P, TT, 2]), sb("slot_row", [P, 2, TT], U32), sb("rounds", [P, 1], U32)
        route.slots = sb("slots", [P, 2, P], U32)
        tokens, table, pair_rows = [nc.dram_tensor(n, shape, dt, kind="Internal").ap() for n, shape, dt in (
            ("tokens", [T, D], F32), ("slot_table", [EXPERTS * T, 2], U32), ("pair_rows_out", [2 * T, D], F32))]
        dev = sb("y2", [P, DC, T])
        with ExitStack() as moe:
            route.tokens = moe.enter_context(nc.sbuf_tensor("tokens_sb", [P, TT, D], F32))
            with ExitStack() as r_ctx:
                def sr(n, shape, dt=F32):
                    return r_ctx.enter_context(nc.sbuf_tensor(n, shape, dt))
                h, rt, rt_bias = sr("h2", [P, DC, T]), sr("rt", [P, DC, E_GROUPS + EXPERTS]), sr("rt_bias", [1, E_GROUPS + EXPERTS])
                iota, earlier, pairs = sr("iota", [P, EXPERTS]), sr("earlier", [P, P]), sr("pairs", [P, TT, 2, 2], U32)
                load_stage(nc, [(dev[:, :, :], x[:, :, :]), (rt[:, :, :], a["rt"]), (rt_bias[:, :], a["rt_bias"]), (iota[:, :], a["iota"]),
                                (earlier[:, :], a["earlier"]), (pairs[:, :, :, :], a["pairs"])], "load_rt")
                layer_norm_stage(nc, c, dev, h, T, at(4, 0, True), at(3), "lnm")
                router_stage(nc, c, h, rt, rt_bias, iota, earlier, route, tokens)
                slots_stage(nc, c, route, pairs, table)
            experts_stage(nc, c, w, route, tokens, pair_rows)
        combine_stage(nc, c, route, pair_rows, dev)
        last_residual_stage(nc, c, x, dev, at(5))
        layer_norm_stage(nc, c, x, x, T, col("ln2_g"), col("ln2_b"), "ln2")
        if upto == 10:
            return dump(x)
        stored = nc.alloc_semaphore("output_stored")
        with nc.Block() as block:
            @block.sync
            def _(sp):
                sp.dma_start(out, x[:, :, :]).then_inc(stored, 16)
                sp.wait_ge(stored, 16)



COLS = {}


def columns(names):
    at = 0
    for n, wide in names:
        COLS[n] = at
        at += wide
    return at


N_COLS = columns([("norm_mix0", DC), ("norm_mix1", DC), ("norm_ffn0", DC), ("norm_ffn1", DC), ("norm_final", DC),
                  ("conv", 9 * CONV_CHUNKS), ("r_w0", 2 * MC), ("r_a0", MC), ("r_kk", MC), ("r_ka", MC), ("r_bonus", MC),
                  ("m_norm_w", MC), ("r_norm_w", MC), ("r_norm_b", MC), ("ln1_g", DC), ("ln1_b", DC), ("ln2_g", DC), ("ln2_b", DC)])


def first_block(nc, c, w, a, x, upto, dump):
    with ExitStack() as first:
        h = tuple(first.enter_context(nc.sbuf_tensor(n, [P, DC, T], F32R)) for n in ("h_hi", "h_lo"))
        w.hi = [first.enter_context(nc.sbuf_tensor(f"unit_hi{i}", [P, UNIT], F32R)) for i in range(2)]
        rms_stage(nc, c, x, h, COLS["norm_mix0"], "rms0")
        with ExitStack() as layer:
            def sl(n, shape):
                return layer.enter_context(nc.sbuf_tensor(n, shape, F32))
            q, k_, v, o = sl("q_a", [P, DC, T]), sl("k_a", [P, 2, T]), sl("v_a", [P, TT, 2 * P]), sl("o_a", [P, DC, T])
            dist, sink = sl("dist_a", [P, 3 * P]), sl("sink", [P, HEADS])
            consts = nc.alloc_semaphore("consts_a")
            with nc.Block() as block:
                @block.sync
                def _(sp):
                    sp.dma_start(dist[:, :], a["dist_a"]).then_inc(consts, 16)
                    sp.dma_start(sink[:, :], a["sink"].partition_broadcast(P)).then_inc(consts, 16)
                    sp.wait_ge(consts, 32)
            project_a_stage(nc, c, w, h, q, k_, v)
            attention_stage(nc, c, w, attention_a_items(q, k_, v, dist, o), "att_a", sink)
            out_stage(nc, c, w, o, h, x, "out_a")
        if upto == 1:
            return dump(x)
        rms_stage(nc, c, x, h, COLS["norm_ffn0"], "rms1")
        ffn_stage(nc, c, w, h, x, "ffn0")
        if upto == 2:
            return dump(x)
        rms_stage(nc, c, x, h, COLS["norm_mix1"], "rms2")
        with ExitStack() as layer:
            def sl(n, shape):
                return layer.enter_context(nc.sbuf_tensor(n, shape, F32))
            v = sl("v_b", [P, 3, TT, D])
            kept, o = nc.dram_tensor("x_kept", [P, DC, T], F32, kind="Internal").ap(), x
            qk = [sl(f"qk{i}", [P, 6, T]) for i in range(2)]
            dist = sl("dist_b", [P, TT, T + 2 * P])
            consts = nc.alloc_semaphore("consts_b")
            with nc.Block() as block:
                @block.sync
                def _(sp):
                    sp.dma_start(dist[:, :, :], a["dist_b"]).then_inc(consts, 16)
                    sp.dma_start(kept, x[:, :, :]).then_inc(consts, 16)
                    sp.wait_ge(consts, 32)
            values_b_stage(nc, c, w, h, v)
            attention_stage(nc, c, w, attention_b_items(qk, v, dist, o), "att_b", None, ProjectB(c, h, qk))
            out_stage(nc, c, w, o, h, x, "out_b", kept)
        if upto == 3:
            return dump(x)
        rms_stage(nc, c, x, h, COLS["norm_ffn1"], "rms3")
        ffn_stage(nc, c, w, h, x, "ffn1")
        rms_stage(nc, c, x, x, COLS["norm_final"], "rms4")
        if upto == 4:
            return dump(x)
        return True


def program(nc, a, out, upto=99, dump=None):
    with ExitStack() as ctx:
        def sb(n, shape, dt=F32):
            return ctx.enter_context(nc.sbuf_tensor(n, shape, dt))

        c = Core(nc)
        ring, lo = [], []
        for i in range(RING):
            lo.append(nc.alloc_sbuf_tensor_at(f"ring_lo{i}", [P, UNIT], F32R, offset=-(-nc.sbuf_base // 32) * 32))
            ring.append(sb(f"ring{i}", [P, UNIT]))
        c.wide = [ctx.enter_context(nc.psum_tensor(f"wide{i}", [P, 1024], F32)) for i in range(4)]
        c.bank = [c.wide[i // 2][:, i % 2 * 512:(i % 2 + 1) * 512] for i in range(8)]
        c.ident = sb("ident", [P, P])
        c.ones = sb("ones", [P, P])
        c.cols = sb("cols", [P, N_COLS])
        x = sb("x", [P, DC, T])
        units = a["weights"].shape[0]
        w = Weights(ring, a["weights"], [nc.alloc_semaphore(f"loaded{i}") for i in range(RING)],
                    nc.alloc_semaphore("used"), units)
        w.lo = lo
        inputs = nc.alloc_semaphore("inputs_loaded")
        with nc.Block() as block:
            @block.sync
            def _(sp):
                sp.dma_start(x[:, :, :], a["x"]).then_inc(inputs, 16)
                sp.dma_start(c.cols[:, :], a["cols"]).then_inc(inputs, 16)
                sp.dma_start(c.ident[:, :], a["ident"]).then_inc(inputs, 16)
                for n in range(RING):
                    w.load(sp, n)
                sp.wait_ge(inputs, 48)

            @block.vector
            def _(dve):
                dve.memset(c.ones[:, :], 1.0)

        if not first_block(nc, c, w, a, x, upto, dump):
            return
        second_block(nc, c, w, a, x, out, upto, dump)



def blocks(wt):
    k, n = wt.shape
    return wt.reshape(k // P, P, n // P, P).transpose(2, 0, 1, 3)


def unitize(b):
    return b.reshape(-1, BLOCKS, P, P).transpose(0, 2, 1, 3).reshape(-1, P, UNIT)


def by_column_chunk(wt):
    return unitize(blocks(wt).reshape(-1, P, P))


def by_row_chunk(wt):
    return unitize(blocks(wt).transpose(1, 0, 2, 3).reshape(-1, P, P))


def gate_and_up(g, u):
    return unitize(np.stack([blocks(g), blocks(u)], 1).reshape(-1, P, P))


def feature_columns(v):
    return v.reshape(-1, P).T


def first_block_units(i):
    order = [m // 4 * 8 + m % 4 + 4 * half for m in range(DC) for half in range(2)]
    heads = np.concatenate([np.arange(h * DH, (h + 1) * DH) for h in order])
    qkv, out_a = i["w_qkv_a"][0], i["w_out_a"][0]
    yield by_column_chunk(np.concatenate([qkv[:, :D][:, heads], qkv[:, D:D + 2 * P]], 1))
    yield by_row_chunk(qkv[:, D + 2 * P:])
    yield by_column_chunk(out_a[heads, :])
    yield gate_and_up(i["w_gate"][0], i["w_up"][0])
    yield by_column_chunk(i["w_down"][0])
    b = i["w_qkv_b"][0].reshape(D, 3, 3, D)
    for g in range(3):
        for half in range(2):
            yield by_row_chunk(b[:, g, 2, half * T:(half + 1) * T])
    for m in range(DC):
        cols = slice(m * P, (m + 1) * P)
        yield by_column_chunk(np.concatenate([b[:, g, s, cols] for g in range(3) for s in range(2)], 1))
    yield by_column_chunk(i["w_out_b"][0])
    yield gate_and_up(i["w_gate"][1], i["w_up"][1])
    yield by_column_chunk(i["w_down"][1])


def second_block_units(i):
    for g in range(6 * D // T):
        yield by_row_chunk(i["w_ada_2"][0][:, g * T:(g + 1) * T])
    w_in = i["w_in_2"][0]
    at = np.cumsum([0, DM, DM, DM, DM, DM, DM, DM, 4 * NH, 64, 64, 64, P])
    mv, mo, gates, lw_f, lw_b, la, lg = [w_in[:, at[n]:at[n + 1]] for n in range(5, 12)]
    zeros = np.zeros((D, P), w_in.dtype)
    pad = lambda n: zeros[:, :n]
    gate = lambda n: [gates[:, n * NH:(n + 1) * NH], pad(24), gates[:, (n + 2) * NH:(n + 3) * NH], pad(24)]
    yield by_column_chunk(np.concatenate([w_in[:, :5 * DM], lw_f, lw_b, la, pad(64), lg, *gate(0), *gate(1), mo], 1))
    yield by_row_chunk(mv)
    yield by_column_chunk(i["w_out_2"][0])
    for s in range(EXPERTS + 1):
        if s < EXPERTS:
            yield by_row_chunk(i["ex_gate_2"][0, s])
            yield by_row_chunk(i["ex_up_2"][0, s])
        if s >= 1:
            yield by_row_chunk(i["ex_down_2"][0, s - 1])


def distances():
    i, j = np.arange(P)[:, None], np.arange(3 * P)[None, :]
    rel = np.abs(j - P - i)
    dist_a = np.where(rel <= P, rel, FAR).astype(np.float32)
    dist_b = np.empty((P, TT, T + 2 * P), np.float32)
    own = np.abs(i - np.arange(P)[None, :])
    for r in range(TT):
        rel = np.abs(4 * i + r - np.arange(T)[None, :])
        dist_b[:, r, :T] = np.where(rel <= 64, rel, FAR)
        dist_b[:, r, T:T + P] = np.where(own <= 64, 4 * own, FAR)
        dist_b[:, r, T + P:] = np.where(own % 4 == 0, 4 * own, FAR)
    return dist_a, dist_b


def mixer_constants():
    pair = np.zeros((GR, 8, P), np.float32)
    for d in range(2):
        for h in range(NH):
            pair[SIDE[d] + h, d * MC + h // 2, h % 2 * DH:h % 2 * DH + DH] = 1
    i = np.arange(P)
    same = (i[:, None] // DH == i[None, :] // DH).astype(np.float32)
    before = [i[:, None] < i[None, :], i[:, None] > i[None, :]]
    upto = [b | np.eye(P, dtype=bool) for b in before]
    never = np.stack([np.where(u_, 0, -1e30) for u_ in upto], 1).astype(np.float32)
    pair_mask = np.stack([np.concatenate([b, u_], 1) for b, u_ in zip(before, upto)], 1).astype(np.float32)
    token = P * np.arange(TT)[None, :, None] + i[:, None, None] + np.zeros((1, 1, 2), int)
    pairs = np.stack([token, 2 * token + np.arange(2)], 3).astype(np.uint32)
    level = np.zeros((P, 2, LEVELS, P), np.uint32)
    for k in range(LEVELS):
        in_block = i[:, None] >> (k + 1) == i[None, :] >> (k + 1)
        high, low = i[:, None] >> k & 1, i[None, :] >> k & 1
        level[:, 0, k, :] = in_block & (high == 1) & (low == 0)
        level[:, 1, k, :] = in_block & (high == 0) & (low == 1)
    return {"pair_rows": pair, "same": same, "never": never, "pair_mask": pair_mask,
            "level_mask": level, "first_mask": np.ascontiguousarray(level[:, :, 0, :]).astype(np.float32),
            "iota": np.tile(np.arange(EXPERTS, dtype=np.float32), (P, 1)),
            "earlier": before[0].astype(np.float32), "pairs": pairs}


def feature_major(v):
    return np.ascontiguousarray(v.T.reshape(-1, P, v.shape[0]).transpose(1, 0, 2))


def arrays_of(i):
    i = {k: np.asarray(v) for k, v in i.items()}
    dist_a, dist_b = distances()
    of = lambda name: i[name + "_2"][0].reshape(-1)
    cols = [i["norm_mix"][0], i["norm_mix"][1], i["norm_ffn"][0], i["norm_ffn"][1], i["norm_final"], of("conv_w"), of("r_w0"),
            of("r_a0"), of("r_kk"), of("r_ka"), of("r_bonus"), of("m_norm_w"), of("r_norm_w"), of("r_norm_b"),
            of("ln1_g"), of("ln1_b"), of("ln2_g"), of("ln2_b")]
    gate_bias = np.zeros((64, 2), np.float32)
    for n, name in enumerate(("m_bias_i_2", "m_bias_f_2")):
        gate_bias[0:NH, n], gate_bias[32:32 + NH, n] = i[name][0]
    lowrank = np.zeros((P, 3, DM), np.float32)
    lowrank[:, 0, :] = i["r_wB_2"][0].reshape(P, DM)
    lowrank[:64, 1, :], lowrank[:, 2, :] = i["r_aB_2"][0], i["r_gB_2"][0]
    rt = np.concatenate([i["rt_g_2"][0], i["rt_e_2"][0]], 1)
    return {
        "weights": np.concatenate([*first_block_units(i), *second_block_units(i)]),
        "x": feature_major(i["x"][0]),
        "ctx": feature_major(i["ctx_2"][0]),
        "cond": np.ascontiguousarray(np.stack([feature_columns(i["c_2"][0]), feature_columns(i["c_ctx_2"])], 2)),
        "ada_b": np.ascontiguousarray(feature_columns(i["b_ada_2"][0])),
        "cols": np.ascontiguousarray(np.concatenate([feature_columns(v) for v in cols], 1)),
        "gate_bias": gate_bias,
        "lowrank": lowrank,
        "rt": np.ascontiguousarray(rt.reshape(DC, P, -1).transpose(1, 0, 2)),
        "rt_bias": np.concatenate([i["rt_g_b_2"][0], i["rt_e_b_2"][0]])[None, :],
        "ident": np.eye(P, dtype=np.float32),
        "dist_a": dist_a,
        "dist_b": dist_b,
        "sink": np.ascontiguousarray(i["sink_a"][0]),
        **mixer_constants(),
    }



def kernel(**inputs):
    import concourse.bacc as bacc
    from concourse.bass_utils import run_bass_kernel_spmd

    nc = bacc.Bacc("TRN2", target_bir_lowering=False, num_devices=1)
    arrays = {"in_" + k: v for k, v in arrays_of(inputs).items()}
    aps = {k[3:]: nc.dram_tensor(k, v.shape, mybir.dt.from_np(v.dtype), kind="ExternalInput").ap() for k, v in arrays.items()}
    out = nc.dram_tensor("out", (P, DC, T), F32, kind="ExternalOutput").ap()
    program(nc, aps, out)
    result = run_bass_kernel_spmd(nc, [arrays], core_ids=[0]).results[0]["out"]
    return np.ascontiguousarray(result.transpose(1, 0, 2).reshape(D, T).T)[None]
```
